# Optimizing a Trainium2 kernel written in Bass

```python
import math
import jax, jax.numpy as jnp
from jax import lax
import numpy as np

D_MODEL = 1024
BATCH = 1
SEQ = 512
DEPTH = 1

D_MIX = D_MODEL
M_HEADS = 4
M_DH = D_MODEL // 8
M_WIDTH = M_HEADS * M_DH
CONV_W = 4
CHUNK = 64
A_HEADS = 8
A_DH = D_MODEL // 16
A_WIDTH = A_HEADS * A_DH
IDX_HEADS = 8
IDX_DH = 64
TOPK_MAX = 256
Q_BLOCK = 128
P_HEADS = 8
N_KEYS = 128
N_EXPERTS = N_KEYS * N_KEYS
P_DK = 128
P_TOPK = 16
P_TOK_BLOCK = 128
EPS = 1e-6

_COL_SIZES = (M_WIDTH, M_WIDTH, M_WIDTH, M_WIDTH, M_HEADS, M_HEADS,
              A_WIDTH, A_DH, A_DH, IDX_HEADS * IDX_DH, IDX_DH, IDX_HEADS)
D_IN = 4 * M_WIDTH + 2 * M_HEADS + A_WIDTH + 2 * A_DH + IDX_HEADS * IDX_DH + IDX_DH + IDX_HEADS
F_GATE_OFFSET = 4 * M_WIDTH + M_HEADS

kernel_name = "hymba_mlstm_dsa_peer_block"

def _rmsnorm(x, g):
    xf = x.astype(jnp.float32)
    y = xf * lax.rsqrt(jnp.mean(xf * xf, axis=-1, keepdims=True) + EPS)
    return (y * g.astype(jnp.float32)).astype(x.dtype)

def _headnorm(h, g):
    B, T, H, d = h.shape
    return _rmsnorm(h, g.reshape(H, d)).reshape(B, T, H * d)

def _split_cols(z):
    parts, off = [], 0
    for n in _COL_SIZES:
        parts.append(z[..., off:off + n])
        off += n
    return parts

def _causal_conv(x, w):
    T = x.shape[1]
    xp = jnp.pad(x, ((0, 0), (CONV_W - 1, 0), (0, 0)))
    out = xp[:, 0:T] * w[0]
    for j in range(1, CONV_W):
        out = out + xp[:, j:j + T] * w[j]
    return out

def _mlstm(q, k, v, i_pre, f_pre):
    B, T, H, Dk = q.shape
    Dv = v.shape[-1]
    NC = T // CHUNK

    def to_chunks(a):
        a = a.astype(jnp.float32).reshape((B, NC, CHUNK, H) + a.shape[3:])
        return jnp.moveaxis(a, 3, 1)

    q = to_chunks(q) * (Dk ** -0.5)
    k = to_chunks(k)
    v = to_chunks(v)
    ig = to_chunks(i_pre)
    b = jnp.cumsum(jax.nn.log_sigmoid(to_chunks(f_pre)), -1)
    b_last = b[..., -1]

    causal = jnp.tril(jnp.ones((CHUNK, CHUNK), dtype=bool))
    log_d = jnp.where(causal, b[..., :, None] - b[..., None, :] + ig[..., None, :], -jnp.inf)

    a = b_last[..., None] - b + ig
    m_loc = jnp.max(a, axis=-1)
    w_loc = jnp.exp(a - m_loc[..., None])
    kv = jnp.einsum('bhcsd,bhcse->bhcde', k * w_loc[..., None], v)
    ks = jnp.einsum('bhcs,bhcsd->bhcd', w_loc, k)

    def step(carry, inp):
        C, n, m = carry
        bl, ml, kvc, ksc = inp
        m_new = jnp.maximum(bl + m, ml)
        dec = jnp.exp(bl + m - m_new)
        inj = jnp.exp(ml - m_new)
        C_new = dec[..., None, None] * C + inj[..., None, None] * kvc
        n_new = dec[..., None] * n + inj[..., None] * ksc
        return (C_new, n_new, m_new), (C, n, m)

    init = (jnp.zeros((B, H, Dk, Dv), jnp.float32),
            jnp.zeros((B, H, Dk), jnp.float32),
            jnp.zeros((B, H), jnp.float32))
    xs = (jnp.moveaxis(b_last, 2, 0), jnp.moveaxis(m_loc, 2, 0),
          jnp.moveaxis(kv, 2, 0), jnp.moveaxis(ks, 2, 0))
    _, (C0, n0, m0) = lax.scan(step, init, xs)
    C0 = jnp.moveaxis(C0, 0, 2)
    n0 = jnp.moveaxis(n0, 0, 2)
    m0 = jnp.moveaxis(m0, 0, 2)

    m_inter = b + m0[..., None]
    m_t = jnp.maximum(m_inter, jnp.max(log_d, axis=-1))
    w_inter = jnp.exp(m_inter - m_t)
    s = jnp.einsum('bhctd,bhcsd->bhcts', q, k) * jnp.exp(log_d - m_t[..., None])
    num = (jnp.einsum('bhcts,bhcse->bhcte', s, v)
           + w_inter[..., None] * jnp.einsum('bhctd,bhcde->bhcte', q, C0))
    den = jnp.sum(s, axis=-1) + w_inter * jnp.einsum('bhctd,bhcd->bhct', q, n0)
    h = num / jnp.maximum(jnp.abs(den), jnp.exp(-m_t))[..., None]
    return jnp.moveaxis(h, 1, 3).reshape(B, T, H, Dv)

def _dsa(q, k, v, qi, ki, wi):
    B, T, H, dh = q.shape
    n_sel = min(TOPK_MAX, T // 4)
    NB = T // Q_BLOCK
    idx_scale = (IDX_DH ** -0.5) * (IDX_HEADS ** -0.5)
    att_scale = dh ** -0.5
    key_pos = jnp.arange(T)

    def blocks(a):
        return jnp.moveaxis(a.reshape((B, NB, Q_BLOCK) + a.shape[2:]), 1, 0)

    def block(args):
        qb, qib, wib, tb = args
        rel = jax.nn.relu(jnp.einsum('bqhd,bsd->bqhs', qib, ki))
        score = jnp.einsum('bqhs,bqh->bqs', rel, wib).astype(jnp.float32) * idx_scale
        admissible = key_pos[None, :] <= tb[:, None]
        score = jnp.where(admissible[None], score, -jnp.inf)
        _, idx = lax.top_k(score, n_sel)
        kg = jax.vmap(lambda kk, ii: kk[ii])(k, idx)
        vg = jax.vmap(lambda vv, ii: vv[ii])(v, idx)
        s = jnp.einsum('bqhd,bqkd->bqhk', qb, kg).astype(jnp.float32) * att_scale
        ok = idx <= tb[None, :, None]
        s = jnp.where(ok[:, :, None, :], s, -jnp.inf)
        p = jax.nn.softmax(s, axis=-1).astype(vg.dtype)
        return jnp.einsum('bqhk,bqkd->bqhd', p, vg)

    out = lax.map(block, (blocks(q), blocks(qi), blocks(wi), key_pos.reshape(NB, Q_BLOCK)))
    return jnp.moveaxis(out, 0, 1).reshape(B, T, H, dh)

def _peer(h, w_q, sub_keys, u_tab, v_tab):
    B, T, D = h.shape
    n_tok = B * T
    xt = h.reshape(n_tok, D)
    qry = (xt @ w_q).reshape(n_tok, P_HEADS, 2, P_DK // 2)
    s = jnp.einsum('nhpd,hpkd->nhpk', qry, sub_keys).astype(jnp.float32)
    s1, i1 = lax.top_k(s[:, :, 0], P_TOPK)
    s2, i2 = lax.top_k(s[:, :, 1], P_TOPK)
    cand = (s1[..., :, None] + s2[..., None, :]).reshape(n_tok, P_HEADS, P_TOPK * P_TOPK)
    cidx = (i1[..., :, None] * N_KEYS + i2[..., None, :]).reshape(n_tok, P_HEADS, P_TOPK * P_TOPK)
    top, pos = lax.top_k(cand, P_TOPK)
    eidx = jnp.take_along_axis(cidx, pos, axis=-1).reshape(n_tok, P_HEADS * P_TOPK)
    gate = jax.nn.softmax(top, axis=-1).reshape(n_tok, P_HEADS * P_TOPK).astype(h.dtype)
    nb = n_tok // P_TOK_BLOCK

    def block(args):
        xb, eb, gb = args
        a = jnp.einsum('nd,nkd->nk', xb, u_tab[eb])
        return jnp.einsum('nk,nkd->nd', gb * jax.nn.gelu(a, approximate=False), v_tab[eb])

    out = lax.map(block, (xt.reshape(nb, P_TOK_BLOCK, D),
                          eidx.reshape(nb, P_TOK_BLOCK, P_HEADS * P_TOPK),
                          gate.reshape(nb, P_TOK_BLOCK, P_HEADS * P_TOPK)))
    return out.reshape(B, T, D)

def setup_inputs(seed: int = 0) -> dict:
    key = jax.random.key(seed)
    ks = jax.random.split(key, 20)
    f32 = jnp.float32
    D = D_MODEL
    nrm = lambda k, s: jax.random.normal(k, s, f32)
    x = nrm(ks[0], (BATCH, SEQ, D))
    c = nrm(ks[1], (BATCH, D))
    w_ada = nrm(ks[2], (DEPTH, D, 6 * D)) * (0.5 * D ** -0.5)
    b_ada = nrm(ks[3], (DEPTH, 6 * D)) * 0.02
    norm1_g = 1.0 + 0.02 * nrm(ks[4], (DEPTH, D))
    w_in = nrm(ks[5], (DEPTH, D, D_IN)) * D ** -0.5
    f_bias = jnp.linspace(3.0, 6.0, M_HEADS, dtype=f32)
    b_in = (0.02 * nrm(ks[6], (DEPTH, D_IN))).at[:, F_GATE_OFFSET:F_GATE_OFFSET + M_HEADS].add(f_bias)
    conv_qk = nrm(ks[7], (DEPTH, CONV_W, 2 * M_WIDTH)) * CONV_W ** -0.5
    out_norm_m = 1.0 + 0.02 * nrm(ks[8], (DEPTH, M_WIDTH))
    out_norm_a = 1.0 + 0.02 * nrm(ks[9], (DEPTH, A_WIDTH))
    w_out = nrm(ks[10], (DEPTH, D_MIX, D)) * D_MIX ** -0.5
    norm2_g = 1.0 + 0.02 * nrm(ks[11], (DEPTH, D))
    w_peer_q = nrm(ks[12], (DEPTH, D, P_HEADS * P_DK)) * D ** -0.5
    peer_sub_keys = nrm(ks[13], (DEPTH, P_HEADS, 2, N_KEYS, P_DK // 2)) * (P_DK // 2) ** -0.5
    peer_u = nrm(ks[14], (DEPTH, N_EXPERTS, D)) * D ** -0.5
    peer_v = nrm(ks[15], (DEPTH, N_EXPERTS, D)) * P_HEADS ** -0.5
    final_g = 1.0 + 0.02 * nrm(ks[16], (D,))
    return {"x": x, "c": c, "w_ada": w_ada, "b_ada": b_ada, "norm1_g": norm1_g,
            "w_in": w_in, "b_in": b_in, "conv_qk": conv_qk, "out_norm_m": out_norm_m,
            "out_norm_a": out_norm_a, "w_out": w_out, "norm2_g": norm2_g,
            "w_peer_q": w_peer_q, "peer_sub_keys": peer_sub_keys, "peer_u": peer_u,
            "peer_v": peer_v, "final_g": final_g}

def reference(x, c, w_ada, b_ada, norm1_g, w_in, b_in, conv_qk, out_norm_m, out_norm_a,
              w_out, norm2_g, w_peer_q, peer_sub_keys, peer_u, peer_v, final_g):
    B, T, _ = x.shape
    for l in range(DEPTH):
        ada = jax.nn.silu(c) @ w_ada[l] + b_ada[l]
        sh1, sc1, g1, sh2, sc2, g2 = jnp.split(ada, 6, axis=-1)
        h = _rmsnorm(x, norm1_g[l]) * (1.0 + sc1[:, None]) + sh1[:, None]
        z = h @ w_in[l] + b_in[l]
        mq, mk, mv, mo, mi, mf, aq, ak, av, iq, ik, iw = _split_cols(z)
        qk = jax.nn.silu(_causal_conv(jnp.concatenate([mq, mk], axis=-1), conv_qk[l]))
        mq, mk = qk[..., :M_WIDTH], qk[..., M_WIDTH:]
        hm = _mlstm(mq.reshape(B, T, M_HEADS, M_DH), mk.reshape(B, T, M_HEADS, M_DH),
                    mv.reshape(B, T, M_HEADS, M_DH), mi, mf)
        hm = _headnorm(hm, out_norm_m[l]).astype(x.dtype) * jax.nn.sigmoid(mo)
        ha = _dsa(aq.reshape(B, T, A_HEADS, A_DH), ak, av,
                  iq.reshape(B, T, IDX_HEADS, IDX_DH), ik, iw)
        ha = _headnorm(ha, out_norm_a[l]).astype(x.dtype)
        y = jnp.concatenate([hm, ha], axis=-1) @ w_out[l]
        x = x + g1[:, None] * y
        h2 = _rmsnorm(x, norm2_g[l]) * (1.0 + sc2[:, None]) + sh2[:, None]
        x = x + g2[:, None] * _peer(h2, w_peer_q[l], peer_sub_keys[l], peer_u[l], peer_v[l])
    return _rmsnorm(x, final_g)


_drawn_inputs = setup_inputs


def setup_inputs(seed=0):
    import zlib

    import numpy as np

    out = dict(_drawn_inputs(seed))
    spreads = {}
    factors = {'norm1_g': 4.634,
     'out_norm_m': 79.053,
     'out_norm_a': 49.317,
     'norm2_g': 25.204,
     'final_g': 26.175}
    for name, (base, spread) in spreads.items():
        noise = np.random.default_rng([zlib.crc32(name.encode()), seed]).standard_normal(out[name].shape)
        drawn = base * np.exp(spread * noise) if base else spread * noise
        out[name] = __import__('jax').numpy.asarray(drawn.astype(out[name].dtype))
    for name, factor in factors.items():
        out[name] = (out[name] * factor).astype(out[name].dtype)
    return out
```

```python
import concourse.bass as bass
from concourse import mybir
from contextlib import ExitStack

D = 1024
T = 512
P = 128
KB = D // P
NT = T // P
CONV_W = 4
M_HEADS, M_DH = 4, 128
A_HEADS, A_DH = 8, 64
IDX_HEADS = 8
N_SEL = 128
P_HEADS, N_KEYS, P_TOPK = 8, 128, 16
EPS = 1e-6

Z_IQ, Z_IK, Z_MISC, Z_AQ, Z_AK, Z_MQ, Z_MK, Z_MV, Z_MO = 0, 4, 5, 6, 10, 11, 15, 19, 23
Z_TILES = 27
MISC_MI, MISC_IW, MISC_MF, MISC_AV = 0, 8, 32, 64

C_C, C_BADA, C_N1, C_BIN, C_CONV = 0, 8, 56, 64, 91
C_OUTN, C_N2, C_FG, C_END = 123, 131, 139, 147

GROUPS = 4
GI = N_KEYS // GROUPS
UNIT = 512
RAW_SLOTS, SPLIT_SLOTS = 4, 2
ZU, OU, QU, EU = 2 * Z_TILES, 2 * KB, 2 * KB, 2 * GI
UNITS = ZU + OU + QU + 2 * GROUPS * EU
GT = 8
NEG, TAKEN = -1e30, -3e30


def stream_order():
    order = [("z", 0, ZU), ("o", 0, OU), ("q", 0, QU), ("u", 0, EU), ("u", 1, EU)]
    for g in range(GROUPS - 2):
        order += [("v", g, EU), ("u", g + 2, EU)]
    order += [("v", GROUPS - 2, EU), ("v", GROUPS - 1, EU)]
    first, at = {}, 0
    for name, g, n in order:
        first[name, g] = at
        at += n
    return order, first


class Steps:

    def __init__(self, eng, sem):
        self.eng, self.sem, self.n, self.turn, self.skipped = eng, sem, 0, None, 0

    def did(self, ins):
        ins.then_inc(self.sem, 1)
        self.n += 1

    def settle(self, back=0):
        n = self.n - back
        self.eng.wait_ge(self.sem, n if self.turn is None else self.turn + (n - self.skipped))

    def do(self, ins):
        self.did(ins)
        self.settle()

    def loop(self, start, end, per):
        return _StepLoop(self, start, end, per)


class Rounds(Steps):

    def turn_over(self):
        self.settle()
        self.eng.sem_clear(self.sem)
        self.n = 0


class _StepLoop:
    def __init__(self, steps, start, end, per):
        self.s, self.start, self.end, self.per = steps, start, end, per

    def __enter__(self):
        self.ctx = self.s.eng.Fori(self.start, self.end)
        i = self.ctx.__enter__()
        self.before = self.s.n
        self.s.turn, self.s.skipped = i * self.per, self.start * self.per
        return i

    def __exit__(self, *error):
        assert error[0] or self.s.n - self.before == self.per, (self.s.n - self.before, self.per)
        self.s.turn = None
        self.s.n = self.before + self.per * (self.end - self.start)
        return self.ctx.__exit__(*error)


def build_layer(nc, x_t, cols_in, wada_in, stream_in, keys_in, out):
    fp32, fp32r, u32, bf16 = mybir.dt.float32, mybir.dt.float32r, mybir.dt.uint32, mybir.dt.bfloat16
    ALU, ACT, AX = mybir.AluOpType, mybir.ActivationFunctionType, mybir.AxisListType
    ds = bass.ds
    ORDER, FIRST = stream_order()

    x2_dram = nc.dram_tensor("x2_dram", [P, KB, T], fp32, kind="Internal").ap()
    part_dram = nc.dram_tensor("part_dram", [GROUPS - 1, KB, P, T], fp32, kind="Internal").ap()

    BASE = 16512

    def at(name, shape, offset, dt=fp32):
        size = 2 if dt == bf16 else 4
        for n in shape[1:]:
            size *= n
        assert BASE + offset + size <= 229344, (name, offset, size)
        return nc.alloc_sbuf_tensor_at(name, shape, dt, offset=BASE + offset)

    coef = at("coef", [P, 2 * GI, T], 0)
    A0 = 4 * 2 * GI * T
    hs_hi = at("hs_hi", [P, KB, T], A0, fp32r)
    hs_lo = at("hs_lo", [P, KB, T], A0 + 16384, fp32r)
    raw = at("raw", [P, RAW_SLOTS, UNIT], A0 + 32768)
    w_hi = at("w_hi", [P, SPLIT_SLOTS, UNIT], A0 + 40960, fp32r)
    w_lo = at("w_lo", [P, SPLIT_SLOTS, UNIT], A0 + 45056, fp32r)
    B0 = A0 + 49152
    c_hi = at("c_hi", [P, SPLIT_SLOTS, T], B0, fp32r)
    c_lo = at("c_lo", [P, SPLIT_SLOTS, T], B0 + 4096, fp32r)
    slot_i1 = at("slot_i1", [P, T], B0 + 8192, bf16)
    slot_i2 = at("slot_i2", [P, T], B0 + 9216, bf16)
    slot_g = at("slot_g", [P, 3, T], B0 + 10240, bf16)
    eq1 = at("eq1", [P, 2, GI, GT], B0 + 15360, bf16)
    rows1 = at("rows1", [P, 2, 3, GI, GT], B0 + 16384, bf16)
    rows2 = at("rows2", [P, 2, N_KEYS, GT], B0 + 19456, bf16)
    y_stage = [at("y_stage", [P, 4, T], B0 + 15360)] * 2 + [at("y_stage2", [P, 4, T], A0)]
    C0 = B0 + 27648
    cols = at("cols", [P, C_END], C0)
    ada = at("ada", [P, 48], C0 + 608)
    amp1 = at("amp1", [P, KB], C0 + 800)
    amp2 = at("amp2", [P, KB], C0 + 832)
    iota = at("iota", [P, N_KEYS], C0 + 864)
    ones = at("ones", [P, P], C0 + 1376)
    ident = at("ident", [P, P], C0 + 1888)
    silu_c = at("silu_c", [P, KB], C0 + 2400)
    key_rep = at("key_rep", [P, N_KEYS, GT], C0 + 2432, bf16)

    def fa(name, shape, offset, dt=fp32):
        return at(name, shape, 4 * offset, dt)

    def fb(name, shape, offset, dt=fp32):
        return at(name, shape, B0 + 4 * offset, dt)

    x = fa("x", [P, KB, T], 0)
    z = fa("z", [P, Z_TILES, T], 4096)
    ada_w = fa("ada_w", [P, 3, KB, 256], 17920)
    qk = fa("qk", [P, 2 * M_HEADS, T], 24064)
    mask = fa("mask", [P, 1280], 28160)
    score = fa("score", [P, 1152], 29440)
    misc_t = fa("misc_t", [P, NT, P], 30592)
    relu = fa("relu", [P, 2, T], 31104)
    emm = fa("emm", [P, NT, M_HEADS], 32128)
    wcol = fa("wcol", [P, NT, M_HEADS], 32144)
    den = fa("den", [P, NT, M_HEADS], 32160)
    hrs = fa("hrs", [P, NT, M_HEADS], 32176)
    best8 = fa("best8", [P, 8], 32192)
    s_max = fa("s_max", [P, 2], 32200)
    s_sum = fa("s_sum", [P, 2], 32208)
    s_neg = fa("s_neg", [P, 2], 32216)
    o_rs = fa("o_rs", [P, A_HEADS], 32224)
    v_aug = fa("v_aug", [P, NT, M_HEADS, M_DH + 1], 17920)
    num = fa("num", [P, NT, M_HEADS, M_DH + 1], 17920 + 2064)
    decay = fa("decay", [P, 1280], 17920 + 4128)
    hm = fa("hm", [P, NT, M_HEADS, M_DH], 4096 + T * Z_MQ)
    hm2 = fa("hm2", [P, NT, M_HEADS, M_DH], 4096 + T * Z_MK)
    h_tmp = fa("h_tmp", [P, KB, T], 4096)
    rstd = fa("rstd", [P, T], 4096 + T * KB)
    sq = fa("sq", [P, KB, T], 4096 + T * (KB + 1))
    prob = fb("prob", [P, 2, T], 0)
    prob_t = fb("prob_t", [P, 2, NT, P], 1024)
    att = fb("att", [P, A_HEADS, A_DH], 2048)
    att2 = fb("att2", [P, A_HEADS, A_DH], 2560)
    rows = fb("rows", [P, 5, T], 3072)
    R_LF, R_B, R_W, R_MX, R_M = range(5)
    sel = fb("sel", [P, M_HEADS, P], 5632)
    q_t = fa("q_t", [P, P_HEADS, T], 4096)
    s12 = fa("s12", [P, NT * P_HEADS, 2, N_KEYS], 16384)
    keys = fa("keys", [P, P_HEADS, 2 * N_KEYS], 24576)
    best = fa("best", [P, NT * P_HEADS, 2, P_TOPK], 26624)
    best_iu = fa("best_iu", [P, NT * P_HEADS, 2, P_TOPK], 27648, u32)
    top = fa("top", [P, NT * P_HEADS, P_TOPK], 28672)
    pos_u = fa("pos_u", [P, NT * P_HEADS, P_TOPK], 29184, u32)
    cand = fa("cand", [P, 2, P_TOPK * P_TOPK], 29696)
    gsum = fa("gsum", [P, NT * P_HEADS], 30208)
    best_if = fb("best_if", [P, NT * P_HEADS, 2, P_TOPK], 0)
    pos_f = fb("pos_f", [P, 2, NT * P_HEADS, P_TOPK], 1024)
    pick = fa("pick", [P, P_HEADS, P_TOPK, P_TOPK], 16384)
    slot_t = fa("slot_t", [P, 3, NT * P_HEADS * P_TOPK], 18432)
    slot_gf = fa("slot_gf", [P, T], 19968)
    part = fa("part", [P, 4, KB, T], 0)
    sq_end = fa("sq_end", [P, KB, T], 16384)
    rstd_end = fa("rstd_end", [P, T], 20480)

    bank = [nc.alloc_psum_tensor(f"bank{i}", [P, 512], fp32) for i in range(8)]

    ctx = ExitStack()
    with ctx:
        names = {}

        def S(name):
            if name not in names:
                names[name] = ctx.enter_context(nc.semaphore(name))
            return names[name]

        raw_ready = [S(f"raw_ready{i}") for i in range(RAW_SLOTS)]
        block = ctx.enter_context(nc.Block())

        tile_bank = bank[0:2]
        gate_bank = bank[2:4]
        sum_bank = bank[4:8]

        TILE0 = {("z", 0): 0, ("o", 0): Z_TILES, ("q", 0): Z_TILES + KB}
        for g in range(GROUPS):
            TILE0["u", g] = Z_TILES + 2 * KB + g * GI

        @block.sync
        def _(sp):
            for n in range(RAW_SLOTS):
                sp.dma_start(raw[:, n, :], stream_in[n]).then_inc(raw_ready[n], 16)

            def refill(n, slot):
                sp.wait_ge(S("w_split"), n - (RAW_SLOTS - 1))
                src = stream_in[n] if isinstance(n, int) else stream_in[ds(n, 1), :, :].rearrange("a p f -> (a p) f")
                sp.dma_start(raw[:, slot, :], src).then_inc(raw_ready[slot], 16)

            def refills(first, end):
                turns = (end - first) // RAW_SLOTS
                if turns:
                    with sp.Fori(0, turns) as i:
                        for s in range(RAW_SLOTS):
                            refill(i * RAW_SLOTS + (first + s), (first + s) % RAW_SLOTS)
                for n in range(first + turns * RAW_SLOTS, end):
                    refill(n, n % RAW_SLOTS)

            at = RAW_SLOTS
            for g in range(GROUPS - 1):
                for half in range(2):
                    end = FIRST["v", g] + (half + 1) * GI + RAW_SLOTS
                    refills(at, end)
                    at = end
                    for d in range(4):
                        k = half * 4 + d
                        sp.wait_ge(S("y_out"), g * KB + k + 1)
                        sp.dma_start(part_dram[g, k], y_stage[g][:, d, :]).then_inc(S(f"part_saved{d}"), 16)
            sp.wait_ge(S("x2_saved"), 16)
            for d in range(4):
                sp.wait_ge(S(f"part_saved{d}"), 16 * 2 * (GROUPS - 1))
            sp.wait_ge(S("c_split2"), EU)
            sp.dma_start(part[:, 3, :, :], x2_dram).then_inc(S("part_back"), 16)
            for g in range(GROUPS - 1):
                sp.dma_start(part[:, g, :, :], part_dram[g].rearrange("k p t -> p k t")).then_inc(S("part_back"), 16)
            refills(at, UNITS)

        def coef_lows(eng, subtract, g, other=None, halfway=()):
            first, buf = FIRST["v", g], (g % 2) * GI

            def clow(k, s, i1):
                eng.wait_ge(S(f"c_high{g}"), k + 1)
                src = coef[:, i1, :] if isinstance(i1, int) else coef[:, ds(i1, 1), :]
                subtract(c_lo[:, s % SPLIT_SLOTS, :], src, c_hi[:, s % SPLIT_SLOTS, :].bitcast(fp32), ALU.subtract
                         ).then_inc(S(f"c_split{g}"), 1)

            clow(0, first, buf)
            clow(1, first + 1, buf + 1)
            halfway = list(halfway)
            for half in range(2):
                f = half * GI
                with eng.Fori(0, GI // 4 - 1) as i:
                    for u in range(4):
                        if other:
                            other(i * 4 + (first + f + u + 2), first + f + u + 2)
                        clow(i * 4 + (f + u + 2), first + u, i * 4 + (buf + u + 2))
                for u in range(4):
                    k = GI - 4 + u + 2
                    if other:
                        other(first + f + k, first + f + k)
                    if k < GI or half == 0:
                        clow(f + k, first + k, buf + k % GI)
                    if k >= GI and half == 0 and halfway:
                        halfway.pop(0)()

        @block.gpsimd
        def _(pool):
            own = Steps(pool, S("pool_own"))
            own.do(pool.memset(ones[:, :], 1.0))
            own.do(pool.memset(ident[:, :], 0.0))
            own.do(pool.affine_select(out=ident[:, :], in_=ident[:, :], compare_op=ALU.not_equal, fill=1.0, base=0,
                                      pattern=[[-1, P]], channel_multiplier=1))
            own.do(pool.iota(iota[:, :], pattern=[[1, N_KEYS]], base=0, channel_multiplier=0,
                             allow_small_or_imprecise_dtypes=True))
            own.do(pool.iota(key_rep[:, :, :], pattern=[[1, N_KEYS], [0, GT]], base=0, channel_multiplier=0,
                             allow_small_or_imprecise_dtypes=True))
            own.do(pool.memset(sel[:, :, :], 0.0))
            own.do(pool.affine_select(out=sel[:, :, :], in_=sel[:, :, :], compare_op=ALU.not_equal, fill=-1.0, base=0,
                                      pattern=[[-1, M_HEADS], [0, P]], channel_multiplier=1))
            own.do(pool.memset(mask[:, 0:P], 0.0))
            pool.sem_inc(S("consts"), 1)

            def norm_low(n):
                for k in range(KB):
                    pool.wait_ge(S("h_high"), KB * n + k + 1)
                    pool.tensor_tensor(hs_lo[:, k, :], h_tmp[:, k, :], hs_hi[:, k, :].bitcast(fp32), ALU.subtract
                                       ).then_inc(S("h_low"), 1)

            def low(n, slot):
                pool.wait_ge(S("w_high"), n + 1)
                pool.tensor_tensor(w_lo[:, slot % SPLIT_SLOTS, :], raw[:, slot % RAW_SLOTS, :],
                                   w_hi[:, slot % SPLIT_SLOTS, :].bitcast(fp32), ALU.subtract).then_inc(S("w_split"), 1)

            def lows(first, count):
                with pool.Fori(0, count // 4) as i:
                    for u in range(4):
                        low(i * 4 + (first + u), first + u)
                for n in range(first + count // 4 * 4, first + count):
                    low(n, n)

            norm_low(0)
            lows(0, ZU + 2)
            at_score = 0
            for t in range(1, NT):
                w = (t + 1) * P
                pool.wait_ge(S("scored"), t)
                blk = score[:, at_score + t * P:at_score + w]
                pool.affine_select(out=blk, in_=blk, compare_op=ALU.is_ge, fill=NEG, base=0,
                                   pattern=[[-1, P]], channel_multiplier=1).then_inc(S("score_cut"), 1)
                at_score += w
            pool.affine_select(out=mask[:, 0:P], in_=mask[:, 0:P], compare_op=ALU.is_ge, fill=NEG, base=0,
                               pattern=[[-1, P]], channel_multiplier=1).then_inc(S("mask0"), 1)
            for h in range(M_HEADS):
                pool.wait_ge(S("decay_exp"), h + 1)
                off = 0
                for j in range(NT):
                    blk = decay[:, off:off + P]
                    ins = pool.affine_select(out=blk, in_=blk, compare_op=ALU.is_ge, fill=0.0, base=0,
                                             pattern=[[1, P]], channel_multiplier=-1)
                    off += (NT - j) * P
                ins.then_inc(S("decay_cut"), 1)
            for k in range(KB):
                src = z[:, Z_MO + k, :] if k < 4 else z[:, Z_IQ + k - 4, :]
                pool.wait_ge(S("cat_high"), k + 1)
                pool.tensor_tensor(hs_lo[:, k, :], src, hs_hi[:, k, :].bitcast(fp32), ALU.subtract
                                   ).then_inc(S("cat_low"), 1)
            lows(ZU + 2, OU)
            norm_low(1)
            lows(ZU + OU + 2, QU + EU * 2)
            for g in range(GROUPS):
                first = FIRST["v", g]
                if g == GROUPS - 2:
                    coef_lows(pool, pool.tensor_tensor, g, low)
                elif g < GROUPS - 1:
                    lows(first + 2, EU)
                else:
                    lows(first + 2, EU - 4)
                    low(UNITS - 2, UNITS - 2)
                    low(UNITS - 1, UNITS - 1)
                if g + 2 < GROUPS:
                    lows(FIRST["u", g + 2] + 2, EU)

        @block.scalar
        def _(act):
            own = Steps(act, S("act_own"))
            A = act.activation
            act.dma_start(cols[:, :], cols_in).then_inc(S("cols_in"), 16)
            act.dma_start(x[:, :, :], x_t).then_inc(S("x_in"), 16)
            def ada_load(c):
                if c >= 3:
                    act.wait_ge(S("ada_used"), c - 2)
                act.dma_start(ada_w[:, c % 3, :, :], wada_in[c]).then_inc(S(f"ada_in{c % 3}"), 16)
            for c in range(3):
                ada_load(c)
            act.wait_ge(S("cols_in"), 16)
            A(silu_c[:, :], cols[:, C_C:C_C + KB], ACT.Silu).then_inc(S("c_silu"), 1)
            act.wait_ge(S("x_in"), 16)
            for k in range(KB):
                A(sq[:, k, :], x[:, k, :], ACT.Square).then_inc(S("x_sq"), 1)
            for c in range(3, 11):
                ada_load(c)
            act.sem_inc(S("tile_out"), 2)

            def high_at(i, slot, free=True):
                if free:
                    act.wait_ge(S("unit_done"), i * 4 + (slot - 1) if i is not None else slot - 1)
                full = 16 * (slot // RAW_SLOTS + 1)
                act.wait_ge(raw_ready[slot % RAW_SLOTS], i * 16 + full if i is not None else full)
                A(w_hi[:, slot % SPLIT_SLOTS, :], raw[:, slot % RAW_SLOTS, :], ACT.Copy).then_inc(S("w_high"), 1)

            def norm_high(n):
                act.wait_ge(S("mean_ready"), n + 1)
                A(rstd[:, :], rstd[:, :], ACT.Sqrt).then_inc(S("root_ready"), 1)
                for k in range(KB):
                    act.wait_ge(S("h_ready"), KB * n + k + 1)
                    A(hs_hi[:, k, :], h_tmp[:, k, :], ACT.Copy).then_inc(S("h_high"), 1)

            norm_high(0)
            high_at(None, 0, False)
            high_at(None, 1, False)
            def z_out(t, bankno):
                act.wait_ge(S("unit_done"), t * 2 + 2)
                dst = z[:, t, :] if isinstance(t, int) else z[:, ds(t, 1), :]
                b = cols[:, C_BIN + t:C_BIN + t + 1] if isinstance(t, int) else cols[:, ds(t + C_BIN, 1)]
                A(dst, tile_bank[bankno][:, :], ACT.Identity, bias=b).then_inc(S("tile_out"), 1)

            act.wait_ge(S("h_low"), KB)
            with act.Fori(0, Z_TILES // 2) as i:
                for j in range(2):
                    high_at(i, 2 * j + 2)
                    high_at(i, 2 * j + 3)
                    z_out(i * 2 + j, j)
            high_at(None, ZU)
            high_at(None, ZU + 1)
            z_out(Z_TILES - 1, 0)
            for c in range(11, 24):
                ada_load(c)

            act.wait_ge(S("misc_tr"), 1)
            A(misc_t[:, :, :], bank[3][:, :].rearrange("p (t c) -> p t c", t=NT), ACT.Copy).then_inc(S("misc_ready"), 1)
            n = 0
            for t in range(1, NT):
                w = (t + 1) * P
                for h in range(IDX_HEADS):
                    act.wait_ge(S("idx_dot"), n + 1)
                    if n >= 2:
                        act.wait_ge(S("idx_added"), n - 1)
                    A(relu[:, n % 2, 0:w], bank[4 + n % 2][:, 0:w], ACT.Relu).then_inc(S("idx_relu"), 1)
                    n += 1
            act.wait_ge(S("tile_out"), Z_TILES + 2)
            f_row = z[32:36, Z_MISC, :]
            own.do(A(rows[32:36, 0, :], f_row, ACT.Abs))
            own.do(A(rows[32:36, 1, :], rows[32:36, 0, :], ACT.Exp, scale=-1.0))
            A(rows[32:36, 2, :], rows[32:36, 1, :], ACT.Ln, bias=1.0).then_inc(S("soft_f"), 1)
            for t in range(2 * M_HEADS):
                act.wait_ge(S("conv"), t + 1)
                A(qk[:, t, :], qk[:, t, :], ACT.Silu).then_inc(S("qk_ready"), 1)
            for h in range(M_HEADS):
                A(z[:, Z_MO + h, :], z[:, Z_MO + h, :], ACT.Sigmoid).then_inc(S("mo_gate"), 1)
            for h in range(M_HEADS):
                act.wait_ge(S("v_tr"), h + 1)
                A(v_aug[:, :, h, 0:M_DH], bank[4 + h % 2][:, :].rearrange("p (j d) -> p j d", j=NT),
                  ACT.Copy).then_inc(S("v_ready"), 1)
            act.wait_ge(S("col_tr"), 1)
            A(wcol[:, :, :], bank[3][:, 0:NT * M_HEADS].rearrange("p (j h) -> p j h", j=NT), ACT.Copy
              ).then_inc(S("wcol_ready"), 1)
            act.wait_ge(S("wcol_ready"), 1)
            A(emm[:, :, :], bank[3][:, 16:16 + NT * M_HEADS].rearrange("p (j h) -> p j h", j=NT), ACT.Exp,
              scale=-1.0).then_inc(S("emm_ready"), 1)
            for h in range(M_HEADS):
                act.wait_ge(S("decay_arg"), h + 1)
                A(decay[:, :], decay[:, :], ACT.Exp).then_inc(S("decay_exp"), 1)
            act.wait_ge(S("hm_mean"), 1)
            A(hrs[:, :, :], hrs[:, :, :], ACT.Sqrt).then_inc(S("hm_root"), 1)
            n = 0
            for t in range(NT):
                w = (t + 1) * P
                for h in range(A_HEADS):
                    act.wait_ge(S("s_masked"), n + 1)
                    A(prob[:, n % 2, 0:w], prob[:, n % 2, 0:w], ACT.Exp, bias=s_neg[:, n % 2:n % 2 + 1],
                      scale=A_DH ** -0.5, accum_out=s_sum[:, n % 2:n % 2 + 1]).then_inc(S("p_ready"), 1)
                    act.wait_ge(S("p_tr"), n + 1)
                    A(prob_t[:, n % 2, 0:t + 1, :], bank[6 + n % 2][:, 0:w].rearrange("p (s q) -> p s q", q=P),
                      ACT.Copy).then_inc(S("pt_ready"), 1)
                    n += 1
                act.wait_ge(S("att_mean"), t + 1)
                A(o_rs[:, :], o_rs[:, :], ACT.Sqrt).then_inc(S("att_root"), 1)
            for k in range(KB):
                src = z[:, Z_MO + k, :] if k < 4 else z[:, Z_IQ + k - 4, :]
                if k < 4:
                    act.wait_ge(S("cat_m"), k + 1)
                else:
                    act.wait_ge(S("cat_a"), NT)
                A(hs_hi[:, k, :], src, ACT.Copy).then_inc(S("cat_high"), 1)
            act.dma_start(keys[:, :, :], keys_in).then_inc(S("keys_in"), 16)

            def highs(first, count):
                with act.Fori(0, count // 4) as i:
                    for u in range(4):
                        high_at(i, first + u)

            highs(ZU + 2, OU)
            for k in range(KB):
                act.wait_ge(S("tile_out"), TILE0["o", 0] + k + 3)
                A(sq[:, k, :], x[:, k, :], ACT.Square).then_inc(S("x_sq"), 1)
            act.dma_start(x2_dram, x[:, :, :]).then_inc(S("x2_saved"), 16)
            norm_high(1)
            def q_tiles():
                with act.Fori(0, KB // 2) as i:
                    for j in range(2):
                        u = ZU + OU + 2 + 2 * j
                        high_at(i, u)
                        high_at(i, u + 1)
                        t = i * 2 + j
                        act.wait_ge(S("unit_done"), t * 2 + (FIRST["q", 0] + 2))
                        A(q_t[:, ds(t, 1), :], tile_bank[(TILE0["q", 0] + j) % 2][:, :], ACT.Copy
                          ).then_inc(S("tile_out"), 1)
            act.wait_ge(S("h_low"), 2 * KB)
            q_tiles()
            for k in range(NT * P_HEADS // 2):
                act.wait_ge(S("keys_dot"), k + 1)
                t, h = k // 4, 2 * (k % 4)
                A(s12[:, t * P_HEADS + h:t * P_HEADS + h + 2, :, :], bank[4 + k % 2][:, :].rearrange(
                    "p (h a e) -> p h a e", h=2, a=2), ACT.Copy).then_inc(S("s_ready"), 1)

            def u_tiles(g, base=0, count=GI // 2):
                with act.Fori(0, count) as i:
                    for j in range(2):
                        u = FIRST["u", g] + 2 + 2 * j
                        high_at(i, u)
                        high_at(i, u + 1)
                        act.wait_ge(S("unit_done"), i * 4 + (u + 0))
                        A(coef[:, ds(i * 2 + ((g % 2) * GI + j), 1), :], tile_bank[(TILE0["u", g] + j) % 2][:, :],
                          ACT.Gelu).then_inc(S("tile_out"), 1)

            def soft_gates():
                for t in range(NT):
                    act.wait_ge(S("top_shift"), t + 1)
                    A(top[:, t * 8:(t + 1) * 8, :], top[:, t * 8:(t + 1) * 8, :], ACT.Exp).then_inc(S("top_exp"), 1)
                for k in range(3):
                    act.wait_ge(S("slot_tr"), k + 1)
                    dst = (slot_i1, slot_i2, slot_gf)[k]
                    A(dst[:, :], bank[4 + k][:, :], ACT.Copy).then_inc(S("slot_out"), 1)

            def v_units(g):
                first, buf = FIRST["v", g], (g % 2) * GI
                act.wait_ge(S("gated"), (g + 1) * T // GT + 2)
                def chigh(slot, i1):
                    src = coef[:, i1, :] if isinstance(i1, int) else coef[:, ds(i1, 1), :]
                    A(c_hi[:, slot % SPLIT_SLOTS, :], src, ACT.Copy).then_inc(S(f"c_high{g}"), 1)
                chigh(first, buf)
                chigh(first + 1, buf + 1)
                for half in range(2):
                    f = first + half * GI
                    with act.Fori(0, GI // 4 - 1) as i:
                        for u in range(4):
                            high_at(i, f + u + 2)
                            chigh(f + u + 2, i * 4 + (buf + u + 2))
                    for u in range(4):
                        k = GI - 4 + u + 2
                        if f + k < UNITS:
                            high_at(None, f + k)
                        if k < GI or half == 0:
                            if f + k >= UNITS:
                                act.wait_ge(S("unit_done"), f + k - 1)
                            chigh(f + k, buf + k % GI)

            act.wait_ge(S("x2_saved"), 16)
            u_tiles(0)
            soft_gates()
            act.wait_ge(S("gate_split"), 1)
            u_tiles(1)
            for g in range(GROUPS):
                v_units(g)
                if g + 2 < GROUPS:
                    act.wait_ge(S(f"c_split{g}"), EU)
                    u_tiles(g + 2)
            for k in range(KB):
                act.wait_ge(S("x3_ready"), k + 1)
                A(sq_end[:, k, :], part[:, 3, k, :], ACT.Square).then_inc(S("x_sq"), 1)
            act.wait_ge(S("mean_ready"), 3)
            A(rstd_end[:, :], rstd_end[:, :], ACT.Sqrt).then_inc(S("root_ready"), 1)
            for k in range(KB):
                act.wait_ge(S("out_ready"), k + 1)
                act.dma_start(out[:, k, :], part[:, 2, k, :]).then_inc(S("out_saved"), 16)
            act.wait_ge(S("out_saved"), 16 * KB)

        @block.vector
        def _(dve):
            own = Steps(dve, S("dve_own"))
            rnd = Rounds(dve, S("dve_round"))
            V = nc.vector

            dve.sem_inc(S("gated"), 2)

            def mean(n, src_bank, rstd=rstd):
                dve.wait_ge(S("sq_sum"), n + 1)
                V.tensor_scalar(rstd[:, :], src_bank[:, :], 1.0 / D, EPS, ALU.mult, ALU.add
                                ).then_inc(S("mean_ready"), 1)
                dve.wait_ge(S("root_ready"), n + 1)
                own.do(V.reciprocal(rstd[:, :], rstd[:, :]))

            def normed(n, amp, shift):
                for k in range(KB):
                    own.do(V.scalar_tensor_tensor(out=h_tmp[:, k, :], in0=x[:, k, :], scalar=amp[:, k:k + 1],
                                                  in1=rstd[:, :], op0=ALU.mult, op1=ALU.mult))
                    V.tensor_scalar(h_tmp[:, k, :], h_tmp[:, k, :], ada[:, shift + k:shift + k + 1], None, ALU.add
                                    ).then_inc(S("h_ready"), 1)

            dve.wait_ge(S("cols_in"), 16)
            dve.wait_ge(S("ada_used"), 8)
            own.do(V.tensor_tensor(ada[:, 0:16], bank[2][:, 0:16], cols[:, C_BADA:C_BADA + 16], ALU.add))
            own.do(V.scalar_tensor_tensor(out=amp1[:, :], in0=ada[:, 8:16], scalar=1.0, in1=cols[:, C_N1:C_N1 + 8],
                                          op0=ALU.add, op1=ALU.mult))
            mean(0, bank[3])
            normed(0, amp1, 0)

            dve.wait_ge(S("ada_used"), 24)
            V.tensor_tensor(ada[:, 16:48], bank[2][:, 16:48], cols[:, C_BADA + 16:C_BADA + 48], ALU.add
                            ).then_inc(S("ada_ready"), 1)
            dve.wait_ge(S("ada_ready"), 1)
            own.do(V.scalar_tensor_tensor(out=amp2[:, :], in0=ada[:, 32:40], scalar=1.0, in1=cols[:, C_N2:C_N2 + 8],
                                          op0=ALU.add, op1=ALU.mult))
            dve.wait_ge(S("consts"), 1)
            def weights(t, h):
                return misc_t[:, t, MISC_IW + h:MISC_IW + h + 1]
            n, at_score = 0, 0
            for t in range(1, NT):
                w = (t + 1) * P
                dst = score[:, at_score:at_score + w]
                for h in range(IDX_HEADS):
                    dve.wait_ge(S("idx_relu"), n + 1)
                    if h == 0:
                        dve.wait_ge(S("misc_ready"), 1)
                        ins = V.tensor_scalar(dst, relu[:, n % 2, 0:w], weights(t, h), None, ALU.mult)
                    else:
                        dve.wait_ge(S("idx_added"), n)
                        ins = V.scalar_tensor_tensor(out=dst, in0=relu[:, n % 2, 0:w], scalar=weights(t, h), in1=dst,
                                                     op0=ALU.mult, op1=ALU.add)
                    ins.then_inc(S("idx_added"), 1)
                    n += 1
                dve.wait_ge(S("idx_added"), n)
                V.tensor_scalar(dst, dst, 64.0 ** -0.5 * IDX_HEADS ** -0.5, None, ALU.mult).then_inc(S("scored"), 1)
                at_score += w

            def conv_tile(c):
                src, dst = z[:, Z_MQ + c, :], qk[:, c, :]
                tap = lambda j: cols[:, C_CONV + 4 * c + j:C_CONV + 4 * c + j + 1]
                own.do(V.tensor_scalar(dst, src, tap(CONV_W - 1), None, ALU.mult))
                for back in range(1, CONV_W):
                    ins = V.scalar_tensor_tensor(out=dst[:, back:T], in0=src[:, 0:T - back],
                                                 scalar=tap(CONV_W - 1 - back), in1=dst[:, back:T],
                                                 op0=ALU.mult, op1=ALU.add)
                    if back < CONV_W - 1:
                        own.do(ins)
                ins.then_inc(S("conv"), 1)

            dve.wait_ge(S("tile_out"), Z_TILES + 2)
            for c in range(2 * M_HEADS):
                conv_tile(c)

            dve.wait_ge(S("soft_f"), 1)
            R = lambda k: rows[0:4, k, :]
            own.do(V.scalar_tensor_tensor(out=R(R_LF), in0=z[32:36, Z_MISC, :], scalar=0.0, in1=rows[32:36, 2, :],
                                          op0=ALU.min, op1=ALU.subtract))
            own.do(V.memset(R(R_W), 1.0))
            own.do(V.tensor_tensor_scan(out=R(R_B), data0=R(R_W), data1=R(R_LF), initial=0.0, op0=ALU.mult, op1=ALU.add))
            own.do(V.tensor_tensor(R(R_W), z[0:4, Z_MISC, :], R(R_B), ALU.subtract))
            own.do(V.tensor_tensor_scan(out=R(R_MX), data0=R(R_W), data1=R(R_W), initial=0.0, op0=ALU.max, op1=ALU.max))
            V.tensor_tensor(R(R_M), R(R_B), R(R_MX), ALU.add).then_inc(S("rows_ready"), 1)
            dve.wait_ge(S("ada_used"), 24)
            V.memset(v_aug[:, :, :, M_DH:M_DH + 1], 1.0).then_inc(S("v_ones"), 1)
            n = 0
            for h in range(M_HEADS):
                dve.wait_ge(S("neg_m"), h + 1)
                if h == 0:
                    dve.wait_ge(S("wcol_ready"), 1)
                else:
                    dve.wait_ge(S("num_half"), 2 * h)
                off = 0
                for j in range(NT):
                    w = (NT - j) * P
                    ins = V.tensor_scalar(decay[:, off:off + w], bank[2][:, j * P:T], wcol[:, j, h:h + 1], 0.0,
                                          ALU.add, ALU.min)
                    off += w
                ins.then_inc(S("decay_arg"), 1)
                off = 0
                dve.wait_ge(S("decay_cut"), h + 1)
                for j in range(NT):
                    w = (NT - j) * P
                    dve.wait_ge(S("qk_dot"), n + 1)
                    V.scalar_tensor_tensor(out=decay[:, off:off + w], in0=bank[4 + n % 2][:, 0:w],
                                           scalar=float(M_DH) ** -0.5, in1=decay[:, off:off + w],
                                           op0=ALU.mult, op1=ALU.mult).then_inc(S("decayed"), 1)
                    off += w
                    n += 1
                for half in range(2):
                    dve.wait_ge(S("num_half"), 2 * h + half + 1)
                    V.tensor_copy(num[:, 2 * half:2 * half + 2, h, :],
                                  bank[6 + half][:, 0:2 * (M_DH + 1)].rearrange("p (i e) -> p i e", i=2)
                                  ).then_inc(S("num_out"), 1)
            dve.wait_ge(S("num_out"), 2 * M_HEADS)
            dve.wait_ge(S("emm_ready"), 1)
            bc = lambda a, n: a.unsqueeze(3).broadcast_to([P, NT, M_HEADS, n])
            own.do(V.scalar_tensor_tensor(out=den[:, :, :], in0=num[:, :, :, M_DH], scalar=-1.0,
                                          in1=num[:, :, :, M_DH], op0=ALU.mult, op1=ALU.max))
            own.do(V.tensor_tensor(den[:, :, :], den[:, :, :], emm[:, :, :], ALU.max))
            own.do(V.reciprocal(den[:, :, :], den[:, :, :]))
            own.do(V.tensor_tensor(hm[:, :, :, :], num[:, :, :, 0:M_DH], bc(den[:, :, :], M_DH), ALU.mult))
            own.do(V.tensor_tensor(hm2[:, :, :, :], hm[:, :, :, :], hm[:, :, :, :], ALU.mult))
            own.do(V.reduce_sum(hrs[:, :, :], hm2[:, :, :, :], AX.X))
            V.tensor_scalar(hrs[:, :, :], hrs[:, :, :], 1.0 / M_DH, EPS, ALU.mult, ALU.add).then_inc(S("hm_mean"), 1)
            dve.wait_ge(S("hm_root"), 1)
            own.do(V.reciprocal(hrs[:, :, :], hrs[:, :, :]))
            V.tensor_tensor(hm[:, :, :, :], hm[:, :, :, :], bc(hrs[:, :, :], M_DH), ALU.mult).then_inc(S("hm_ready"), 1)
            dve.wait_ge(S("mo_gate"), M_HEADS)
            for h in range(M_HEADS):
                dve.wait_ge(S("hm_tr"), h + 1)
                V.scalar_tensor_tensor(out=z[:, Z_MO + h, :], in0=bank[4 + h % 2][:, :],
                                       scalar=cols[:, C_OUTN + h:C_OUTN + h + 1], in1=z[:, Z_MO + h, :],
                                       op0=ALU.mult, op1=ALU.mult).then_inc(S("cat_m"), 1)

            at_score, at_mask = 0, P
            for t in range(1, NT):
                w = (t + 1) * P
                work = score[:, at_score:at_score + w]
                dve.wait_ge(S("score_cut"), t)
                with dve.Fori(0, N_SEL // 8):
                    rnd.do(V.max(best8[:, :], work))
                    rnd.did(V.match_replace(work, best8[:, :], work, TAKEN))
                    rnd.turn_over()
                V.tensor_scalar(mask[:, at_mask:at_mask + w], work, (NEG + TAKEN) / 2, NEG, ALU.is_gt, ALU.mult
                                ).then_inc(S("mask_ready"), 1)
                at_score += w
                at_mask += w

            dve.wait_ge(S("mask0"), 1)
            n, at_mask = 0, 0
            for t in range(NT):
                w = (t + 1) * P
                if t:
                    dve.wait_ge(S("mask_ready"), t)
                for h in range(A_HEADS):
                    r = n % 2
                    dve.wait_ge(S("s_dot"), n + 1)
                    if n >= 2:
                        dve.wait_ge(S("p_tr"), n - 1)
                    own.do(V.tensor_tensor_reduce(out=prob[:, r, 0:w], in0=bank[4 + r][:, 0:w],
                                                  in1=mask[:, at_mask:at_mask + w], scale=1.0, scalar=-3.0e38,
                                                  op0=ALU.add, op1=ALU.max, accum_out=s_max[:, r:r + 1]))
                    V.tensor_scalar(s_neg[:, r:r + 1], s_max[:, r:r + 1], -A_DH ** -0.5, None, ALU.mult
                                    ).then_inc(S("s_masked"), 1)
                    def finish(m, head):
                        dve.wait_ge(S("o_dot"), m + 1)
                        own.do(V.reciprocal(s_sum[:, m % 2:m % 2 + 1], s_sum[:, m % 2:m % 2 + 1]))
                        V.tensor_scalar(att[:, head, :], bank[2 + m % 2][:, 0:A_DH], s_sum[:, m % 2:m % 2 + 1], None,
                                        ALU.mult).then_inc(S("o_out"), 1)
                    if h:
                        finish(n - 1, h - 1)
                    n += 1
                finish(n - 1, A_HEADS - 1)
                dve.wait_ge(S("o_out"), n)
                own.do(V.tensor_tensor(att2[:, :, :], att[:, :, :], att[:, :, :], ALU.mult))
                own.do(V.reduce_sum(o_rs[:, :], att2[:, :, :], AX.X))
                V.tensor_scalar(o_rs[:, :], o_rs[:, :], 1.0 / A_DH, EPS, ALU.mult, ALU.add).then_inc(S("att_mean"), 1)
                dve.wait_ge(S("att_root"), t + 1)
                own.do(V.reciprocal(o_rs[:, :], o_rs[:, :]))
                V.tensor_tensor(att[:, :, :], att[:, :, :], o_rs[:, :].unsqueeze(2).broadcast_to([P, A_HEADS, A_DH]),
                                ALU.mult).then_inc(S("att_ready"), 1)
                dve.wait_ge(S("att_tr"), t + 1)
                V.tensor_tensor(z[:, Z_IQ:Z_IQ + 4, t * P:(t + 1) * P],
                                bank[2][:, :].rearrange("p (f q) -> p f q", f=4),
                                cols[:, C_OUTN + 4:C_OUTN + 8].unsqueeze(2).broadcast_to([P, 4, P]), ALU.mult
                                ).then_inc(S("cat_a"), 1)
                at_mask += w

            for k in range(KB):
                dve.wait_ge(S("unit_done"), FIRST["o", 0] + 2 * k + 2)
                V.scalar_tensor_tensor(out=x[:, k, :], in0=tile_bank[(TILE0["o", 0] + k) % 2][:, :],
                                       scalar=ada[:, 16 + k:17 + k], in1=x[:, k, :], op0=ALU.mult, op1=ALU.add
                                       ).then_inc(S("tile_out"), 1)
            dve.wait_ge(S("tile_out"), TILE0["o", 0] + KB + 2)
            mean(1, bank[3])
            normed(1, amp2, 24)

            dve.wait_ge(S("s_ready"), NT * P_HEADS // 2)
            H = P_HEADS
            for t in range(NT):
                sl = slice(t * H, (t + 1) * H)
                for h in range(H):
                    b = lambda a, k: best[:, t * H + h, a, 8 * k:8 * k + 8]
                    bi = lambda a, k: best_iu[:, t * H + h, a, 8 * k:8 * k + 8]
                    for k in range(2):
                        for a in range(2):
                            own.did(V.max(b(a, k), s12[:, t * H + h, a, :]))
                        for a in range(2):
                            own.settle(1)
                            own.did(V.max_index(bi(a, k), b(a, k), s12[:, t * H + h, a, :]))
                        if k == 0:
                            for a in range(2):
                                own.settle(1)
                                own.did(V.match_replace(s12[:, t * H + h, a, :], b(a, 0), s12[:, t * H + h, a, :], TAKEN))
                            own.settle()
                    own.settle()
                    c0, c1 = cand[:, 0, :], cand[:, 1, :]
                    own.do(V.tensor_tensor(c0.rearrange("p (a b) -> p a b", a=16),
                                           best[:, t * H + h, 0, :].unsqueeze(2).broadcast_to([P, 16, 16]),
                                           best[:, t * H + h, 1, :].unsqueeze(1).broadcast_to([P, 16, 16]), ALU.add))
                    own.do(V.max(top[:, t * H + h, 0:8], c0))
                    own.did(V.max_index(pos_u[:, t * H + h, 0:8], top[:, t * H + h, 0:8], c0))
                    own.do(V.match_replace(c1, top[:, t * H + h, 0:8], c0, TAKEN))
                    own.do(V.max(top[:, t * H + h, 8:16], c1))
                    own.did(V.max_index(pos_u[:, t * H + h, 8:16], top[:, t * H + h, 8:16], c1))
                own.settle()
                own.did(V.tensor_copy(best_if[:, sl, :, :], best_iu[:, sl, :, :]))
                own.did(V.tensor_copy(gsum[:, sl], top[:, sl, 0]))
                own.settle()
            own.do(V.tensor_scalar(pos_f[:, 1, :, :].bitcast(u32), pos_u[:, :, :], 15, None, ALU.bitwise_and))
            own.do(V.tensor_scalar(pos_u[:, :, :], pos_u[:, :, :], 4, None, ALU.logical_shift_right))
            own.do(V.tensor_copy(pos_f[:, 1, :, :], pos_f[:, 1, :, :].bitcast(u32)))
            own.do(V.tensor_copy(pos_f[:, 0, :, :], pos_u[:, :, :]))
            for t in range(NT):
                sl = slice(t * P_HEADS, (t + 1) * P_HEADS)
                V.tensor_tensor(top[:, sl, :], top[:, sl, :], gsum[:, sl].unsqueeze(2).broadcast_to([P, P_HEADS, 16]),
                                ALU.subtract).then_inc(S("top_shift"), 1)
                for a in range(2):
                    ranks = iota[:, 0:16].unsqueeze(1).unsqueeze(1).broadcast_to([P, P_HEADS, 16, 16])
                    pf = pos_f[:, a, sl, :].unsqueeze(3).broadcast_to([P, P_HEADS, 16, 16])
                    idx = best_if[:, sl, a, :].unsqueeze(2).broadcast_to([P, P_HEADS, 16, 16])
                    own.do(V.tensor_tensor(pick[:, :, :, :], pf, ranks, ALU.is_equal))
                    own.do(V.tensor_tensor(pick[:, :, :, :], pick[:, :, :, :], idx, ALU.mult))
                    own.do(V.reduce_sum(slot_t[:, a, t * P:(t + 1) * P].rearrange("p (h k) -> p h k", h=P_HEADS),
                                        pick[:, :, :, :], AX.X))
            for t in range(NT):
                sl = slice(t * P_HEADS, (t + 1) * P_HEADS)
                dve.wait_ge(S("top_exp"), t + 1)
                own.do(V.reduce_sum(gsum[:, sl], top[:, sl, :], AX.X))
                own.do(V.reciprocal(gsum[:, sl], gsum[:, sl]))
                V.tensor_tensor(slot_t[:, 2, t * P:(t + 1) * P].rearrange("p (h k) -> p h k", h=P_HEADS), top[:, sl, :],
                                gsum[:, sl].unsqueeze(2).broadcast_to([P, P_HEADS, 16]), ALU.mult
                                ).then_inc(S("slots_ready"), 1)
            dve.wait_ge(S("slot_out"), 3)
            for k in range(3):
                ins = V.tensor_copy(slot_g[:, k, :], slot_gf[:, :])
                if k < 2:
                    own.do(ins)
                    own.do(V.tensor_tensor(slot_gf[:, :], slot_gf[:, :], slot_g[:, k, :], ALU.subtract))
            ins.then_inc(S("gate_split"), 1)
            dve.wait_ge(S("gate_split"), 1)

            def one_hots(g, i, par):
                if g or not isinstance(i, int):
                    dve.wait_ge(S("rows_used"), i + (g * (T // GT) - 1))
                keys_of = lambda table, n: table[:, ds(i * GT, GT)].unsqueeze(1).broadcast_to([P, n, GT])
                own.did(V.tensor_tensor(eq1[:, par, :, :], key_rep[:, g * GI:(g + 1) * GI, :], keys_of(slot_i1, GI),
                                        ALU.is_equal))
                V.tensor_tensor(rows2[:, par, :, :], key_rep[:, :, :], keys_of(slot_i2, N_KEYS), ALU.is_equal
                                ).then_inc(S("rows2_ready"), 1)
                own.settle()
                V.tensor_tensor(rows1[:, par, :, :, :], eq1[:, par, :, :].unsqueeze(1).broadcast_to([P, 3, GI, GT]),
                                slot_g[:, :, ds(i * GT, GT)].unsqueeze(2).broadcast_to([P, 3, GI, GT]), ALU.mult
                                ).then_inc(S("rows1_ready"), 1)

            def apply_gates(g, i, par):
                buf = (g % 2) * GI
                dve.wait_ge(S("rows_used"), i + (g * (T // GT) + 1))
                c = coef[:, buf:buf + GI, ds(i * GT, GT)]
                V.tensor_tensor(c, c, gate_bank[par][:, 0:GT * GI].rearrange("p (n e) -> p e n", n=GT), ALU.mult
                                ).then_inc(S("gated"), 1)

            def gate_group(g, between=None):
                dve.wait_ge(S("tile_out"), TILE0["u", g] + GI + 2)
                if g:
                    for d in range(4):
                        if g < GROUPS - 1:
                            dve.wait_ge(S(f"part_saved{d}"), 16 * 2 * g)
                for q in range(2):
                    one_hots(g, q, q)
                pairs = T // GT // 2
                for start, end in ((1, pairs // 2), (pairs // 2, pairs)):
                    with own.loop(start, end, 2) as i:
                        for par in range(2):
                            one_hots(g, i * 2 + par, par)
                            apply_gates(g, i * 2 + (par - 2), par)
                    if between and end < pairs:
                        between()
                for q in range(T // GT - 2, T // GT):
                    apply_gates(g, q, q % 2)

            def sums_out(g, half, ds_=range(4)):
                dve.wait_ge(S("unit_done"), FIRST["v", g] + (half + 1) * GI)
                for d in ds_:
                    k = half * 4 + d
                    if g < GROUPS - 1:
                        if half:
                            dve.wait_ge(S(f"part_saved{d}"), 16 * (2 * g + 1))
                        V.tensor_copy(y_stage[g][:, d, :], sum_bank[d][:, :]).then_inc(S("y_out"), 1)
                    else:
                        own.do(V.tensor_tensor(part[:, 2, k, :], part[:, 2, k, :], sum_bank[d][:, :], ALU.add))
                        V.scalar_tensor_tensor(out=part[:, 3, k, :], in0=part[:, 2, k, :],
                                               scalar=ada[:, 40 + k:41 + k], in1=part[:, 3, k, :],
                                               op0=ALU.mult, op1=ALU.add).then_inc(S("x3_ready"), 1)

            def v_phase(g):
                coef_lows(dve, V.tensor_tensor, g, None, (lambda: sums_out(g, 0, range(1)),
                                                          lambda: sums_out(g, 0, range(1, 4))))
                sums_out(g, 1)

            for g in range(GROUPS - 2):
                gate_group(g)
                v_phase(g)
            gate_group(GROUPS - 2)
            gate_group(GROUPS - 1, lambda: sums_out(GROUPS - 2, 0))
            sums_out(GROUPS - 2, 1)
            def combine():
                dve.wait_ge(S("part_back"), 16 * GROUPS)
                for k in range(KB):
                    own.did(V.tensor_tensor(part[:, 0, k, :], part[:, 0, k, :], part[:, 1, k, :], ALU.add))
                own.settle()
                for k in range(KB):
                    own.did(V.tensor_tensor(part[:, 2, k, :], part[:, 2, k, :], part[:, 0, k, :], ALU.add))
                own.settle()
            def first_half_out():
                combine()
                sums_out(GROUPS - 1, 0, range(1))
            coef_lows(dve, V.tensor_tensor, GROUPS - 1, None,
                      (first_half_out, lambda: sums_out(GROUPS - 1, 0, range(1, 4))))
            sums_out(GROUPS - 1, 1)
            dve.wait_ge(S("x3_ready"), KB)
            mean(2, bank[3], rstd_end)
            for k in range(KB):
                V.scalar_tensor_tensor(out=part[:, 2, k, :], in0=part[:, 3, k, :], scalar=cols[:, C_FG + k:C_FG + k + 1],
                                       in1=rstd_end[:, :], op0=ALU.mult, op1=ALU.mult).then_inc(S("out_ready"), 1)

        @block.tensor
        def _(pe):
            mm = nc.tensor.matmul

            def square_sums(n, sq=sq):
                for k in range(KB):
                    pe.wait_ge(S("x_sq"), KB * n + k + 1)
                    ins = mm(bank[3][:, :], ones[:, :], sq[:, k, :], start=(k == 0), stop=(k == KB - 1))
                ins.then_inc(S("sq_sum"), 1)

            def ada_chunk(c):
                pe.wait_ge(S(f"ada_in{c % 3}"), 16 * (c // 3 + 1))
                for j in range(2):
                    for k in range(KB):
                        ins = mm(bank[2][:, 2 * c + j:2 * c + j + 1], ada_w[:, c % 3, k, j * P:(j + 1) * P],
                                 silu_c[:, k:k + 1], start=(k == 0), stop=(k == KB - 1))
                ins.then_inc(S("ada_used"), 1)
                return ins

            def split_unit(u, out_of, start, stop):
                s = u % SPLIT_SLOTS
                half = 4 * (not start)
                for k in range(4):
                    wh = w_hi[:, s, k * P:(k + 1) * P]
                    mm(out_of, wh, hs_hi[:, half + k, :], start=(start and k == 0), stop=False)
                    mm(out_of, wh, hs_lo[:, half + k, :], start=False, stop=False)
                    ins = mm(out_of, w_lo[:, s, k * P:(k + 1) * P], hs_hi[:, half + k, :], start=False,
                             stop=(stop and k == 3))
                return ins

            def tile(phase, i, j, extra=None):
                u0, t0 = FIRST[phase] + 2 * j, TILE0[phase] + j
                dst = tile_bank[t0 % 2][:, :]
                pe.wait_ge(S("tile_out"), i * 2 + (t0 + 1))
                for h in range(2):
                    pe.wait_ge(S("w_split"), i * 4 + (u0 + h + 1))
                    split_unit(u0 + h, dst, h == 0, h == 1).then_inc(S("unit_done"), 1)
                    if extra:
                        extra(i, 2 * j + h)

            def tiles(phase, count, extra=None):
                with pe.Fori(0, count // 2) as i:
                    for j in range(2):
                        tile(phase, i, j, extra)

            def transposes(dst, sources):
                for n, src in enumerate(sources):
                    w = src.shape[0]
                    ins = nc.tensor.transpose(dst[:, n * w:(n + 1) * w], src, ident[0:w, 0:w])
                return ins

            pe.wait_ge(S("consts"), 1)
            square_sums(0)
            pe.wait_ge(S("c_silu"), 1)
            for c in range(8):
                ada_chunk(c)
            pe.wait_ge(S("h_low"), KB)
            tiles(("z", 0), Z_TILES - 1)
            tile(("z", 0), (Z_TILES - 1) // 2, 0)
            for c in range(8, 24):
                ada_chunk(c)
            pe.wait_ge(S("tile_out"), Z_TILES + 2)
            transposes(bank[3], [z[:, Z_MISC, t * P:(t + 1) * P] for t in range(NT)]).then_inc(S("misc_tr"), 1)
            n = 0
            for t in range(1, NT):
                for h in range(IDX_HEADS):
                    if n >= 2:
                        pe.wait_ge(S("idx_relu"), n - 1)
                    r = slice(64 * (h % 2), 64 * (h % 2) + 64)
                    mm(bank[4 + n % 2][:, 0:(t + 1) * P], z[r, Z_IQ + h // 2, t * P:(t + 1) * P],
                       z[r, Z_IK, 0:(t + 1) * P], start=True, stop=True).then_inc(S("idx_dot"), 1)
                    n += 1
            pe.wait_ge(S("idx_relu"), n)
            for h in range(M_HEADS):
                if h >= 2:
                    pe.wait_ge(S("v_ready"), h - 1)
                transposes(bank[4 + h % 2], [z[:, Z_MV + h, t * P:(t + 1) * P] for t in range(NT)]
                           ).then_inc(S("v_tr"), 1)
            pe.wait_ge(S("rows_ready"), 1)
            pe.wait_ge(S("misc_ready"), 1)
            for k, row in enumerate((R_W, R_M)):
                for j in range(NT):
                    c = 16 * k + 4 * j
                    ins = nc.tensor.transpose(bank[3][:, c:c + 4], rows[0:4, row, j * P:(j + 1) * P], ident[0:4, 0:4])
            ins.then_inc(S("col_tr"), 1)
            pe.wait_ge(S("qk_ready"), 2 * M_HEADS)
            pe.wait_ge(S("v_ready"), M_HEADS)
            pe.wait_ge(S("v_ones"), 1)
            pe.wait_ge(S("ada_ready"), 1)
            n = 0
            for h in range(M_HEADS):
                if h:
                    pe.wait_ge(S("decay_arg"), h)
                mm(bank[2][:, :], sel[0:4, h, :], rows[0:4, R_MX, :], start=True, stop=True).then_inc(S("neg_m"), 1)
                for j in range(NT):
                    if n >= 2:
                        pe.wait_ge(S("decayed"), n - 1)
                    mm(bank[4 + n % 2][:, 0:(NT - j) * P], qk[:, M_HEADS + h, j * P:(j + 1) * P], qk[:, h, j * P:T],
                       start=True, stop=True).then_inc(S("qk_dot"), 1)
                    n += 1
                pe.wait_ge(S("decayed"), n)
                for i in range(NT):
                    if h and i % 2 == 0:
                        pe.wait_ge(S("num_out"), 2 * (h - 1) + i // 2 + 1)
                    c = (i % 2) * (M_DH + 1)
                    off = 0
                    for j in range(i + 1):
                        a = off + (i - j) * P
                        ins = mm(bank[6 + i // 2][:, c:c + M_DH + 1], decay[:, a:a + P], v_aug[:, j, h, :],
                                 start=(j == 0), stop=(j == i))
                        off += (NT - j) * P
                    if i % 2:
                        ins.then_inc(S("num_half"), 1)
            pe.wait_ge(S("hm_ready"), 1)
            for h in range(M_HEADS):
                if h >= 2:
                    pe.wait_ge(S("cat_m"), h - 1)
                transposes(bank[4 + h % 2], [hm[:, t, h, :] for t in range(NT)]).then_inc(S("hm_tr"), 1)
            pe.wait_ge(S("cat_m"), M_HEADS)

            def scores(n):
                t, h = divmod(n, A_HEADS)
                if n >= 2:
                    pe.wait_ge(S("s_masked"), n - 1)
                r = slice(64 * (h % 2), 64 * (h % 2) + 64)
                mm(bank[4 + n % 2][:, 0:(t + 1) * P], z[r, Z_AQ + h // 2, t * P:(t + 1) * P],
                   z[r, Z_AK, 0:(t + 1) * P], start=True, stop=True).then_inc(S("s_dot"), 1)

            heads = NT * A_HEADS
            pe.wait_ge(S("emm_ready"), 1)
            scores(0)
            for n in range(heads):
                t = n // A_HEADS
                if n + 1 < heads:
                    scores(n + 1)
                pe.wait_ge(S("p_ready"), n + 1)
                if n >= 2:
                    pe.wait_ge(S("pt_ready"), n - 1)
                transposes(bank[6 + n % 2], [prob[:, n % 2, s * P:(s + 1) * P] for s in range(t + 1)]
                           ).then_inc(S("p_tr"), 1)
                pe.wait_ge(S("pt_ready"), n + 1)
                if n >= 2:
                    pe.wait_ge(S("o_out"), n - 1)
                for s in range(t + 1):
                    ins = mm(bank[2 + n % 2][:, 0:A_DH], prob_t[:, n % 2, s, :], misc_t[:, s, MISC_AV:MISC_AV + A_DH],
                             start=(s == 0), stop=(s == t))
                ins.then_inc(S("o_dot"), 1)
                if n % A_HEADS == A_HEADS - 1:
                    pe.wait_ge(S("att_ready"), t + 1)
                    transposes(bank[2], [att[:, 2 * f:2 * f + 2, :].rearrange("p h d -> p (h d)") for f in range(4)]
                               ).then_inc(S("att_tr"), 1)
                    pe.wait_ge(S("cat_a"), t + 1)
            pe.wait_ge(S("cat_low"), KB)
            tiles(("o", 0), KB)
            square_sums(1)
            pe.wait_ge(S("h_low"), 2 * KB)
            tiles(("q", 0), KB)
            pe.wait_ge(S("tile_out"), TILE0["u", 0] + 2)
            pe.wait_ge(S("keys_in"), 16)
            for k in range(NT * P_HEADS // 2):
                t = k // 4
                if k >= 2:
                    pe.wait_ge(S("s_ready"), k - 1)
                for a in range(2):
                    h = 2 * (k % 4) + a
                    ins = mm(bank[4 + k % 2][:, a * 256:(a + 1) * 256], q_t[:, h, t * P:(t + 1) * P], keys[:, h, :],
                             start=True, stop=True)
                ins.then_inc(S("keys_dot"), 1)

            def gates(g, q, par):
                pe.wait_ge(S("gated"), q + (g * (T // GT) + 1))
                pe.wait_ge(S("rows1_ready"), q + (g * (T // GT) + 1))
                pe.wait_ge(S("rows2_ready"), q + (g * (T // GT) + 1))
                for n in range(GT):
                    dst = gate_bank[par][:, n * GI:(n + 1) * GI]
                    for k in range(3):
                        ins = mm(dst, rows2[:, par, :, n], rows1[:, par, k, :, n], start=(k == 0), stop=(k == 2))
                ins.then_inc(S("rows_used"), 1)

            def v_units(g, with_gates):
                first = FIRST["v", g]
                for half in range(2):
                    f = first + half * GI

                    def unit(i, u, start, stop):
                        s = (f + u) % SPLIT_SLOTS
                        pe.wait_ge(S("w_split"), i * 4 + (f + u + 1))
                        pe.wait_ge(S(f"c_split{g}"), i * 4 + (half * GI + u + 1))
                        for d in range(4):
                            if start and (g or half):
                                if g == GROUPS - 1 and half:
                                    pe.wait_ge(S("x3_ready"), d + 1)
                                else:
                                    pe.wait_ge(S("y_out"), g * KB + (half - 1) * 4 + d + 1)
                            wh, wl = (w[:, s, d * P:(d + 1) * P] for w in (w_hi, w_lo))
                            dst = sum_bank[d][:, :]
                            mm(dst, wh, c_hi[:, s, :], start=start, stop=False)
                            mm(dst, wh, c_lo[:, s, :], start=False, stop=False)
                            ins = mm(dst, wl, c_hi[:, s, :], start=False, stop=stop)
                        ins.then_inc(S("unit_done"), 1)
                        if with_gates is not None:
                            gates(with_gates, i * 4 + (half * GI + u), u % 2)

                    for u in range(4):
                        unit(0, u, u == 0, False)
                    with pe.Fori(1, GI // 4 - 1) as i:
                        for u in range(4):
                            unit(i, u, False, False)
                    for u in range(4):
                        unit(GI // 4 - 1, u, False, u == 3)

            tiles(("u", 0), GI)
            pe.wait_ge(S("s_ready"), NT * P_HEADS // 2)
            pe.wait_ge(S("slots_ready"), NT)
            for k in range(3):
                transposes(bank[4 + k], [slot_t[:, k, t * P:(t + 1) * P] for t in range(NT)]).then_inc(S("slot_tr"), 1)
            tiles(("u", 1), GI, lambda i, q: gates(0, i * 4 + q, q % 2))
            pe.wait_ge(S("slot_out"), 3)
            for g in range(GROUPS):
                v_units(g, GROUPS - 1 if g == GROUPS - 2 else None)
                if g + 2 < GROUPS:
                    tiles(("u", g + 2), GI, lambda i, q: gates(g + 1, i * 4 + q, q % 2))
            square_sums(2, sq_end)


_INS = ["x_t", "cols", "wada", "stream", "keys"]


def lay_out(inputs):
    import numpy as np

    a = {k: np.asarray(v) for k, v in inputs.items()}
    f32 = np.float32
    by_block = lambda v: v.reshape(-1, P).T
    x_t = a["x"].reshape(T, KB, P).transpose(2, 1, 0)

    sizes = (512, 512, 512, 512, 4, 4, 512, 64, 64, 512, 64, 8)
    starts = np.concatenate([[0], np.cumsum(sizes)])
    mq, mk, mv, mo, mi, mf, aq, ak, av, iq, ik, iw = (slice(starts[n], starts[n + 1]) for n in range(12))
    w_in, b_in = a["w_in"][0], a["b_in"][0][None, :]

    def arrange(m):
        out = np.zeros((m.shape[0], Z_TILES * P), f32)
        put = lambda c, s: out.__setitem__((slice(None), slice(c, c + s.stop - s.start)), m[:, s])
        put(Z_IQ * P, iq)
        put(Z_IK * P, ik)
        put(Z_IK * P + 64, ik)
        put(Z_MISC * P + MISC_MI, mi)
        put(Z_MISC * P + MISC_IW, iw)
        put(Z_MISC * P + MISC_MF, mf)
        put(Z_MISC * P + MISC_AV, av)
        put(Z_AQ * P, aq)
        put(Z_AK * P, ak)
        put(Z_AK * P + 64, ak)
        for c, s in ((Z_MQ, mq), (Z_MK, mk), (Z_MV, mv), (Z_MO, mo)):
            put(c * P, s)
        return out

    cols = np.concatenate([
        by_block(a["c"].reshape(-1)), by_block(a["b_ada"].reshape(-1)), by_block(a["norm1_g"].reshape(-1)),
        by_block(arrange(b_in).reshape(-1)),
        a["conv_qk"][0].reshape(CONV_W, 8, P).transpose(2, 1, 0).reshape(P, 32),
        by_block(a["out_norm_m"].reshape(-1)), by_block(a["out_norm_a"].reshape(-1)),
        by_block(a["norm2_g"].reshape(-1)), by_block(a["final_g"].reshape(-1))], axis=1)
    wada = a["w_ada"][0].reshape(KB, P, 24, 256).transpose(2, 1, 0, 3)

    def units(w):
        n = w.shape[1] // P
        return w.reshape(2, 4, P, n, P).transpose(3, 0, 2, 1, 4).reshape(2 * n, P, UNIT)

    u, v = a["peer_u"][0], a["peer_v"][0]
    order, first = stream_order()
    stream = np.empty((UNITS, P, UNIT), f32)
    for name, g, n in order:
        e = slice(g * GI * N_KEYS, (g + 1) * GI * N_KEYS)
        if name == "u":
            part = units(u[e].T)
        elif name == "v":
            part = v[e].reshape(GI, P, 2, UNIT).transpose(2, 0, 1, 3).reshape(n, P, UNIT)
        else:
            part = units({"z": arrange(w_in) if name == "z" else None, "o": a["w_out"][0], "q": a["w_peer_q"][0]}[name])
        stream[first[name, g]:first[name, g] + n] = part
    keys = np.zeros((P, P_HEADS, 2 * N_KEYS), f32)
    sub = a["peer_sub_keys"][0]
    for side in range(2):
        keys[side * 64:(side + 1) * 64, :, side * N_KEYS:(side + 1) * N_KEYS] = sub[:, side].transpose(2, 0, 1)
    return {"x_t": x_t, "cols": cols, "wada": wada, "stream": stream, "keys": keys}


def kernel(**inputs):
    import numpy as np
    import concourse.bacc as bacc
    from concourse.bass_utils import run_bass_kernel_spmd

    nc = bacc.Bacc("TRN2", target_bir_lowering=False, num_devices=1)
    laid = lay_out(inputs)
    arrays, args = {}, []
    for name in _INS:
        arr = np.ascontiguousarray(laid[name])
        arrays[f"in_{name}"] = arr
        args.append(nc.dram_tensor(f"in_{name}", arr.shape, mybir.dt.float32, kind="ExternalInput").ap())
    out = nc.dram_tensor("out_t", [P, KB, T], mybir.dt.float32, kind="ExternalOutput").ap()
    build_layer(nc, *args, out)
    r = run_bass_kernel_spmd(nc, [arrays], core_ids=[0])
    return np.ascontiguousarray(np.asarray(r.results[0]["out_t"]).transpose(2, 1, 0)).reshape(1, T, D)
```

```python
import concourse.bass as bass
from concourse import mybir
from contextlib import ExitStack

D = 1024
T = 512
P = 128
KB = D // P
NT = T // P
CONV_W = 4
M_HEADS, M_DH = 4, 128
A_HEADS, A_DH = 8, 64
IDX_HEADS = 8
N_SEL = 128
P_HEADS, N_KEYS, P_TOPK = 8, 128, 16
EPS = 1e-6

Z_IQ, Z_IK, Z_MISC, Z_MQ, Z_MK, Z_AQ, Z_AK, Z_MV, Z_MO = 0, 4, 5, 6, 10, 14, 18, 19, 23
Z_TILES = 27
Z_HEAD = 6
ADA_HEAD, ADA_CHUNKS = 8, 24
ADA_DVE = 5
MISC_MI, MISC_IW, MISC_MF, MISC_AV = 0, 8, 32, 64

C_C, C_BADA, C_N1, C_BIN, C_CONV = 0, 8, 56, 64, 91
C_OUTN, C_N2, C_FG, C_END = 123, 131, 139, 147

GROUPS = 4
GI = N_KEYS // GROUPS
UNIT = 512
RAW_SLOTS, SPLIT_SLOTS = 4, 2
ZU, OU, QU, EU = 2 * Z_TILES, 2 * KB, 2 * KB, 2 * GI
UNITS = ZU + OU + QU + 2 * GROUPS * EU
GT = 8
NEG, TAKEN = -1e30, -3e30


def stream_order():
    order = [("z", 0, ZU), ("o", 0, OU), ("q", 0, QU), ("u", 0, EU), ("u", 1, EU)]
    for g in range(GROUPS - 2):
        order += [("v", g, EU), ("u", g + 2, EU)]
    order += [("v", GROUPS - 2, EU), ("v", GROUPS - 1, EU)]
    first, at = {}, 0
    for name, g, n in order:
        first[name, g] = at
        at += n
    return order, first


class Steps:

    def __init__(self, eng, sem):
        self.eng, self.sem, self.n, self.turn, self.skipped = eng, sem, 0, None, 0

    def did(self, ins):
        ins.then_inc(self.sem, 1)
        self.n += 1

    def settle(self, back=0):
        n = self.n - back
        self.eng.wait_ge(self.sem, n if self.turn is None else self.turn + (n - self.skipped))

    def do(self, ins):
        self.did(ins)
        self.settle()

    def loop(self, start, end, per):
        return _StepLoop(self, start, end, per)


class Rounds(Steps):

    def turn_over(self):
        self.settle()
        self.eng.sem_clear(self.sem)
        self.n = 0


class _StepLoop:
    def __init__(self, steps, start, end, per):
        self.s, self.start, self.end, self.per = steps, start, end, per

    def __enter__(self):
        self.ctx = self.s.eng.Fori(self.start, self.end)
        i = self.ctx.__enter__()
        self.before = self.s.n
        self.s.turn, self.s.skipped = i * self.per, self.start * self.per
        return i

    def __exit__(self, *error):
        assert error[0] or self.s.n - self.before == self.per, (self.s.n - self.before, self.per)
        self.s.turn = None
        self.s.n = self.before + self.per * (self.end - self.start)
        return self.ctx.__exit__(*error)


def build_layer(nc, x_t, cols_in, wada_in, stream_in, keys_in, out):
    fp32, fp32r, u32, bf16 = mybir.dt.float32, mybir.dt.float32r, mybir.dt.uint32, mybir.dt.bfloat16
    ALU, ACT, AX = mybir.AluOpType, mybir.ActivationFunctionType, mybir.AxisListType
    ds = bass.ds
    ORDER, FIRST = stream_order()

    x2_dram = nc.dram_tensor("x2_dram", [P, KB, T], fp32, kind="Internal").ap()
    part_dram = nc.dram_tensor("part_dram", [GROUPS - 1, KB, P, T], fp32, kind="Internal").ap()

    BASE = 16512

    def at(name, shape, offset, dt=fp32):
        size = 2 if dt == bf16 else 4
        for n in shape[1:]:
            size *= n
        assert BASE + offset + size <= 229344, (name, offset, size)
        return nc.alloc_sbuf_tensor_at(name, shape, dt, offset=BASE + offset)

    coef = at("coef", [P, 2 * GI, T], 0)
    A0 = 4 * 2 * GI * T
    hs_hi = at("hs_hi", [P, KB, T], A0, fp32r)
    hs_lo = at("hs_lo", [P, KB, T], A0 + 16384, fp32r)
    raw = at("raw", [P, RAW_SLOTS, UNIT], A0 + 32768)
    w_hi = at("w_hi", [P, SPLIT_SLOTS, UNIT], A0 + 40960, fp32r)
    w_lo = at("w_lo", [P, SPLIT_SLOTS, UNIT], A0 + 45056, fp32r)
    B0 = A0 + 49152
    c_hi = at("c_hi", [P, SPLIT_SLOTS, T], B0, fp32r)
    c_lo = at("c_lo", [P, SPLIT_SLOTS, T], B0 + 4096, fp32r)
    slot_i1 = at("slot_i1", [P, T], B0 + 8192, bf16)
    slot_i2 = at("slot_i2", [P, T], B0 + 9216, bf16)
    slot_g = at("slot_g", [P, 3, T], B0 + 10240, bf16)
    eq1 = at("eq1", [P, 2, GI, GT], B0 + 15360, bf16)
    rows1 = at("rows1", [P, 2, 3, GI, GT], B0 + 16384, bf16)
    rows2 = at("rows2", [P, 2, N_KEYS, GT], B0 + 19456, bf16)
    y_stage = [at("y_stage", [P, 4, T], B0 + 15360)] * 2 + [at("y_stage2", [P, 4, T], A0)]
    C0 = B0 + 27648
    cols = at("cols", [P, C_END], C0)
    ada = at("ada", [P, 48], C0 + 608)
    amp1 = at("amp1", [P, KB], C0 + 800)
    amp2 = at("amp2", [P, KB], C0 + 832)
    iota = at("iota", [P, N_KEYS], C0 + 864)
    ones = at("ones", [P, P], C0 + 1376)
    ident = at("ident", [P, P], C0 + 1888)
    silu_c = at("silu_c", [P, KB], C0 + 2400)
    key_rep = at("key_rep", [P, N_KEYS, GT], C0 + 2432, bf16)

    def fa(name, shape, offset, dt=fp32):
        return at(name, shape, 4 * offset, dt)

    def fb(name, shape, offset, dt=fp32):
        return at(name, shape, B0 + 4 * offset, dt)

    x = fa("x", [P, KB, T], 0)
    z = fa("z", [P, Z_TILES, T], 4096)
    ada_w0 = fa("ada_w0", [P, ADA_HEAD, KB, 256], 16384)
    ada_acc0 = fa("ada_acc0", [P, ADA_HEAD, 256], 12800)
    ada_w = fa("ada_w", [P, 3, KB, 256], 17920)
    qk = fa("qk", [P, 2 * M_HEADS, T], 24064)
    mask = fa("mask", [P, 1280], 28160)
    score = fa("score", [P, 1152], 29440)
    relu = fa("relu", [P, 2, T], 30592)
    misc_t = fa("misc_t", [P, NT, P], 31616)
    emm = fa("emm", [P, NT, M_HEADS], 32128)
    wcol = fa("wcol", [P, NT, M_HEADS], 32144)
    den = fa("den", [P, NT, M_HEADS], 32160)
    hrs = fa("hrs", [P, NT, M_HEADS], 32176)
    ada_acc = fb("ada_acc", [P, 2, 256], 6200)
    best8 = fb("best8", [P, 3 * 8], 6144)
    s_max = fa("s_max", [P, 4], 32192)
    s_sum = fa("s_sum", [P, 4], 32200)
    s_neg = fa("s_neg", [P, 4], 32208)
    o_rs = fa("o_rs", [P, NT, A_HEADS], 32216)
    v_aug = fa("v_aug", [P, NT, M_HEADS, M_DH + 1], 4096 + T * Z_IQ)
    decay = [fa(f"decay{n}", [P, 1280], o) for n, o in enumerate((29440, 19984, 21264))]
    num = fa("num", [P, NT, M_HEADS, M_DH + 1], 17920)
    hm = fa("hm", [P, NT, M_HEADS, M_DH], 4096 + T * Z_MQ)
    hm2 = fa("hm2", [P, NT, M_HEADS, M_DH], 4096 + T * Z_MK)
    h_tmp = fa("h_tmp", [P, KB, T], 4096)
    rstd = fa("rstd", [P, T], 4096 + T * KB)
    sq = fa("sq", [P, KB, T], 4096 + T * (KB + 1))
    prob = fb("prob", [P, 3, T], 0)
    prob_t = fb("prob_t", [P, 2, NT, P], 1536)
    att = fa("att", [P, NT, A_HEADS, A_DH], 24064)
    att2 = fb("att2", [P, A_HEADS, A_DH], 2560)
    rows = fb("rows", [P, 5, T], 3072)
    R_LF, R_B, R_W, R_MX, R_M = range(5)
    sel = fb("sel", [P, M_HEADS, P], 5632)
    q_t = fa("q_t", [P, P_HEADS, T], 4096)
    s12 = fa("s12", [P, NT * P_HEADS, 2, N_KEYS], 16384)
    keys = fa("keys", [P, P_HEADS, 2 * N_KEYS], 24576)
    best = fa("best", [P, NT * P_HEADS, 2, P_TOPK], 26624)
    best_iu = fa("best_iu", [P, NT * P_HEADS, 2, P_TOPK], 27648, u32)
    top = fa("top", [P, NT * P_HEADS, P_TOPK], 28672)
    pos_u = fa("pos_u", [P, NT * P_HEADS, P_TOPK], 29184, u32)
    cand = fa("cand", [P, 2, P_TOPK * P_TOPK], 29696)
    gsum = fa("gsum", [P, NT * P_HEADS], 30208)
    best_if = fb("best_if", [P, NT * P_HEADS, 2, P_TOPK], 0)
    pos_f = fb("pos_f", [P, 2, NT * P_HEADS, P_TOPK], 1024)
    pick = fa("pick", [P, P_HEADS, P_TOPK, P_TOPK], 16384)
    slot_t = fa("slot_t", [P, 3, NT * P_HEADS * P_TOPK], 18432)
    slot_gf = fa("slot_gf", [P, T], 19968)
    part = fa("part", [P, 4, KB, T], 0)
    sq_end = fa("sq_end", [P, KB, T], 16384)
    rstd_end = fa("rstd_end", [P, T], 20480)

    bank = [nc.alloc_psum_tensor(f"bank{i}", [P, 512], fp32) for i in range(8)]

    ctx = ExitStack()
    with ctx:
        names = {}

        def S(name):
            if name not in names:
                names[name] = ctx.enter_context(nc.semaphore(name))
            return names[name]

        raw_ready = [S(f"raw_ready{i}") for i in range(RAW_SLOTS)]
        block = ctx.enter_context(nc.Block())

        tile_bank = bank[0:2]
        gate_bank = bank[2:4]
        sum_bank = bank[4:8]

        def ada_loads(c):
            return (c - ADA_HEAD) // 3 + 1

        ADA_BESIDE = list(range(1, 8)) + list(range(9, 15)) + [19, 23, Z_TILES - 1]
        HM_TR = (8, 9, 11, 12)
        ATT_TR = 2 * A_HEADS

        def att_bank(t):
            return bank[t % 2] if t < NT - 1 else bank[2]

        POOL_ADA_TILES = (14, 18, 22)
        POOL_ADA = 30
        V_TR = Z_MV + 3
        TILE0 = {("z", 0): 0, ("o", 0): Z_TILES, ("q", 0): Z_TILES + KB}
        for g in range(GROUPS):
            TILE0["u", g] = Z_TILES + 2 * KB + g * GI

        @block.sync
        def _(sp):
            sp.wait_ge(S("x_in"), 16)
            for c in range(ADA_HEAD):
                sp.dma_start(ada_w0[:, c, :, :], wada_in[c]).then_inc(S(f"ada_head{c}"), 16)
            for n in range(RAW_SLOTS):
                sp.dma_start(raw[:, n, :], stream_in[n]).then_inc(raw_ready[n], 16)

            def refill(n, slot):
                sp.wait_ge(S("w_split"), n - (RAW_SLOTS - 1))
                src = stream_in[n] if isinstance(n, int) else stream_in[ds(n, 1), :, :].rearrange("a p f -> (a p) f")
                sp.dma_start(raw[:, slot, :], src).then_inc(raw_ready[slot], 16)

            def refills(first, end):
                turns = (end - first) // RAW_SLOTS
                if turns:
                    with sp.Fori(0, turns) as i:
                        for s in range(RAW_SLOTS):
                            refill(i * RAW_SLOTS + (first + s), (first + s) % RAW_SLOTS)
                for n in range(first + turns * RAW_SLOTS, end):
                    refill(n, n % RAW_SLOTS)

            at = RAW_SLOTS
            for g in range(GROUPS - 1):
                for half in range(2):
                    end = FIRST["v", g] + (half + 1) * GI + RAW_SLOTS
                    refills(at, end)
                    at = end
                    for d in range(4):
                        k = half * 4 + d
                        sp.wait_ge(S("y_out"), g * KB + k + 1)
                        sp.dma_start(part_dram[g, k], y_stage[g][:, d, :]).then_inc(S(f"part_saved{d}"), 16)
            sp.wait_ge(S("x2_saved"), 16)
            for d in range(4):
                sp.wait_ge(S(f"part_saved{d}"), 16 * 2 * (GROUPS - 1))
            sp.wait_ge(S("c_split2"), EU)
            with sp.Fori(0, KB) as k:
                sp.dma_start(part[:, 3, ds(k, 1), :], x2_dram[:, ds(k, 1), :]).then_inc(S("x2_back"), 16)
                for s in range(4):
                    refill(k * 4 + (at + s), (at + s) % RAW_SLOTS)
                    if s < GROUPS - 1:
                        sp.dma_start(part[:, s, ds(k, 1), :], part_dram[s, ds(k, 1), :, :].rearrange("k p t -> p k t")
                                     ).then_inc(S("part_back"), 16)
            refills(at + 4 * KB, UNITS)

        def coef_lows(eng, own, subtract, g, other=None, halfway=(), beside=None):
            first, buf = FIRST["v", g], (g % 2) * GI

            def clow(k, s, i1):
                eng.wait_ge(S(f"c_high{g}"), k + 1)
                src = coef[:, i1, :] if isinstance(i1, int) else coef[:, ds(i1, 1), :]
                subtract(c_lo[:, s % SPLIT_SLOTS, :], src, c_hi[:, s % SPLIT_SLOTS, :].bitcast(fp32), ALU.subtract
                         ).then_inc(S(f"c_split{g}"), 1)

            clow(0, first, buf)
            clow(1, first + 1, buf + 1)
            halfway = list(halfway)
            for half in range(2):
                f = half * GI
                along = beside if half else None
                with (own.loop(0, GI // 4 - 1, 3) if along else eng.Fori(0, GI // 4 - 1)) as i:
                    for u in range(4):
                        if other:
                            other(i * 4 + (first + f + u + 2), first + f + u + 2)
                        clow(i * 4 + (f + u + 2), first + u, i * 4 + (buf + u + 2))
                        if along and u < 3:
                            along(i, u)
                for u in range(4):
                    k = GI - 4 + u + 2
                    if other:
                        other(first + f + k, first + f + k)
                    if k < GI or half == 0:
                        clow(f + k, first + k, buf + k % GI)
                    if along and u < 3:
                        along(GI // 4 - 1, u)
                    if k >= GI and half == 0 and halfway:
                        halfway.pop(0)()

        @block.gpsimd
        def _(pool):
            own = Steps(pool, S("pool_own"))
            own.do(pool.memset(ones[:, :], 1.0))
            own.do(pool.memset(ident[:, :], 0.0))
            own.do(pool.affine_select(out=ident[:, :], in_=ident[:, :], compare_op=ALU.not_equal, fill=1.0, base=0,
                                      pattern=[[-1, P]], channel_multiplier=1))
            own.do(pool.iota(iota[:, :], pattern=[[1, N_KEYS]], base=0, channel_multiplier=0,
                             allow_small_or_imprecise_dtypes=True))
            own.do(pool.iota(key_rep[:, :, :], pattern=[[1, N_KEYS], [0, GT]], base=0, channel_multiplier=0,
                             allow_small_or_imprecise_dtypes=True))
            own.do(pool.memset(sel[:, :, :], 0.0))
            own.do(pool.affine_select(out=sel[:, :, :], in_=sel[:, :, :], compare_op=ALU.not_equal, fill=-1.0, base=0,
                                      pattern=[[-1, M_HEADS], [0, P]], channel_multiplier=1))
            pool.sem_inc(S("consts"), 1)

            def norm_low(n):
                for k in range(KB // 2):
                    pool.wait_ge(S("h_high"), KB * n + k + 1)
                    pool.tensor_tensor(hs_lo[:, k, :], h_tmp[:, k, :], hs_hi[:, k, :].bitcast(fp32), ALU.subtract
                                       ).then_inc(S("h_low"), 1)

            def low(n, slot):
                pool.wait_ge(S("w_high"), n + 1)
                pool.tensor_tensor(w_lo[:, slot % SPLIT_SLOTS, :], raw[:, slot % RAW_SLOTS, :],
                                   w_hi[:, slot % SPLIT_SLOTS, :].bitcast(fp32), ALU.subtract).then_inc(S("w_split"), 1)

            def lows(first, count):
                with pool.Fori(0, count // 4) as i:
                    for u in range(4):
                        low(i * 4 + (first + u), first + u)
                for n in range(first + count // 4 * 4, first + count):
                    low(n, n)

            pool.wait_ge(S("rstd0"), 1)
            pool.wait_ge(S("x_in"), 16)
            for k in range(KB):
                own.did(pool.tensor_tensor(h_tmp[:, k, :], x[:, k, :], rstd[:, :], ALU.mult))
            own.settle()
            pool.sem_inc(S("x_scaled"), 1)
            low(0, 0)
            low(1, 1)
            norm_low(0)
            own.do(pool.memset(mask[:, 0:P], 0.0))
            pool.affine_select(out=mask[:, 0:P], in_=mask[:, 0:P], compare_op=ALU.is_ge, fill=NEG, base=0,
                               pattern=[[-1, P]], channel_multiplier=1).then_inc(S("mask0"), 1)
            lows(2, POOL_ADA - 2)
            for n in range(ZU + 2 - POOL_ADA):
                low(POOL_ADA + n, POOL_ADA + n)
                c, k = ADA_CHUNKS - 3 + n // KB, n % KB
                if c < ADA_CHUNKS:
                    w, acc = ada_w[:, c % 3, :, :], ada_acc[:, c % 2, :]
                    if k == 0:
                        continue
                    if k == 1:
                        pool.wait_ge(S("ada_scaled"), ADA_HEAD + c - (ADA_CHUNKS - 3) + 1)
                        pool.wait_ge(S("ada_used"), c - 1)
                    else:
                        own.settle()
                    ins = pool.tensor_tensor(acc, w[:, 0, :] if k == 1 else acc, w[:, k, :], ALU.add)
                    if k < KB - 1:
                        own.did(ins)
                    else:
                        ins.then_inc(S("ada_summed_pool"), 1)
            for h in range(M_HEADS):
                pool.wait_ge(S("decay_exp"), h + 1)
                off = 0
                for j in range(NT):
                    blk = decay[h % 3][:, off:off + P]
                    ins = pool.affine_select(out=blk, in_=blk, compare_op=ALU.is_ge, fill=0.0, base=0,
                                             pattern=[[1, P]], channel_multiplier=-1)
                    off += (NT - j) * P
                ins.then_inc(S("decay_cut"), 1)
            for k in range(KB):
                src = z[:, Z_MO + k, :] if k < 4 else z[:, Z_IQ + k - 4, :]
                pool.wait_ge(S("cat_high"), k + 1)
                pool.tensor_tensor(hs_lo[:, k, :], src, hs_hi[:, k, :].bitcast(fp32), ALU.subtract
                                   ).then_inc(S("cat_low"), 1)
            lows(ZU + 2, OU)
            norm_low(1)
            lows(ZU + OU + 2, QU + EU * 2)
            for g in range(GROUPS):
                first = FIRST["v", g]
                if g == GROUPS - 2:
                    coef_lows(pool, own, pool.tensor_tensor, g, low)
                elif g < GROUPS - 1:
                    lows(first + 2, EU)
                else:
                    lows(first + 2, EU - 4)
                    low(UNITS - 2, UNITS - 2)
                    low(UNITS - 1, UNITS - 1)
                if g + 2 < GROUPS:
                    lows(FIRST["u", g + 2] + 2, EU)

        @block.scalar
        def _(act):
            own = Steps(act, S("act_own"))
            A = act.activation
            act.dma_start(cols[:, :], cols_in).then_inc(S("cols_in"), 16)
            act.dma_start(x[:, :, :], x_t).then_inc(S("x_in"), 16)
            def ada_load(c):
                act.wait_ge(S("ada_summed"), max(c - 2, ADA_HEAD))
                act.dma_start(ada_w[:, c % 3, :, :], wada_in[c]).then_inc(S(f"ada_in{c % 3}"), 16)
            act.wait_ge(S("cols_in"), 16)
            A(silu_c[:, :], cols[:, C_C:C_C + KB], ACT.Silu).then_inc(S("c_silu"), 1)
            act.wait_ge(S("x_in"), 16)
            for k in range(KB):
                A(sq[:, k, :], x[:, k, :], ACT.Square).then_inc(S("x_sq"), 1)
            act.sem_inc(S("tile_out"), 2)

            def high_at(i, slot, free=True):
                if free:
                    act.wait_ge(S("unit_done"), i * 4 + (slot - 1) if i is not None else slot - 1)
                full = 16 * (slot // RAW_SLOTS + 1)
                act.wait_ge(raw_ready[slot % RAW_SLOTS], i * 16 + full if i is not None else full)
                A(w_hi[:, slot % SPLIT_SLOTS, :], raw[:, slot % RAW_SLOTS, :], ACT.Copy).then_inc(S("w_high"), 1)

            def root(n):
                act.wait_ge(S("mean_ready"), n + 1)
                A(rstd[:, :], rstd[:, :], ACT.Sqrt).then_inc(S("root_ready"), 1)

            def norm_high(n):
                for k in range(KB):
                    act.wait_ge(S("h_ready"), KB * n + k + 1)
                    A(hs_hi[:, k, :], h_tmp[:, k, :], ACT.Copy).then_inc(S("h_high"), 1)

            act.wait_ge(S("c_silu"), 1)
            for c in range(ADA_HEAD):
                act.wait_ge(S(f"ada_head{c}"), 16)
                for k in range(ADA_DVE, KB):
                    ins = A(ada_w0[:, c, k, :], ada_w0[:, c, k, :], ACT.Copy, scale=silu_c[:, k:k + 1])
                ins.then_inc(S("ada_scaled"), 1)
                if c == 2:
                    root(0)
            high_at(None, 0, False)
            high_at(None, 1, False)
            norm_high(0)
            def z_out(t, bankno):
                act.wait_ge(S("unit_done"), t * 2 + 2)
                dst = z[:, t, :] if isinstance(t, int) else z[:, ds(t, 1), :]
                b = cols[:, C_BIN + t:C_BIN + t + 1] if isinstance(t, int) else cols[:, ds(t + C_BIN, 1)]
                A(dst, tile_bank[bankno][:, :], ACT.Identity, bias=b).then_inc(S("tile_out"), 1)

            act.wait_ge(S("h_low"), KB // 2)
            act.wait_ge(S("h_low_late"), KB // 2)
            for c in range(ADA_HEAD, ADA_HEAD + 3):
                ada_load(c)
            idx_tiles = [t for t in range(1, NT) for h in range(IDX_HEADS)]
            for t in range(Z_TILES):
                high_at(None, 2 * t + 2)
                high_at(None, 2 * t + 3)
                z_out(t, t % 2)
                if t == Z_HEAD:
                    act.wait_ge(S("misc_tr"), 1)
                    A(misc_t[:, :, :], bank[3][:, :].rearrange("p (t c) -> p t c", t=NT), ACT.Copy
                      ).then_inc(S("misc_ready"), 1)
                for n in range(4 * (t - Z_HEAD - 1), 4 * (t - Z_HEAD)):
                    if 0 <= n < len(idx_tiles):
                        w = (idx_tiles[n] + 1) * P
                        act.wait_ge(S("idx_dot"), n + 1)
                        if n >= 2:
                            act.wait_ge(S("idx_added"), n - 1)
                        A(relu[:, n % 2, 0:w], bank[4 + n % 4][:, 0:w], ACT.Relu).then_inc(S("idx_relu"), 1)
                if t in ADA_BESIDE[:-3]:
                    ada_load(ADA_HEAD + 3 + ADA_BESIDE.index(t))
                if t in POOL_ADA_TILES:
                    c = ADA_CHUNKS - 3 + POOL_ADA_TILES.index(t)
                    act.wait_ge(S(f"ada_in{c % 3}"), 16 * ada_loads(c))
                    for k in range(KB):
                        ins = A(ada_w[:, c % 3, k, :], ada_w[:, c % 3, k, :], ACT.Copy, scale=silu_c[:, k:k + 1])
                    ins.then_inc(S("ada_scaled"), 1)
                if t == Z_MQ + 7:
                    f_row = z[32:36, Z_MISC, :]
                    own.do(A(rows[32:36, 0, :], f_row, ACT.Abs))
                    own.do(A(rows[32:36, 1, :], rows[32:36, 0, :], ACT.Exp, scale=-1.0))
                    A(rows[32:36, 2, :], rows[32:36, 1, :], ACT.Ln, bias=1.0).then_inc(S("soft_f"), 1)
                h = t - V_TR
                if 0 <= h < M_HEADS:
                    act.wait_ge(S("v_tr"), h + 1)
                    A(v_aug[:, :, h, 0:M_DH], bank[4 + h][:, :].rearrange("p (j d) -> p j d", j=NT),
                      ACT.Copy).then_inc(S("v_ready"), 1)
            act.wait_ge(S("tile_out"), Z_TILES + 2)
            for t in range(2 * M_HEADS):
                act.wait_ge(S("conv"), t + 1)
                A(qk[:, t, :], qk[:, t, :], ACT.Silu).then_inc(S("qk_ready"), 1)
            for h in range(M_HEADS):
                A(z[:, Z_MO + h, :], z[:, Z_MO + h, :], ACT.Sigmoid).then_inc(S("mo_gate"), 1)
            act.wait_ge(S("col_tr"), 1)
            A(wcol[:, :, :], bank[3][:, 0:NT * M_HEADS].rearrange("p (j h) -> p j h", j=NT), ACT.Copy
              ).then_inc(S("wcol_ready"), 1)
            act.wait_ge(S("wcol_ready"), 1)
            A(emm[:, :, :], bank[3][:, 16:16 + NT * M_HEADS].rearrange("p (j h) -> p j h", j=NT), ACT.Exp,
              scale=-1.0).then_inc(S("emm_ready"), 1)
            for h in range(M_HEADS):
                act.wait_ge(S("decay_arg"), h + 1)
                A(decay[h % 3][:, :], decay[h % 3][:, :], ACT.Exp).then_inc(S("decay_exp"), 1)
            heads = NT * A_HEADS

            def att_root(t):
                act.wait_ge(S("att_mean"), t + 1)
                A(o_rs[:, t, :], o_rs[:, t, :], ACT.Sqrt).then_inc(S("att_root"), 1)

            def cat_high(k):
                src = z[:, Z_MO + k, :] if k < 4 else z[:, Z_IQ + k - 4, :]
                A(hs_hi[:, k, :], src, ACT.Copy).then_inc(S("cat_high"), 1)

            for n in range(heads + 1):
                if n < heads:
                    act.wait_ge(S("s_masked"), n + 1)
                    w = (n // A_HEADS + 1) * P
                    A(prob[:, n % 3, 0:w], prob[:, n % 3, 0:w], ACT.Exp, bias=s_neg[:, n % 4:n % 4 + 1],
                      scale=A_DH ** -0.5, accum_out=s_sum[:, n % 4:n % 4 + 1]).then_inc(S("p_ready"), 1)
                m = n - 1
                if m >= 0:
                    tiles_of = m // A_HEADS + 1
                    act.wait_ge(S("p_tr"), m + 1)
                    if m >= 2:
                        act.wait_ge(S("o_dot"), m - 1)
                    A(prob_t[:, m % 2, 0:tiles_of, :], bank[6 + m % 2][:, 0:tiles_of * P].rearrange(
                        "p (s q) -> p s q", q=P), ACT.Copy).then_inc(S("pt_ready"), 1)
                if n == 4:
                    act.wait_ge(S("hm_mean"), 1)
                    A(hrs[:, :, :], hrs[:, :, :], ACT.Sqrt).then_inc(S("hm_root"), 1)
                if n > A_HEADS + 4 and n % A_HEADS == 5:
                    att_root(n // A_HEADS - 1)
                if n == 18:
                    for k in range(4):
                        act.wait_ge(S("cat_m"), k + 1)
                        cat_high(k)
            att_root(NT - 1)
            act.wait_ge(S("cat_a"), NT)
            for k in range(4, KB):
                cat_high(k)
            act.dma_start(keys[:, :, :], keys_in).then_inc(S("keys_in"), 16)

            def highs(first, count):
                with act.Fori(0, count // 4) as i:
                    for u in range(4):
                        high_at(i, first + u)

            highs(ZU + 2, OU)
            for k in range(KB):
                act.wait_ge(S("tile_out"), TILE0["o", 0] + k + 3)
                A(sq[:, k, :], x[:, k, :], ACT.Square).then_inc(S("x_sq"), 1)
            act.dma_start(x2_dram, x[:, :, :]).then_inc(S("x2_saved"), 16)
            root(1)
            norm_high(1)
            def q_tiles():
                with act.Fori(0, KB // 2) as i:
                    for j in range(2):
                        u = ZU + OU + 2 + 2 * j
                        high_at(i, u)
                        high_at(i, u + 1)
                        t = i * 2 + j
                        act.wait_ge(S("unit_done"), t * 2 + (FIRST["q", 0] + 2))
                        A(q_t[:, ds(t, 1), :], tile_bank[(TILE0["q", 0] + j) % 2][:, :], ACT.Copy
                          ).then_inc(S("tile_out"), 1)
            act.wait_ge(S("h_low"), KB)
            act.wait_ge(S("h_low_late"), KB)
            q_tiles()
            for k in range(NT * P_HEADS // 2):
                act.wait_ge(S("keys_dot"), k + 1)
                t, h = k // 4, 2 * (k % 4)
                A(s12[:, t * P_HEADS + h:t * P_HEADS + h + 2, :, :], bank[4 + k % 2][:, :].rearrange(
                    "p (h a e) -> p h a e", h=2, a=2), ACT.Copy).then_inc(S("s_ready"), 1)

            def u_tiles(g, base=0, count=GI // 2):
                with act.Fori(0, count) as i:
                    for j in range(2):
                        u = FIRST["u", g] + 2 + 2 * j
                        high_at(i, u)
                        high_at(i, u + 1)
                        act.wait_ge(S("unit_done"), i * 4 + (u + 0))
                        A(coef[:, ds(i * 2 + ((g % 2) * GI + j), 1), :], tile_bank[(TILE0["u", g] + j) % 2][:, :],
                          ACT.Gelu).then_inc(S("tile_out"), 1)

            def soft_gates():
                for t in range(NT):
                    act.wait_ge(S("top_shift"), t + 1)
                    A(top[:, t * 8:(t + 1) * 8, :], top[:, t * 8:(t + 1) * 8, :], ACT.Exp).then_inc(S("top_exp"), 1)
                for k in range(3):
                    act.wait_ge(S("slot_tr"), k + 1)
                    dst = (slot_i1, slot_i2, slot_gf)[k]
                    A(dst[:, :], bank[4 + k][:, :], ACT.Copy).then_inc(S("slot_out"), 1)

            def v_units(g):
                first, buf = FIRST["v", g], (g % 2) * GI
                act.wait_ge(S("gated"), (g + 1) * T // GT + 2)
                def chigh(slot, i1):
                    src = coef[:, i1, :] if isinstance(i1, int) else coef[:, ds(i1, 1), :]
                    A(c_hi[:, slot % SPLIT_SLOTS, :], src, ACT.Copy).then_inc(S(f"c_high{g}"), 1)
                chigh(first, buf)
                chigh(first + 1, buf + 1)
                for half in range(2):
                    f = first + half * GI
                    with act.Fori(0, GI // 4 - 1) as i:
                        for u in range(4):
                            high_at(i, f + u + 2)
                            chigh(f + u + 2, i * 4 + (buf + u + 2))
                    for u in range(4):
                        k = GI - 4 + u + 2
                        if f + k < UNITS:
                            high_at(None, f + k)
                        if k < GI or half == 0:
                            if f + k >= UNITS:
                                act.wait_ge(S("unit_done"), f + k - 1)
                            chigh(f + k, buf + k % GI)

            act.wait_ge(S("x2_saved"), 16)
            u_tiles(0)
            soft_gates()
            act.wait_ge(S("gate_split"), 1)
            u_tiles(1)
            for g in range(GROUPS):
                v_units(g)
                if g + 2 < GROUPS:
                    act.wait_ge(S(f"c_split{g}"), EU)
                    u_tiles(g + 2)
            for k in range(KB):
                act.wait_ge(S("earlier_added"), min(k + 2, KB))
                act.wait_ge(S("sums_added"), k + 1)
                A(sq_end[:, k, :], part[:, 3, k, :], ACT.Square).then_inc(S("x_sq"), 1)
            act.wait_ge(S("mean_ready"), 3)
            A(rstd_end[:, :], rstd_end[:, :], ACT.Sqrt).then_inc(S("root_ready"), 1)
            for k in range(KB):
                act.wait_ge(S("out_ready"), k + 1)
                act.dma_start(out[:, k, :], part[:, 2, k, :]).then_inc(S("out_saved"), 16)
            act.wait_ge(S("out_saved"), 16 * KB)

        @block.vector
        def _(dve):
            own = Steps(dve, S("dve_own"))
            rnd = Rounds(dve, S("dve_round"))
            V = nc.vector

            dve.sem_inc(S("gated"), 2)

            def mean(n, src_bank, rstd=rstd):
                dve.wait_ge(S("sq_sum"), n + 1)
                V.tensor_scalar(rstd[:, :], src_bank[:, :], 1.0 / D, EPS, ALU.mult, ALU.add
                                ).then_inc(S("mean_ready"), 1)
                dve.wait_ge(S("root_ready"), n + 1)
                own.do(V.reciprocal(rstd[:, :], rstd[:, :]))

            def normed(amp, shift):
                for k in range(KB):
                    V.tensor_scalar(h_tmp[:, k, :], h_tmp[:, k, :], amp[:, k:k + 1], ada[:, shift + k:shift + k + 1],
                                    ALU.mult, ALU.add).then_inc(S("h_ready"), 1)

            def ada_sums(c):
                if c < ADA_HEAD:
                    dve.wait_ge(S(f"ada_head{c}"), 16)
                    w, acc, blocks = ada_w0[:, c, :, :], ada_acc0[:, c, :], ADA_DVE
                else:
                    dve.wait_ge(S(f"ada_in{c % 3}"), 16 * ada_loads(c))
                    if c >= ADA_HEAD + 2:
                        dve.wait_ge(S("ada_used"), c - 1)
                    w, acc, blocks = ada_w[:, c % 3, :, :], ada_acc[:, c % 2, :], KB
                for k in range(blocks):
                    if k == 0:
                        ins = V.tensor_scalar(acc, w[:, k, :], silu_c[:, k:k + 1], None, ALU.mult)
                    else:
                        ins = V.scalar_tensor_tensor(out=acc, in0=w[:, k, :], scalar=silu_c[:, k:k + 1], in1=acc,
                                                     op0=ALU.mult, op1=ALU.add)
                    if k < blocks - 1:
                        own.do(ins)
                ins.then_inc(S("ada_summed"), 1)

            dve.wait_ge(S("c_silu"), 1)
            dve.wait_ge(S("cols_in"), 16)
            for c in range(ADA_HEAD):
                ada_sums(c)
                if c == 2:
                    mean(0, bank[3])
                    dve.sem_inc(S("rstd0"), 1)
            def late_lows(n):
                for k in range(KB // 2, KB):
                    dve.wait_ge(S("h_high"), KB * n + k + 1)
                    V.tensor_tensor(hs_lo[:, k, :], h_tmp[:, k, :], hs_hi[:, k, :].bitcast(fp32), ALU.subtract
                                    ).then_inc(S("h_low_late"), 1)

            dve.wait_ge(S("cols_in"), 16)
            dve.wait_ge(S("ada_used"), ADA_HEAD)
            own.do(V.tensor_tensor(ada[:, 0:16], bank[2][:, 0:16], cols[:, C_BADA:C_BADA + 16], ALU.add))
            own.do(V.scalar_tensor_tensor(out=amp1[:, :], in0=ada[:, 8:16], scalar=1.0, in1=cols[:, C_N1:C_N1 + 8],
                                          op0=ALU.add, op1=ALU.mult))
            dve.wait_ge(S("x_scaled"), 1)
            normed(amp1, 0)
            late_lows(0)
            dve.wait_ge(S("consts"), 1)
            dve.wait_ge(S("mask0"), 1)
            for c in range(ADA_HEAD, ADA_HEAD + 7):
                ada_sums(c)

            def conv_tile(c):
                dve.wait_ge(S("tile_out"), Z_MQ + c + 3)
                src, dst = z[:, Z_MQ + c, :], qk[:, c, :]
                tap = lambda j: cols[:, C_CONV + 4 * c + j:C_CONV + 4 * c + j + 1]
                own.do(V.tensor_scalar(dst, src, tap(CONV_W - 1), None, ALU.mult))
                for back in range(1, CONV_W):
                    ins = V.scalar_tensor_tensor(out=dst[:, back:T], in0=src[:, 0:T - back],
                                                 scalar=tap(CONV_W - 1 - back), in1=dst[:, back:T],
                                                 op0=ALU.mult, op1=ALU.add)
                    if back < CONV_W - 1:
                        own.do(ins)
                ins.then_inc(S("conv"), 1)

            def weights(t, h):
                return misc_t[:, t, MISC_IW + h:MISC_IW + h + 1]
            n, at_score = 0, 0
            for t in range(1, NT):
                w = (t + 1) * P
                dst = score[:, at_score:at_score + w]
                for h in range(IDX_HEADS):
                    dve.wait_ge(S("idx_relu"), n + 1)
                    if h == 0:
                        dve.wait_ge(S("misc_ready"), 1)
                        ins = V.tensor_scalar(dst, relu[:, n % 2, 0:w], weights(t, h), None, ALU.mult)
                    else:
                        dve.wait_ge(S("idx_added"), n)
                        ins = V.scalar_tensor_tensor(out=dst, in0=relu[:, n % 2, 0:w], scalar=weights(t, h), in1=dst,
                                                     op0=ALU.mult, op1=ALU.add)
                    ins.then_inc(S("idx_added"), 1)
                    n += 1
                    if n % 4 == 0:
                        conv_tile(n // 4 - 1)
                        ada_sums(ADA_HEAD + 6 + n // 4)
                dve.wait_ge(S("idx_added"), n)
                own.do(V.tensor_scalar(dst, dst, 64.0 ** -0.5 * IDX_HEADS ** -0.5, None, ALU.mult))
                own.did(V.tensor_tensor(dst[:, t * P:w], dst[:, t * P:w], mask[:, 0:P], ALU.add))
                at_score += w

            own.settle()
            spans, at_score = [], 0
            for t in range(1, NT):
                spans.append(slice(at_score, at_score + (t + 1) * P))
                at_score += (t + 1) * P
            with dve.Fori(0, N_SEL // 8):
                for k, span in enumerate(spans):
                    rnd.did(V.max(best8[:, 8 * k:8 * k + 8], score[:, span]))
                for k, span in enumerate(spans):
                    rnd.settle(len(spans) - 1)
                    rnd.did(V.match_replace(score[:, span], best8[:, 8 * k:8 * k + 8], score[:, span], TAKEN))
                rnd.turn_over()
            V.tensor_scalar(mask[:, P:P + at_score], score[:, 0:at_score], (NEG + TAKEN) / 2, NEG, ALU.is_gt, ALU.mult
                            ).then_inc(S("mask_ready"), 1)
            for c in range(len(spans) * IDX_HEADS // 4, 2 * M_HEADS):
                conv_tile(c)

            dve.wait_ge(S("soft_f"), 1)
            R = lambda k: rows[0:4, k, :]
            own.do(V.scalar_tensor_tensor(out=R(R_LF), in0=z[32:36, Z_MISC, :], scalar=0.0, in1=rows[32:36, 2, :],
                                          op0=ALU.min, op1=ALU.subtract))
            own.do(V.memset(R(R_W), 1.0))
            own.do(V.tensor_tensor_scan(out=R(R_B), data0=R(R_W), data1=R(R_LF), initial=0.0, op0=ALU.mult, op1=ALU.add))
            own.do(V.tensor_tensor(R(R_W), z[0:4, Z_MISC, :], R(R_B), ALU.subtract))
            own.do(V.tensor_tensor_scan(out=R(R_MX), data0=R(R_W), data1=R(R_W), initial=0.0, op0=ALU.max, op1=ALU.max))
            V.tensor_tensor(R(R_M), R(R_B), R(R_MX), ALU.add).then_inc(S("rows_ready"), 1)
            dve.wait_ge(S("ada_used"), ADA_CHUNKS)
            V.tensor_tensor(ada[:, 16:48], bank[2][:, 16:48], cols[:, C_BADA + 16:C_BADA + 48], ALU.add
                            ).then_inc(S("ada_ready"), 1)
            dve.wait_ge(S("ada_ready"), 1)
            own.do(V.scalar_tensor_tensor(out=amp2[:, :], in0=ada[:, 32:40], scalar=1.0, in1=cols[:, C_N2:C_N2 + 8],
                                          op0=ALU.add, op1=ALU.mult))
            dve.wait_ge(S("idx_dot"), len(spans) * IDX_HEADS)
            V.memset(v_aug[:, :, :, M_DH:M_DH + 1], 1.0).then_inc(S("v_ones"), 1)
            def decay_arg(h):
                dve.wait_ge(S("neg_m"), h + 1)
                if h == 0:
                    dve.wait_ge(S("wcol_ready"), 1)
                if h >= 3:
                    dve.wait_ge(S("num_half"), 2 * (h - 2))
                off = 0
                for j in range(NT):
                    w = (NT - j) * P
                    ins = V.tensor_scalar(decay[h % 3][:, off:off + w], bank[2 + h % 2][:, j * P:T],
                                          wcol[:, j, h:h + 1], 0.0, ALU.add, ALU.min)
                    off += w
                ins.then_inc(S("decay_arg"), 1)

            def num_out(h):
                for half in range(2):
                    dve.wait_ge(S("num_half"), 2 * h + half + 1)
                    V.tensor_copy(num[:, 2 * half:2 * half + 2, h, :],
                                  bank[6 + half][:, 0:2 * (M_DH + 1)].rearrange("p (i e) -> p i e", i=2)
                                  ).then_inc(S("num_out"), 1)

            decay_arg(0)
            decay_arg(1)
            for h in range(M_HEADS):
                dve.wait_ge(S("decay_cut"), h + 1)
                off = 0
                for j in range(NT):
                    w, n = (NT - j) * P, h * NT + j
                    dve.wait_ge(S("qk_dot"), n + 1)
                    V.scalar_tensor_tensor(out=decay[h % 3][:, off:off + w], in0=bank[4 + n % 2][:, 0:w],
                                           scalar=float(M_DH) ** -0.5, in1=decay[h % 3][:, off:off + w],
                                           op0=ALU.mult, op1=ALU.mult).then_inc(S("decayed"), 1)
                    off += w
                if h:
                    num_out(h - 1)
                if h + 2 < M_HEADS:
                    decay_arg(h + 2)
            num_out(M_HEADS - 1)
            dve.wait_ge(S("num_out"), 2 * M_HEADS)
            dve.wait_ge(S("emm_ready"), 1)

            bc = lambda a, n: a.unsqueeze(3).broadcast_to([P, NT, M_HEADS, n])

            def hm_step(n):
                own.settle()
                if n == 0:
                    own.do(V.scalar_tensor_tensor(out=den[:, :, :], in0=num[:, :, :, M_DH], scalar=-1.0,
                                                  in1=num[:, :, :, M_DH], op0=ALU.mult, op1=ALU.max))
                    own.do(V.tensor_tensor(den[:, :, :], den[:, :, :], emm[:, :, :], ALU.max))
                    own.did(V.reciprocal(den[:, :, :], den[:, :, :]))
                elif n == 1:
                    own.did(V.tensor_tensor(hm[:, :, :, :], num[:, :, :, 0:M_DH], bc(den[:, :, :], M_DH), ALU.mult))
                elif n == 2:
                    own.did(V.tensor_tensor(hm2[:, :, :, :], hm[:, :, :, :], hm[:, :, :, :], ALU.mult))
                elif n == 3:
                    own.do(V.reduce_sum(hrs[:, :, :], hm2[:, :, :, :], AX.X))
                    V.tensor_scalar(hrs[:, :, :], hrs[:, :, :], 1.0 / M_DH, EPS, ALU.mult, ALU.add
                                    ).then_inc(S("hm_mean"), 1)
                elif n == 5:
                    dve.wait_ge(S("hm_root"), 1)
                    own.do(V.reciprocal(hrs[:, :, :], hrs[:, :, :]))
                    V.tensor_tensor(hm[:, :, :, :], hm[:, :, :, :], bc(hrs[:, :, :], M_DH), ALU.mult
                                    ).then_inc(S("hm_ready"), 1)

            def cat_m(h):
                dve.wait_ge(S("mo_gate"), h + 1)
                dve.wait_ge(S("hm_tr"), h + 1)
                V.scalar_tensor_tensor(out=z[:, Z_MO + h, :], in0=bank[h % 2][:, :],
                                       scalar=cols[:, C_OUTN + h:C_OUTN + h + 1], in1=z[:, Z_MO + h, :],
                                       op0=ALU.mult, op1=ALU.mult).then_inc(S("cat_m"), 1)

            def att_step(t, n):
                o = att[:, t, :, :]
                if n == 0:
                    dve.wait_ge(S("o_out"), (t + 1) * A_HEADS)
                    own.did(V.tensor_tensor(att2[:, :, :], o, o, ALU.mult))
                elif n == 1:
                    own.settle()
                    own.do(V.reduce_sum(o_rs[:, t, :], att2[:, :, :], AX.X))
                    V.tensor_scalar(o_rs[:, t, :], o_rs[:, t, :], 1.0 / A_DH, EPS, ALU.mult, ALU.add
                                    ).then_inc(S("att_mean"), 1)
                elif n == 2:
                    dve.wait_ge(S("att_root"), t + 1)
                    own.do(V.reciprocal(o_rs[:, t, :], o_rs[:, t, :]))
                    V.tensor_tensor(o, o, o_rs[:, t, :].unsqueeze(2).broadcast_to([P, A_HEADS, A_DH]), ALU.mult
                                    ).then_inc(S("att_ready"), 1)
                else:
                    dve.wait_ge(S("att_tr"), t + 1)
                    V.tensor_tensor(z[:, Z_IQ:Z_IQ + 4, t * P:(t + 1) * P],
                                    att_bank(t)[:, :].rearrange("p (f q) -> p f q", f=4),
                                    cols[:, C_OUTN + 4:C_OUTN + 8].unsqueeze(2).broadcast_to([P, 4, P]), ALU.mult
                                    ).then_inc(S("cat_a"), 1)

            dve.wait_ge(S("mask_ready"), 1)
            heads = NT * A_HEADS
            for n in range(heads + 3):
                if n < heads:
                    t = n // A_HEADS
                    w, at_mask = (t + 1) * P, t * (t + 1) // 2 * P
                    dve.wait_ge(S("s_dot"), n + 1)
                    if n >= 3:
                        dve.wait_ge(S("p_tr"), n - 2)
                    own.did(V.tensor_tensor_reduce(out=prob[:, n % 3, 0:w], in0=bank[4 + n % 2][:, 0:w],
                                                   in1=mask[:, at_mask:at_mask + w], scale=1.0, scalar=-3.0e38,
                                                   op0=ALU.add, op1=ALU.max, accum_out=s_max[:, n % 4:n % 4 + 1]))
                m = n - 3
                if m >= 0:
                    dve.wait_ge(S("o_dot"), m + 1)
                    own.did(V.reciprocal(s_sum[:, m % 4:m % 4 + 1], s_sum[:, m % 4:m % 4 + 1]))
                if n < heads:
                    own.settle(1 if m >= 0 else 0)
                    V.tensor_scalar(s_neg[:, n % 4:n % 4 + 1], s_max[:, n % 4:n % 4 + 1], -A_DH ** -0.5, None, ALU.mult
                                    ).then_inc(S("s_masked"), 1)
                if m >= 0:
                    own.settle()
                    V.tensor_scalar(att[:, m // A_HEADS, m % A_HEADS, :], bank[2 + m % 2][:, 0:A_DH],
                                    s_sum[:, m % 4:m % 4 + 1], None, ALU.mult).then_inc(S("o_out"), 1)
                if n <= 5:
                    hm_step(n)
                if n - 1 in HM_TR:
                    cat_m(HM_TR.index(n - 1))
                if n >= A_HEADS + 3:
                    t, k = n // A_HEADS - 1, n % A_HEADS
                    if t < NT - 1 and k in (3, 4, 6):
                        att_step(t, (3, 4, 6).index(k))
                if n >= 2 * A_HEADS + 2 and n % A_HEADS == 2:
                    att_step(n // A_HEADS - 2, 3)
            for k in range(4):
                att_step(NT - 1, k)

            for k in range(KB):
                dve.wait_ge(S("unit_done"), FIRST["o", 0] + 2 * k + 2)
                V.scalar_tensor_tensor(out=x[:, k, :], in0=tile_bank[(TILE0["o", 0] + k) % 2][:, :],
                                       scalar=ada[:, 16 + k:17 + k], in1=x[:, k, :], op0=ALU.mult, op1=ALU.add
                                       ).then_inc(S("tile_out"), 1)
            dve.wait_ge(S("tile_out"), TILE0["o", 0] + KB + 2)
            mean(1, bank[3])
            for k in range(KB):
                own.did(V.tensor_tensor(h_tmp[:, k, :], x[:, k, :], rstd[:, :], ALU.mult))
            own.settle()
            normed(amp2, 24)
            late_lows(1)

            dve.wait_ge(S("s_ready"), NT * P_HEADS // 2)
            H = P_HEADS
            for t in range(NT):
                sl = slice(t * H, (t + 1) * H)
                for h in range(H):
                    b = lambda a, k: best[:, t * H + h, a, 8 * k:8 * k + 8]
                    bi = lambda a, k: best_iu[:, t * H + h, a, 8 * k:8 * k + 8]
                    for k in range(2):
                        for a in range(2):
                            own.did(V.max(b(a, k), s12[:, t * H + h, a, :]))
                        for a in range(2):
                            own.settle(1)
                            own.did(V.max_index(bi(a, k), b(a, k), s12[:, t * H + h, a, :]))
                        if k == 0:
                            for a in range(2):
                                own.settle(1)
                                own.did(V.match_replace(s12[:, t * H + h, a, :], b(a, 0), s12[:, t * H + h, a, :], TAKEN))
                            own.settle()
                    own.settle()
                    c0, c1 = cand[:, 0, :], cand[:, 1, :]
                    own.do(V.tensor_tensor(c0.rearrange("p (a b) -> p a b", a=16),
                                           best[:, t * H + h, 0, :].unsqueeze(2).broadcast_to([P, 16, 16]),
                                           best[:, t * H + h, 1, :].unsqueeze(1).broadcast_to([P, 16, 16]), ALU.add))
                    own.do(V.max(top[:, t * H + h, 0:8], c0))
                    own.did(V.max_index(pos_u[:, t * H + h, 0:8], top[:, t * H + h, 0:8], c0))
                    own.do(V.match_replace(c1, top[:, t * H + h, 0:8], c0, TAKEN))
                    own.do(V.max(top[:, t * H + h, 8:16], c1))
                    own.did(V.max_index(pos_u[:, t * H + h, 8:16], top[:, t * H + h, 8:16], c1))
                own.settle()
                own.did(V.tensor_copy(best_if[:, sl, :, :], best_iu[:, sl, :, :]))
                own.did(V.tensor_copy(gsum[:, sl], top[:, sl, 0]))
                own.settle()
            own.do(V.tensor_scalar(pos_f[:, 1, :, :].bitcast(u32), pos_u[:, :, :], 15, None, ALU.bitwise_and))
            own.do(V.tensor_scalar(pos_u[:, :, :], pos_u[:, :, :], 4, None, ALU.logical_shift_right))
            own.do(V.tensor_copy(pos_f[:, 1, :, :], pos_f[:, 1, :, :].bitcast(u32)))
            own.do(V.tensor_copy(pos_f[:, 0, :, :], pos_u[:, :, :]))
            for t in range(NT):
                sl = slice(t * P_HEADS, (t + 1) * P_HEADS)
                V.tensor_tensor(top[:, sl, :], top[:, sl, :], gsum[:, sl].unsqueeze(2).broadcast_to([P, P_HEADS, 16]),
                                ALU.subtract).then_inc(S("top_shift"), 1)
                for a in range(2):
                    ranks = iota[:, 0:16].unsqueeze(1).unsqueeze(1).broadcast_to([P, P_HEADS, 16, 16])
                    pf = pos_f[:, a, sl, :].unsqueeze(3).broadcast_to([P, P_HEADS, 16, 16])
                    idx = best_if[:, sl, a, :].unsqueeze(2).broadcast_to([P, P_HEADS, 16, 16])
                    own.do(V.tensor_tensor(pick[:, :, :, :], pf, ranks, ALU.is_equal))
                    own.do(V.tensor_tensor(pick[:, :, :, :], pick[:, :, :, :], idx, ALU.mult))
                    own.do(V.reduce_sum(slot_t[:, a, t * P:(t + 1) * P].rearrange("p (h k) -> p h k", h=P_HEADS),
                                        pick[:, :, :, :], AX.X))
            for t in range(NT):
                sl = slice(t * P_HEADS, (t + 1) * P_HEADS)
                dve.wait_ge(S("top_exp"), t + 1)
                own.do(V.reduce_sum(gsum[:, sl], top[:, sl, :], AX.X))
                own.do(V.reciprocal(gsum[:, sl], gsum[:, sl]))
                V.tensor_tensor(slot_t[:, 2, t * P:(t + 1) * P].rearrange("p (h k) -> p h k", h=P_HEADS), top[:, sl, :],
                                gsum[:, sl].unsqueeze(2).broadcast_to([P, P_HEADS, 16]), ALU.mult
                                ).then_inc(S("slots_ready"), 1)
            dve.wait_ge(S("slot_out"), 3)
            for k in range(3):
                ins = V.tensor_copy(slot_g[:, k, :], slot_gf[:, :])
                if k < 2:
                    own.do(ins)
                    own.do(V.tensor_tensor(slot_gf[:, :], slot_gf[:, :], slot_g[:, k, :], ALU.subtract))
            ins.then_inc(S("gate_split"), 1)
            dve.wait_ge(S("gate_split"), 1)

            def one_hots(g, i, par):
                if g or not isinstance(i, int):
                    dve.wait_ge(S("rows_used"), i + (g * (T // GT) - 1))
                keys_of = lambda table, n: table[:, ds(i * GT, GT)].unsqueeze(1).broadcast_to([P, n, GT])
                own.did(V.tensor_tensor(eq1[:, par, :, :], key_rep[:, g * GI:(g + 1) * GI, :], keys_of(slot_i1, GI),
                                        ALU.is_equal))
                V.tensor_tensor(rows2[:, par, :, :], key_rep[:, :, :], keys_of(slot_i2, N_KEYS), ALU.is_equal
                                ).then_inc(S("rows2_ready"), 1)
                own.settle()
                V.tensor_tensor(rows1[:, par, :, :, :], eq1[:, par, :, :].unsqueeze(1).broadcast_to([P, 3, GI, GT]),
                                slot_g[:, :, ds(i * GT, GT)].unsqueeze(2).broadcast_to([P, 3, GI, GT]), ALU.mult
                                ).then_inc(S("rows1_ready"), 1)

            def apply_gates(g, i, par):
                buf = (g % 2) * GI
                dve.wait_ge(S("rows_used"), i + (g * (T // GT) + 1))
                c = coef[:, buf:buf + GI, ds(i * GT, GT)]
                V.tensor_tensor(c, c, gate_bank[par][:, 0:GT * GI].rearrange("p (n e) -> p e n", n=GT), ALU.mult
                                ).then_inc(S("gated"), 1)

            def gate_group(g, between=None):
                dve.wait_ge(S("tile_out"), TILE0["u", g] + GI + 2)
                if g:
                    for d in range(4):
                        if g < GROUPS - 1:
                            dve.wait_ge(S(f"part_saved{d}"), 16 * 2 * g)
                for q in range(2):
                    one_hots(g, q, q)
                pairs = T // GT // 2
                for start, end in ((1, pairs // 2), (pairs // 2, pairs)):
                    with own.loop(start, end, 2) as i:
                        for par in range(2):
                            one_hots(g, i * 2 + par, par)
                            apply_gates(g, i * 2 + (par - 2), par)
                    if between and end < pairs:
                        between()
                for q in range(T // GT - 2, T // GT):
                    apply_gates(g, q, q % 2)

            def sums_out(g, half, ds_=range(4)):
                dve.wait_ge(S("unit_done"), FIRST["v", g] + (half + 1) * GI)
                for d in ds_:
                    k = half * 4 + d
                    if g < GROUPS - 1:
                        if half:
                            dve.wait_ge(S(f"part_saved{d}"), 16 * (2 * g + 1))
                        V.tensor_copy(y_stage[g][:, d, :], sum_bank[d][:, :]).then_inc(S("y_out"), 1)
                    else:
                        V.scalar_tensor_tensor(out=part[:, 3, k, :], in0=sum_bank[d][:, :],
                                               scalar=ada[:, 40 + k:41 + k], in1=part[:, 3, k, :],
                                               op0=ALU.mult, op1=ALU.add).then_inc(S("sums_added"), 1)

            def v_phase(g):
                coef_lows(dve, own, V.tensor_tensor, g, None, (lambda: sums_out(g, 0, range(1)),
                                                          lambda: sums_out(g, 0, range(1, 4))))
                sums_out(g, 1)

            for g in range(GROUPS - 2):
                gate_group(g)
                v_phase(g)
            gate_group(GROUPS - 2)
            gate_group(GROUPS - 1, lambda: sums_out(GROUPS - 2, 0))
            sums_out(GROUPS - 2, 1)
            def add_earlier(k, step):
                blk = lambda n: part[:, n, k, :] if isinstance(k, int) else part[:, n, ds(k, 1), :]
                if step == 0:
                    own.did(V.tensor_tensor(blk(0), blk(0), blk(1), ALU.add))
                    return
                own.settle()
                if step == 1:
                    own.did(V.tensor_tensor(blk(2), blk(2), blk(0), ALU.add))
                    return
                ins = V.scalar_tensor_tensor(out=blk(3), in0=blk(2), scalar=ada[:, 40 + k:41 + k] if isinstance(
                    k, int) else ada[:, ds(k + 40, 1)], in1=blk(3), op0=ALU.mult, op1=ALU.add)
                own.did(ins)
                dve.sem_inc(S("earlier_added"), 1)
            def first_half_out():
                dve.wait_ge(S("x2_back"), 16 * KB)
                sums_out(GROUPS - 1, 0, range(1))
            def rest_out():
                sums_out(GROUPS - 1, 0, range(1, 4))
                dve.wait_ge(S("part_back"), 16 * KB * (GROUPS - 1))
                dve.wait_ge(S("sums_added"), 4)
            coef_lows(dve, own, V.tensor_tensor, GROUPS - 1, None, (first_half_out, rest_out), add_earlier)
            own.settle()
            sums_out(GROUPS - 1, 1)
            dve.wait_ge(S("sums_added"), KB)
            mean(2, bank[3], rstd_end)
            for k in range(KB):
                V.scalar_tensor_tensor(out=part[:, 2, k, :], in0=part[:, 3, k, :], scalar=cols[:, C_FG + k:C_FG + k + 1],
                                       in1=rstd_end[:, :], op0=ALU.mult, op1=ALU.mult).then_inc(S("out_ready"), 1)

        @block.tensor
        def _(pe):
            mm = nc.tensor.matmul

            def square_sums(n, sq=sq):
                for k in range(KB):
                    pe.wait_ge(S("x_sq"), KB * n + k + 1)
                    ins = mm(bank[3][:, :], ones[:, :], sq[:, k, :], start=(k == 0), stop=(k == KB - 1))
                ins.then_inc(S("sq_sum"), 1)

            def ada_chunk(c):
                if c < ADA_CHUNKS - 3:
                    pe.wait_ge(S("ada_summed"), c + 1)
                else:
                    pe.wait_ge(S("ada_summed_pool"), c - (ADA_CHUNKS - 3) + 1)
                parts = [ada_acc[:, c % 2, :]]
                if c < ADA_HEAD:
                    pe.wait_ge(S("ada_scaled"), c + 1)
                    parts = [ada_acc0[:, c, :]] + [ada_w0[:, c, k, :] for k in range(ADA_DVE, KB)]
                for j in range(2):
                    for n, part_sum in enumerate(parts):
                        ins = mm(bank[2][:, 2 * c + j:2 * c + j + 1], part_sum[:, j * P:(j + 1) * P], ones[:, 0:1],
                                 start=(n == 0), stop=(n == len(parts) - 1))
                ins.then_inc(S("ada_used"), 1)

            def split_unit(u, out_of, start, stop, inputs=None):
                s = u % SPLIT_SLOTS
                half = 4 * (not start)
                for k in range(4):
                    if inputs:
                        inputs(half + k)
                    wh = w_hi[:, s, k * P:(k + 1) * P]
                    mm(out_of, wh, hs_hi[:, half + k, :], start=(start and k == 0), stop=False)
                    mm(out_of, wh, hs_lo[:, half + k, :], start=False, stop=False)
                    ins = mm(out_of, w_lo[:, s, k * P:(k + 1) * P], hs_hi[:, half + k, :], start=False,
                             stop=(stop and k == 3))
                return ins

            def tile(phase, i, j, extra=None, inputs=None):
                u0, t0 = FIRST[phase] + 2 * j, TILE0[phase] + j
                dst = tile_bank[t0 % 2][:, :]
                pe.wait_ge(S("tile_out"), i * 2 + (t0 + 1))
                for h in range(2):
                    pe.wait_ge(S("w_split"), i * 4 + (u0 + h + 1))
                    split_unit(u0 + h, dst, h == 0, h == 1, inputs).then_inc(S("unit_done"), 1)
                    if extra:
                        extra(i, 2 * j + h)

            def tiles(phase, count, extra=None, inputs=None):
                if inputs:
                    for j in range(2):
                        tile(phase, 0, j, extra, inputs if j == 0 else None)
                with pe.Fori(1 if inputs else 0, count // 2) as i:
                    for j in range(2):
                        tile(phase, i, j, extra)

            def normed_input(n):
                half = KB // 2
                return lambda k: pe.wait_ge(S("h_low" if k < half else "h_low_late"), n * half + k % half + 1)

            def transposes(dst, sources):
                for n, src in enumerate(sources):
                    w = src.shape[0]
                    ins = nc.tensor.transpose(dst[:, n * w:(n + 1) * w], src, ident[0:w, 0:w])
                return ins

            pe.wait_ge(S("consts"), 1)
            square_sums(0)
            for c in range(ADA_HEAD):
                ada_chunk(c)

            idx = [(t, h) for t in range(1, NT) for h in range(IDX_HEADS)]

            def index_product(n):
                t, h = idx[n]
                if n >= 4:
                    pe.wait_ge(S("idx_relu"), n - 3)
                r = slice(64 * (h % 2), 64 * (h % 2) + 64)
                mm(bank[4 + n % 4][:, 0:(t + 1) * P], z[r, Z_IQ + h // 2, t * P:(t + 1) * P],
                   z[r, Z_IK, 0:(t + 1) * P], start=True, stop=True).then_inc(S("idx_dot"), 1)

            def beside(i, unit):
                u = unit - 2 * Z_HEAD
                if u == 1:
                    pe.wait_ge(S("tile_out"), Z_HEAD + 2)
                    transposes(bank[3], [z[:, Z_MISC, t * P:(t + 1) * P] for t in range(NT)]).then_inc(S("misc_tr"), 1)
                for n in (2 * u - 4, 2 * u - 3):
                    if 0 <= n < len(idx):
                        index_product(n)
                if unit % 2 and unit // 2 in ADA_BESIDE:
                    ada_chunk(ADA_HEAD + ADA_BESIDE.index(unit // 2))
                h = unit // 2 - V_TR
                if unit % 2 and 0 <= h < M_HEADS:
                    pe.wait_ge(S("idx_relu"), len(idx))
                    pe.wait_ge(S("tile_out"), Z_MV + h + 3)
                    transposes(bank[4 + h], [z[:, Z_MV + h, t * P:(t + 1) * P] for t in range(NT)]
                               ).then_inc(S("v_tr"), 1)

            for t in range(Z_TILES):
                tile(("z", 0), 0, t, beside, normed_input(0) if t == 0 else None)
            pe.wait_ge(S("v_ready"), M_HEADS)
            pe.wait_ge(S("rows_ready"), 1)
            pe.wait_ge(S("misc_ready"), 1)
            for k, row in enumerate((R_W, R_M)):
                for j in range(NT):
                    c = 16 * k + 4 * j
                    ins = nc.tensor.transpose(bank[3][:, c:c + 4], rows[0:4, row, j * P:(j + 1) * P], ident[0:4, 0:4])
            ins.then_inc(S("col_tr"), 1)
            pe.wait_ge(S("qk_ready"), 2 * M_HEADS)
            pe.wait_ge(S("v_ready"), M_HEADS)
            pe.wait_ge(S("v_ones"), 1)
            pe.wait_ge(S("ada_ready"), 1)
            pe.wait_ge(S("emm_ready"), 1)

            def neg_m(h):
                if h >= 2:
                    pe.wait_ge(S("decay_arg"), h - 1)
                mm(bank[2 + h % 2][:, :], sel[0:4, h, :], rows[0:4, R_MX, :], start=True, stop=True
                   ).then_inc(S("neg_m"), 1)

            def key_products(h):
                for j in range(NT):
                    n = h * NT + j
                    if n >= 2:
                        pe.wait_ge(S("decayed"), n - 1)
                    mm(bank[4 + n % 2][:, 0:(NT - j) * P], qk[:, M_HEADS + h, j * P:(j + 1) * P], qk[:, h, j * P:T],
                       start=True, stop=True).then_inc(S("qk_dot"), 1)

            def value_products(h):
                pe.wait_ge(S("decayed"), (h + 1) * NT)
                for i in range(NT):
                    if h and i % 2 == 0:
                        pe.wait_ge(S("num_out"), 2 * (h - 1) + i // 2 + 1)
                    c = (i % 2) * (M_DH + 1)
                    off = 0
                    for j in range(i + 1):
                        a = off + (i - j) * P
                        ins = mm(bank[6 + i // 2][:, c:c + M_DH + 1], decay[h % 3][:, a:a + P], v_aug[:, j, h, :],
                                 start=(j == 0), stop=(j == i))
                        off += (NT - j) * P
                    if i % 2:
                        ins.then_inc(S("num_half"), 1)

            def att_transposes(t):
                pe.wait_ge(S("cat_m"), M_HEADS)
                pe.wait_ge(S("att_ready"), t + 1)
                if t >= 2:
                    pe.wait_ge(S("cat_a"), t if t == NT - 1 else t - 1)
                transposes(att_bank(t), [att[:, t, 2 * f:2 * f + 2, :].rearrange("p h d -> p (h d)") for f in range(4)]
                           ).then_inc(S("att_tr"), 1)

            neg_m(0)
            for h in range(M_HEADS):
                if h + 1 < M_HEADS:
                    neg_m(h + 1)
                key_products(h)
                if h:
                    value_products(h - 1)
            value_products(M_HEADS - 1)

            heads = NT * A_HEADS
            pe.wait_ge(S("decayed"), M_HEADS * NT)
            pe.wait_ge(S("num_out"), 2 * M_HEADS)
            for n in range(heads + 2):
                if n < heads:
                    t, h = divmod(n, A_HEADS)
                    if n >= 2:
                        pe.wait_ge(S("s_masked"), n - 1)
                    r = slice(64 * (h % 2), 64 * (h % 2) + 64)
                    mm(bank[4 + n % 2][:, 0:(t + 1) * P], z[r, Z_AQ + h // 2, t * P:(t + 1) * P],
                       z[r, Z_AK, 0:(t + 1) * P], start=True, stop=True).then_inc(S("s_dot"), 1)
                m = n - 1
                if 0 <= m < heads:
                    pe.wait_ge(S("p_ready"), m + 1)
                    if m >= 2:
                        pe.wait_ge(S("pt_ready"), m - 1)
                    transposes(bank[6 + m % 2], [prob[:, m % 3, s * P:(s + 1) * P] for s in range(m // A_HEADS + 1)]
                               ).then_inc(S("p_tr"), 1)
                m = n - 2
                if 0 <= m < heads:
                    t = m // A_HEADS
                    pe.wait_ge(S("pt_ready"), m + 1)
                    if m >= 2:
                        pe.wait_ge(S("o_out"), m - 1)
                    for s in range(t + 1):
                        ins = mm(bank[2 + m % 2][:, 0:A_DH], prob_t[:, m % 2, s, :],
                                 misc_t[:, s, MISC_AV:MISC_AV + A_DH], start=(s == 0), stop=(s == t))
                    ins.then_inc(S("o_dot"), 1)
                if n in HM_TR:
                    h = HM_TR.index(n)
                    pe.wait_ge(S("hm_ready"), 1)
                    if h >= 2:
                        pe.wait_ge(S("cat_m"), h - 1)
                    transposes(bank[h % 2], [hm[:, t, h, :] for t in range(NT)]).then_inc(S("hm_tr"), 1)
                if n >= ATT_TR and (n - ATT_TR) % A_HEADS == 0:
                    att_transposes((n - ATT_TR) // A_HEADS)
            att_transposes(NT - 1)
            tiles(("o", 0), KB, inputs=lambda k: pe.wait_ge(S("cat_low"), k + 1))
            square_sums(1)
            tiles(("q", 0), KB, inputs=normed_input(1))
            pe.wait_ge(S("tile_out"), TILE0["u", 0] + 2)
            pe.wait_ge(S("keys_in"), 16)
            for k in range(NT * P_HEADS // 2):
                t = k // 4
                if k >= 2:
                    pe.wait_ge(S("s_ready"), k - 1)
                for a in range(2):
                    h = 2 * (k % 4) + a
                    ins = mm(bank[4 + k % 2][:, a * 256:(a + 1) * 256], q_t[:, h, t * P:(t + 1) * P], keys[:, h, :],
                             start=True, stop=True)
                ins.then_inc(S("keys_dot"), 1)

            def gates(g, q, par):
                pe.wait_ge(S("gated"), q + (g * (T // GT) + 1))
                pe.wait_ge(S("rows1_ready"), q + (g * (T // GT) + 1))
                pe.wait_ge(S("rows2_ready"), q + (g * (T // GT) + 1))
                for n in range(GT):
                    dst = gate_bank[par][:, n * GI:(n + 1) * GI]
                    for k in range(3):
                        ins = mm(dst, rows2[:, par, :, n], rows1[:, par, k, :, n], start=(k == 0), stop=(k == 2))
                ins.then_inc(S("rows_used"), 1)

            def v_units(g, with_gates):
                first = FIRST["v", g]
                for half in range(2):
                    f = first + half * GI

                    def unit(i, u, start, stop):
                        s = (f + u) % SPLIT_SLOTS
                        pe.wait_ge(S("w_split"), i * 4 + (f + u + 1))
                        pe.wait_ge(S(f"c_split{g}"), i * 4 + (half * GI + u + 1))
                        for d in range(4):
                            if start and (g or half):
                                if g == GROUPS - 1 and half:
                                    pe.wait_ge(S("sums_added"), d + 1)
                                else:
                                    pe.wait_ge(S("y_out"), g * KB + (half - 1) * 4 + d + 1)
                            wh, wl = (w[:, s, d * P:(d + 1) * P] for w in (w_hi, w_lo))
                            dst = sum_bank[d][:, :]
                            mm(dst, wh, c_hi[:, s, :], start=start, stop=False)
                            mm(dst, wh, c_lo[:, s, :], start=False, stop=False)
                            ins = mm(dst, wl, c_hi[:, s, :], start=False, stop=stop)
                        ins.then_inc(S("unit_done"), 1)
                        if with_gates is not None:
                            gates(with_gates, i * 4 + (half * GI + u), u % 2)

                    for u in range(4):
                        unit(0, u, u == 0, False)
                    with pe.Fori(1, GI // 4 - 1) as i:
                        for u in range(4):
                            unit(i, u, False, False)
                    for u in range(4):
                        unit(GI // 4 - 1, u, False, u == 3)

            tiles(("u", 0), GI)
            pe.wait_ge(S("s_ready"), NT * P_HEADS // 2)
            pe.wait_ge(S("slots_ready"), NT)
            for k in range(3):
                transposes(bank[4 + k], [slot_t[:, k, t * P:(t + 1) * P] for t in range(NT)]).then_inc(S("slot_tr"), 1)
            tiles(("u", 1), GI, lambda i, q: gates(0, i * 4 + q, q % 2))
            pe.wait_ge(S("slot_out"), 3)
            for g in range(GROUPS):
                v_units(g, GROUPS - 1 if g == GROUPS - 2 else None)
                if g + 2 < GROUPS:
                    tiles(("u", g + 2), GI, lambda i, q: gates(g + 1, i * 4 + q, q % 2))
            square_sums(2, sq_end)


_INS = ["x_t", "cols", "wada", "stream", "keys"]


def lay_out(inputs):
    import numpy as np

    a = {k: np.asarray(v) for k, v in inputs.items()}
    f32 = np.float32
    by_block = lambda v: v.reshape(-1, P).T
    x_t = a["x"].reshape(T, KB, P).transpose(2, 1, 0)

    sizes = (512, 512, 512, 512, 4, 4, 512, 64, 64, 512, 64, 8)
    starts = np.concatenate([[0], np.cumsum(sizes)])
    mq, mk, mv, mo, mi, mf, aq, ak, av, iq, ik, iw = (slice(starts[n], starts[n + 1]) for n in range(12))
    w_in, b_in = a["w_in"][0], a["b_in"][0][None, :]

    def arrange(m):
        out = np.zeros((m.shape[0], Z_TILES * P), f32)
        put = lambda c, s: out.__setitem__((slice(None), slice(c, c + s.stop - s.start)), m[:, s])
        put(Z_IQ * P, iq)
        put(Z_IK * P, ik)
        put(Z_IK * P + 64, ik)
        put(Z_MISC * P + MISC_MI, mi)
        put(Z_MISC * P + MISC_IW, iw)
        put(Z_MISC * P + MISC_MF, mf)
        put(Z_MISC * P + MISC_AV, av)
        put(Z_AQ * P, aq)
        put(Z_AK * P, ak)
        put(Z_AK * P + 64, ak)
        for c, s in ((Z_MQ, mq), (Z_MK, mk), (Z_MV, mv), (Z_MO, mo)):
            put(c * P, s)
        return out

    cols = np.concatenate([
        by_block(a["c"].reshape(-1)), by_block(a["b_ada"].reshape(-1)), by_block(a["norm1_g"].reshape(-1)),
        by_block(arrange(b_in).reshape(-1)),
        a["conv_qk"][0].reshape(CONV_W, 8, P).transpose(2, 1, 0).reshape(P, 32),
        by_block(a["out_norm_m"].reshape(-1)), by_block(a["out_norm_a"].reshape(-1)),
        by_block(a["norm2_g"].reshape(-1)), by_block(a["final_g"].reshape(-1))], axis=1)
    wada = a["w_ada"][0].reshape(KB, P, 24, 256).transpose(2, 1, 0, 3)

    def units(w):
        n = w.shape[1] // P
        return w.reshape(2, 4, P, n, P).transpose(3, 0, 2, 1, 4).reshape(2 * n, P, UNIT)

    u, v = a["peer_u"][0], a["peer_v"][0]
    order, first = stream_order()
    stream = np.empty((UNITS, P, UNIT), f32)
    for name, g, n in order:
        e = slice(g * GI * N_KEYS, (g + 1) * GI * N_KEYS)
        if name == "u":
            part = units(u[e].T)
        elif name == "v":
            part = v[e].reshape(GI, P, 2, UNIT).transpose(2, 0, 1, 3).reshape(n, P, UNIT)
        else:
            part = units({"z": arrange(w_in) if name == "z" else None, "o": a["w_out"][0], "q": a["w_peer_q"][0]}[name])
        stream[first[name, g]:first[name, g] + n] = part
    keys = np.zeros((P, P_HEADS, 2 * N_KEYS), f32)
    sub = a["peer_sub_keys"][0]
    for side in range(2):
        keys[side * 64:(side + 1) * 64, :, side * N_KEYS:(side + 1) * N_KEYS] = sub[:, side].transpose(2, 0, 1)
    return {"x_t": x_t, "cols": cols, "wada": wada, "stream": stream, "keys": keys}


def kernel(**inputs):
    import numpy as np
    import concourse.bacc as bacc
    from concourse.bass_utils import run_bass_kernel_spmd

    nc = bacc.Bacc("TRN2", target_bir_lowering=False, num_devices=1)
    laid = lay_out(inputs)
    arrays, args = {}, []
    for name in _INS:
        arr = np.ascontiguousarray(laid[name])
        arrays[f"in_{name}"] = arr
        args.append(nc.dram_tensor(f"in_{name}", arr.shape, mybir.dt.float32, kind="ExternalInput").ap())
    out = nc.dram_tensor("out_t", [P, KB, T], mybir.dt.float32, kind="ExternalOutput").ap()
    build_layer(nc, *args, out)
    r = run_bass_kernel_spmd(nc, [arrays], core_ids=[0])
    return np.ascontiguousarray(np.asarray(r.results[0]["out_t"]).transpose(2, 1, 0)).reshape(1, T, D)
```

```python
import concourse.bass as bass
from concourse import mybir
from contextlib import ExitStack

D = 1024
T = 512
P = 128
KB = D // P
NT = T // P
CONV_W = 4
M_HEADS, M_DH = 4, 128
A_HEADS, A_DH = 8, 64
IDX_HEADS = 8
N_SEL = 128
P_HEADS, N_KEYS, P_TOPK = 8, 128, 16
EPS = 1e-6

Z_IQ, Z_IK, Z_MISC, Z_MQ, Z_MK, Z_AQ, Z_AK, Z_MV, Z_MO = 0, 4, 5, 6, 10, 14, 18, 19, 23
Z_TILES = 27
Z_HEAD = 6
ADA_HEAD, ADA_CHUNKS = 8, 24
ADA_DVE = 6
MISC_MI, MISC_IW, MISC_MF, MISC_AV = 0, 8, 32, 64

C_C, C_BADA, C_N1, C_BIN, C_CONV = 0, 8, 56, 64, 91
C_OUTN, C_N2, C_FG, C_END = 123, 131, 139, 147

GROUPS = 4
GI = N_KEYS // GROUPS
UNIT = 512
RAW_SLOTS, SPLIT_SLOTS = 4, 2
ZU, OU, QU, EU = 2 * Z_TILES, 2 * KB, 2 * KB, 2 * GI
UNITS = ZU + OU + QU + 2 * GROUPS * EU
GATE_SCALE = 2.0 ** 15
GT = 8
NEG, TAKEN = -1e30, -3e30


def stream_order():
    order = [("z", 0, ZU), ("o", 0, OU), ("q", 0, QU), ("u", 0, EU), ("u", 1, EU)]
    for g in range(GROUPS - 2):
        order += [("v", g, EU), ("u", g + 2, EU)]
    order += [("v", GROUPS - 2, EU), ("v", GROUPS - 1, EU)]
    first, at = {}, 0
    for name, g, n in order:
        first[name, g] = at
        at += n
    return order, first


class Steps:

    def __init__(self, eng, sem):
        self.eng, self.sem, self.n, self.turn, self.skipped = eng, sem, 0, None, 0

    def did(self, ins):
        ins.then_inc(self.sem, 1)
        self.n += 1

    def settle(self, back=0):
        n = self.n - back
        self.eng.wait_ge(self.sem, n if self.turn is None else self.turn + (n - self.skipped))

    def do(self, ins):
        self.did(ins)
        self.settle()

    def loop(self, start, end, per):
        return _StepLoop(self, start, end, per)


class Rounds(Steps):

    def turn_over(self):
        self.settle()
        self.eng.sem_clear(self.sem)
        self.n = 0


class _StepLoop:
    def __init__(self, steps, start, end, per):
        self.s, self.start, self.end, self.per = steps, start, end, per

    def __enter__(self):
        self.ctx = self.s.eng.Fori(self.start, self.end)
        i = self.ctx.__enter__()
        self.before = self.s.n
        self.s.turn, self.s.skipped = i * self.per, self.start * self.per
        return i

    def __exit__(self, *error):
        assert error[0] or self.s.n - self.before == self.per, (self.s.n - self.before, self.per)
        self.s.turn = None
        self.s.n = self.before + self.per * (self.end - self.start)
        return self.ctx.__exit__(*error)


def build_layer(nc, x_t, cols_in, wada_in, stream_in, keys_in, out):
    fp32, fp32r, u32, fp16 = mybir.dt.float32, mybir.dt.float32r, mybir.dt.uint32, mybir.dt.float16
    ALU, ACT, AX = mybir.AluOpType, mybir.ActivationFunctionType, mybir.AxisListType
    ds = bass.ds
    ORDER, FIRST = stream_order()

    x2_dram = nc.dram_tensor("x2_dram", [P, KB, T], fp32, kind="Internal").ap()
    part_dram = nc.dram_tensor("part_dram", [GROUPS - 1, KB, P, T], fp32, kind="Internal").ap()

    BASE = 16512

    def at(name, shape, offset, dt=fp32):
        size = 2 if dt == fp16 else 4
        for n in shape[1:]:
            size *= n
        assert BASE + offset + size <= 229344, (name, offset, size)
        return nc.alloc_sbuf_tensor_at(name, shape, dt, offset=BASE + offset)

    coef = at("coef", [P, 2 * GI, T], 0)
    A0 = 4 * 2 * GI * T
    hs_hi = at("hs_hi", [P, KB, T], A0, fp32r)
    hs_lo = at("hs_lo", [P, KB, T], A0 + 16384, fp32r)
    raw = at("raw", [P, RAW_SLOTS, UNIT], A0 + 32768)
    w_hi = at("w_hi", [P, SPLIT_SLOTS, UNIT], A0 + 40960, fp32r)
    w_lo = at("w_lo", [P, SPLIT_SLOTS, UNIT], A0 + 45056, fp32r)
    B0 = A0 + 49152
    c_hi = at("c_hi", [P, SPLIT_SLOTS, T], B0, fp32r)
    c_lo = at("c_lo", [P, SPLIT_SLOTS, T], B0 + 4096, fp32r)
    slot_i1 = at("slot_i1", [P, T], B0 + 8192, fp16)
    slot_i2 = at("slot_i2", [P, T], B0 + 9216, fp16)
    slot_g = at("slot_g", [P, 2, T], B0 + 10240, fp16)
    eq1 = at("eq1", [P, 2, GI, GT], B0 + 12288, fp16)
    rows1 = at("rows1", [P, 2, 2, GI, GT], B0 + 13312, fp16)
    rows2 = at("rows2", [P, 2, N_KEYS, GT], B0 + 15360, fp16)
    y_stage = at("y_stage", [P, 4, T], B0 + 19456)
    C0 = B0 + 27648
    cols = at("cols", [P, C_END], C0)
    ada = at("ada", [P, 48], C0 + 608)
    amp1 = at("amp1", [P, KB], C0 + 800)
    amp2 = at("amp2", [P, KB], C0 + 832)
    iota = at("iota", [P, N_KEYS], C0 + 864)
    ones = at("ones", [P, P], C0 + 1376)
    ident = at("ident", [P, P], C0 + 1888)
    silu_c = at("silu_c", [P, KB], C0 + 2400)
    key_rep = at("key_rep", [P, N_KEYS, GT], C0 + 2432, fp16)

    def fa(name, shape, offset, dt=fp32):
        return at(name, shape, 4 * offset, dt)

    def fb(name, shape, offset, dt=fp32):
        return at(name, shape, B0 + 4 * offset, dt)

    x = fa("x", [P, KB, T], 0)
    z = fa("z", [P, Z_TILES, T], 4096)
    ada_w0 = fa("ada_w0", [P, ADA_HEAD, KB, 256], 16384)
    ada_acc0 = fa("ada_acc0", [P, ADA_HEAD, 256], 12800)
    ada_w = fa("ada_w", [P, 3, KB, 256], 17920)
    qk = fa("qk", [P, 2 * M_HEADS, T], 24064)
    mask = fa("mask", [P, 1280], 28160)
    score = fa("score", [P, 1152], 29440)
    relu = fa("relu", [P, 2, T], 30592)
    misc_t = fa("misc_t", [P, NT, P], 31616)
    emm = fa("emm", [P, NT, M_HEADS], 32128)
    wcol = fa("wcol", [P, NT, M_HEADS], 32144)
    den = fa("den", [P, NT, M_HEADS], 32160)
    hrs = fa("hrs", [P, NT, M_HEADS], 32176)
    ada_acc = fb("ada_acc", [P, 2, 256], 6200)
    best8 = fb("best8", [P, 3 * 8], 6144)
    s_max = fa("s_max", [P, 4], 32192)
    s_sum = fa("s_sum", [P, 4], 32200)
    s_neg = fa("s_neg", [P, 4], 32208)
    o_rs = fa("o_rs", [P, NT, A_HEADS], 32216)
    v_aug = fa("v_aug", [P, NT, M_HEADS, M_DH + 1], 4096 + T * Z_IQ)
    i_hi = fb("i_hi", [P, 5, T], 0, fp32r)
    i_lo = fa("i_lo", [P, 5, T], 4096 + T * Z_IQ, fp32r)
    aq_hi = at("aq_hi", [P, 4, T], A0 + 16384 + 4 * T * 4, fp32r)
    ak_hi = at("ak_hi", [P, T], A0 + 4 * T * 7, fp32r)
    a_lo = fa("a_lo", [P, 5, T], 4096 + T * Z_AQ, fp32r)
    decay = [fa(f"decay{n}", [P, 1280], o) for n, o in enumerate((29440, 19984, 21264))]
    num = fa("num", [P, NT, M_HEADS, M_DH + 1], 17920)
    hm = fa("hm", [P, NT, M_HEADS, M_DH], 4096 + T * Z_MQ)
    hm2 = fa("hm2", [P, NT, M_HEADS, M_DH], 4096 + T * Z_MK)
    h_tmp = fa("h_tmp", [P, KB, T], 4096)
    rstd = fa("rstd", [P, T], 4096 + T * KB)
    sq = fa("sq", [P, KB, T], 4096 + T * (KB + 1))
    prob = fb("prob", [P, 3, T], 0)
    prob_t = fb("prob_t", [P, 2, NT, P], 1536)
    att = fa("att", [P, NT, A_HEADS, A_DH], 24064)
    att2 = fb("att2", [P, A_HEADS, A_DH], 2560)
    rows = fb("rows", [P, 5, T], 3072)
    R_LF, R_B, R_W, R_MX, R_M = range(5)
    sel = fb("sel", [P, M_HEADS, P], 5632)
    q_t = fa("q_t", [P, P_HEADS, T], 4096)
    s12 = fa("s12", [P, P_HEADS, NT, 2, N_KEYS], 16384)
    keys = fa("keys", [P, P_HEADS, 2 * N_KEYS], 24576)
    best = fa("best", [P, NT * P_HEADS, 2, P_TOPK], 26624)
    best_iu = fa("best_iu", [P, NT * P_HEADS, 2, P_TOPK], 27648, u32)
    top = fa("top", [P, NT * P_HEADS, P_TOPK], 28672)
    pos_u = fa("pos_u", [P, NT * P_HEADS, P_TOPK], 29184, u32)
    cand = fa("cand", [P, 2, 2, P_TOPK * P_TOPK], 29696)
    gsum = fa("gsum", [P, NT * P_HEADS], 30720)
    best_if = fb("best_if", [P, NT * P_HEADS, 2, P_TOPK], 0)
    pos_f = fb("pos_f", [P, 2, NT * P_HEADS, P_TOPK], 1024)
    pick = fa("pick", [P, P_HEADS, P_TOPK, P_TOPK], 16384)
    slot_t = fa("slot_t", [P, 3, NT * P_HEADS * P_TOPK], 18432)
    slot_gf = fa("slot_gf", [P, T], 19968)
    part = fa("part", [P, 4, KB, T], 0)
    sq_end = fa("sq_end", [P, KB, T], 16384)
    rstd_end = fa("rstd_end", [P, T], 20480)

    bank = [nc.alloc_psum_tensor(f"bank{i}", [P, 512], fp32) for i in range(8)]

    ctx = ExitStack()
    with ctx:
        names = {}

        def S(name):
            if name not in names:
                names[name] = ctx.enter_context(nc.semaphore(name))
            return names[name]

        raw_ready = [S(f"raw_ready{i}") for i in range(RAW_SLOTS)]
        block = ctx.enter_context(nc.Block())

        tile_bank = bank[0:2]
        gate_bank = bank[2:4]
        sum_bank = bank[4:8]

        def ada_loads(c):
            return (c - ADA_HEAD) // 3 + 1

        HM_TR = (8, 9, 11, 12)
        ATT_TR = 2 * A_HEADS

        def att_bank(t):
            return bank[t % 2] if t < NT - 1 else bank[2]

        A_SPLIT = ((0, 1), (2, 3), (4,), ())

        def a_high(k):
            return aq_hi[:, k, :] if k < 4 else ak_hi[:, :]

        SILU_AFTER = {16: (0, 1), 17: (2, 3), 18: (4, 5), Z_TILES - 2: (6, 7)}
        IDX_TILE = 8
        POOL_ADA = 26
        ADA_POOL = 18
        ADA_SCALE_AFTER = (11, 13, 15, 17, 20, 22)

        def ada_summed(eng, c):
            if c < ADA_POOL:
                eng.wait_ge(S("ada_summed"), c + 1)
            else:
                eng.wait_ge(S("ada_summed_pool"), c - ADA_POOL + 1)

        ADA_BESIDE = (1, 2, 3, 4, 5, 6, 7, 9, 11, 13, 16, 18, 20, 23, 25, Z_TILES - 1)
        ADA_LOAD_AFTER = (1, 2, 3, 4, 5, 6, 7, 9, 10, 12, 15, 17, 20)
        V_TR = Z_MV + 3
        TILE0 = {("z", 0): 0, ("o", 0): Z_TILES, ("q", 0): Z_TILES + KB}
        for g in range(GROUPS):
            TILE0["u", g] = Z_TILES + 2 * KB + g * GI

        @block.sync
        def _(sp):
            sp.wait_ge(S("x_in"), 16)
            for c in range(ADA_HEAD):
                sp.dma_start(ada_w0[:, c, :, :], wada_in[c]).then_inc(S(f"ada_head{c}"), 16)
            for n in range(RAW_SLOTS):
                sp.dma_start(raw[:, n, :], stream_in[n]).then_inc(raw_ready[n], 16)

            def refill(n, slot):
                sp.wait_ge(S("w_split"), n - (RAW_SLOTS - 1))
                src = stream_in[n] if isinstance(n, int) else stream_in[ds(n, 1), :, :].rearrange("a p f -> (a p) f")
                sp.dma_start(raw[:, slot, :], src).then_inc(raw_ready[slot], 16)

            def refills(first, end):
                turns = (end - first) // RAW_SLOTS
                if turns:
                    with sp.Fori(0, turns) as i:
                        for s in range(RAW_SLOTS):
                            refill(i * RAW_SLOTS + (first + s), (first + s) % RAW_SLOTS)
                for n in range(first + turns * RAW_SLOTS, end):
                    refill(n, n % RAW_SLOTS)

            at = RAW_SLOTS
            for g in range(GROUPS - 1):
                for half in range(2):
                    end = FIRST["v", g] + (half + 1) * GI + RAW_SLOTS
                    refills(at, end)
                    at = end
                    for d in range(4):
                        k = half * 4 + d
                        sp.wait_ge(S("y_out"), g * KB + k + 1)
                        sp.dma_start(part_dram[g, k], y_stage[:, d, :]).then_inc(S(f"part_saved{d}"), 16)
            sp.wait_ge(S("x2_saved"), 16)
            for d in range(4):
                sp.wait_ge(S(f"part_saved{d}"), 16 * 2 * (GROUPS - 1))
            sp.wait_ge(S("c_split2"), EU)
            with sp.Fori(0, KB) as k:
                sp.dma_start(part[:, 3, ds(k, 1), :], x2_dram[:, ds(k, 1), :]).then_inc(S("x2_back"), 16)
                for s in range(4):
                    refill(k * 4 + (at + s), (at + s) % RAW_SLOTS)
                    if s < GROUPS - 1:
                        sp.dma_start(part[:, s, ds(k, 1), :], part_dram[s, ds(k, 1), :, :].rearrange("k p t -> p k t")
                                     ).then_inc(S("part_back"), 16)
            refills(at + 4 * KB, UNITS)

        def coef_lows(eng, own, subtract, g, other=None, halfway=(), beside=None, begun=None):
            first, buf = FIRST["v", g], (g % 2) * GI

            def clow(k, s, i1):
                eng.wait_ge(S(f"c_high{g}"), k + 1)
                src = coef[:, i1, :] if isinstance(i1, int) else coef[:, ds(i1, 1), :]
                subtract(c_lo[:, s % SPLIT_SLOTS, :], src, c_hi[:, s % SPLIT_SLOTS, :].bitcast(fp32), ALU.subtract
                         ).then_inc(S(f"c_split{g}"), 1)

            clow(0, first, buf)
            if begun:
                begun()
            clow(1, first + 1, buf + 1)
            halfway = list(halfway)
            for half in range(2):
                f = half * GI
                along = beside if half else None
                with (own.loop(0, GI // 4 - 1, 3) if along else eng.Fori(0, GI // 4 - 1)) as i:
                    for u in range(4):
                        if other:
                            other(i * 4 + (first + f + u + 2), first + f + u + 2)
                        clow(i * 4 + (f + u + 2), first + u, i * 4 + (buf + u + 2))
                        if along and u < 3:
                            along(i, u)
                for u in range(4):
                    k = GI - 4 + u + 2
                    if other:
                        other(first + f + k, first + f + k)
                    if k < GI or half == 0:
                        clow(f + k, first + k, buf + k % GI)
                    if along and u < 3:
                        along(GI // 4 - 1, u)
                    if k >= GI and half == 0 and halfway:
                        halfway.pop(0)()

        @block.gpsimd
        def _(pool):
            own = Steps(pool, S("pool_own"))
            own.do(pool.memset(ones[:, :], 1.0))
            own.do(pool.memset(ident[:, :], 0.0))
            own.do(pool.affine_select(out=ident[:, :], in_=ident[:, :], compare_op=ALU.not_equal, fill=1.0, base=0,
                                      pattern=[[-1, P]], channel_multiplier=1))
            own.do(pool.iota(iota[:, :], pattern=[[1, N_KEYS]], base=0, channel_multiplier=0,
                             allow_small_or_imprecise_dtypes=True))
            own.do(pool.iota(key_rep[:, :, :], pattern=[[1, N_KEYS], [0, GT]], base=0, channel_multiplier=0,
                             allow_small_or_imprecise_dtypes=True))
            own.do(pool.memset(sel[:, :, :], 0.0))
            own.do(pool.affine_select(out=sel[:, :, :], in_=sel[:, :, :], compare_op=ALU.not_equal, fill=-1.0, base=0,
                                      pattern=[[-1, M_HEADS], [0, P]], channel_multiplier=1))
            pool.sem_inc(S("consts"), 1)

            def norm_low(n):
                for k in range(KB // 2):
                    pool.wait_ge(S("h_high"), KB * n + k + 1)
                    pool.tensor_tensor(hs_lo[:, k, :], h_tmp[:, k, :], hs_hi[:, k, :].bitcast(fp32), ALU.subtract
                                       ).then_inc(S("h_low"), 1)

            def low(n, slot):
                pool.wait_ge(S("w_high"), n + 1)
                pool.tensor_tensor(w_lo[:, slot % SPLIT_SLOTS, :], raw[:, slot % RAW_SLOTS, :],
                                   w_hi[:, slot % SPLIT_SLOTS, :].bitcast(fp32), ALU.subtract).then_inc(S("w_split"), 1)

            def lows(first, count):
                with pool.Fori(0, count // 4) as i:
                    for u in range(4):
                        low(i * 4 + (first + u), first + u)
                for n in range(first + count // 4 * 4, first + count):
                    low(n, n)

            for c in range(ADA_HEAD):
                if c >= ADA_HEAD // 2:
                    if c == ADA_HEAD // 2:
                        pool.wait_ge(S("rstd0"), 1)
                        pool.wait_ge(S("x_in"), 16)
                    for k in (2 * c - ADA_HEAD, 2 * c - ADA_HEAD + 1):
                        own.did(pool.tensor_tensor(h_tmp[:, k, :], x[:, k, :], rstd[:, :], ALU.mult))
                pool.wait_ge(S("ada_scaled"), c + 1)
                w = ada_w0[:, c, :, :]
                for k in range(ADA_DVE + 1, KB):
                    ins = pool.tensor_tensor(w[:, ADA_DVE, :], w[:, ADA_DVE, :], w[:, k, :], ALU.add)
                    if k < KB - 1:
                        own.do(ins)
                ins.then_inc(S("ada_paired"), 1)
            own.settle()
            pool.sem_inc(S("x_scaled"), 1)
            low(0, 0)
            low(1, 1)
            norm_low(0)
            own.do(pool.memset(mask[:, 0:P], 0.0))
            pool.affine_select(out=mask[:, 0:P], in_=mask[:, 0:P], compare_op=ALU.is_ge, fill=NEG, base=0,
                               pattern=[[-1, P]], channel_multiplier=1).then_inc(S("mask0"), 1)
            for t in range(5):
                low(2 * t + 2, 2 * t + 2)
                low(2 * t + 3, 2 * t + 3)
                pool.wait_ge(S("i_high"), t + 1)
                pool.tensor_tensor(i_lo[:, t, :], z[:, Z_IQ + t, :], i_hi[:, t, :].bitcast(fp32), ALU.subtract
                                   ).then_inc(S("i_low"), 1)
            lows(12, POOL_ADA - 12)
            steps = [(c, k) for c in range(ADA_POOL, ADA_CHUNKS) for k in range(1, KB)]
            for n in range(ZU + 2 - POOL_ADA):
                low(POOL_ADA + n, POOL_ADA + n)
                for c, k in steps[3 * n // 2:3 * (n + 1) // 2]:
                    w, acc = ada_w[:, c % 3, :, :], ada_acc[:, c % 2, :]
                    if k == 1:
                        pool.wait_ge(S("ada_scaled"), ADA_HEAD + c - ADA_POOL + 1)
                        pool.wait_ge(S("ada_used"), c - 1)
                    else:
                        own.settle()
                    ins = pool.tensor_tensor(acc, w[:, 0, :] if k == 1 else acc, w[:, k, :], ALU.add)
                    if k < KB - 1:
                        own.did(ins)
                    else:
                        ins.then_inc(S("ada_summed_pool"), 1)
            for h in range(M_HEADS):
                pool.wait_ge(S("decay_exp"), h + 1)
                off = 0
                for j in range(NT):
                    blk = decay[h % 3][:, off:off + P]
                    ins = pool.affine_select(out=blk, in_=blk, compare_op=ALU.is_ge, fill=0.0, base=0,
                                             pattern=[[1, P]], channel_multiplier=-1)
                    off += (NT - j) * P
                ins.then_inc(S("decay_cut"), 1)
                for k in A_SPLIT[h]:
                    pool.wait_ge(S("a_high"), k + 1)
                    pool.tensor_tensor(a_lo[:, k, :], z[:, Z_AQ + k, :], a_high(k).bitcast(fp32), ALU.subtract
                                       ).then_inc(S("a_low"), 1)
            for k in range(KB):
                src = z[:, Z_MO + k, :] if k < 4 else z[:, Z_IQ + k - 4, :]
                pool.wait_ge(S("cat_high"), k + 1)
                pool.tensor_tensor(hs_lo[:, k, :], src, hs_hi[:, k, :].bitcast(fp32), ALU.subtract
                                   ).then_inc(S("cat_low"), 1)
            lows(ZU + 2, OU)
            norm_low(1)
            lows(ZU + OU + 2, QU + EU * 2)
            for g in range(GROUPS):
                first = FIRST["v", g]
                if g == GROUPS - 2:
                    coef_lows(pool, own, pool.tensor_tensor, g, low, begun=lambda: low(first + 1, first + 1))
                elif g < GROUPS - 1:
                    lows(first + 2, EU)
                else:
                    lows(first + 2, EU - 4)
                    low(UNITS - 2, UNITS - 2)
                    low(UNITS - 1, UNITS - 1)
                if g + 2 < GROUPS:
                    lows(FIRST["u", g + 2] + 2, EU - (g + 2 == GROUPS - 1))

        @block.scalar
        def _(act):
            own = Steps(act, S("act_own"))
            A = act.activation
            act.dma_start(cols[:, :], cols_in).then_inc(S("cols_in"), 16)
            act.dma_start(x[:, :, :], x_t).then_inc(S("x_in"), 16)
            def ada_load(c):
                ada_summed(act, max(c - 3, ADA_HEAD - 1))
                act.dma_start(ada_w[:, c % 3, :, :], wada_in[c]).then_inc(S(f"ada_in{c % 3}"), 16)
            act.wait_ge(S("cols_in"), 16)
            A(silu_c[:, :], cols[:, C_C:C_C + KB], ACT.Silu).then_inc(S("c_silu"), 1)
            act.wait_ge(S("x_in"), 16)
            for k in range(KB):
                A(sq[:, k, :], x[:, k, :], ACT.Square).then_inc(S("x_sq"), 1)
            act.sem_inc(S("tile_out"), 2)

            def high_at(i, slot, free=True):
                if free:
                    act.wait_ge(S("unit_done"), i * 4 + (slot - 1) if i is not None else slot - 1)
                full = 16 * (slot // RAW_SLOTS + 1)
                act.wait_ge(raw_ready[slot % RAW_SLOTS], i * 16 + full if i is not None else full)
                A(w_hi[:, slot % SPLIT_SLOTS, :], raw[:, slot % RAW_SLOTS, :], ACT.Copy).then_inc(S("w_high"), 1)

            def root_table():
                own.do(A(silu_c[:, 1:2], ones[:, 0:1], ACT.Sqrt))

            def root(n):
                act.wait_ge(S("mean_ready"), n + 1)
                A(rstd[:, :], rstd[:, :], ACT.Sqrt).then_inc(S("root_ready"), 1)

            def norm_high(n):
                for k in range(KB):
                    act.wait_ge(S("h_ready"), KB * n + k + 1)
                    A(hs_hi[:, k, :], h_tmp[:, k, :], ACT.Copy).then_inc(S("h_high"), 1)

            act.wait_ge(S("c_silu"), 1)
            for c in range(ADA_HEAD):
                act.wait_ge(S(f"ada_head{c}"), 16)
                for k in range(ADA_DVE, KB):
                    ins = A(ada_w0[:, c, k, :], ada_w0[:, c, k, :], ACT.Copy, scale=silu_c[:, k:k + 1])
                ins.then_inc(S("ada_scaled"), 1)
                if c == 2:
                    root(0)
            high_at(None, 0, False)
            high_at(None, 1, False)
            norm_high(0)
            def z_out(t, bankno):
                act.wait_ge(S("unit_done"), t * 2 + 2)
                dst = z[:, t, :] if isinstance(t, int) else z[:, ds(t, 1), :]
                b = cols[:, C_BIN + t:C_BIN + t + 1] if isinstance(t, int) else cols[:, ds(t + C_BIN, 1)]
                A(dst, tile_bank[bankno][:, :], ACT.Identity, bias=b).then_inc(S("tile_out"), 1)

            act.wait_ge(S("h_low"), KB // 2)
            act.wait_ge(S("h_low_late"), KB // 2)
            for c in range(ADA_HEAD, ADA_HEAD + 3):
                ada_load(c)
            idx_tiles = [t for t in range(1, NT) for h in range(IDX_HEADS)]
            for t in range(Z_TILES):
                high_at(None, 2 * t + 2)
                high_at(None, 2 * t + 3)
                z_out(t, t % 2)
                if t < 5:
                    act.wait_ge(S("tile_out"), t + 3)
                    A(i_hi[:, t, :], z[:, Z_IQ + t, :], ACT.Copy).then_inc(S("i_high"), 1)
                if t == Z_HEAD:
                    act.wait_ge(S("misc_tr"), 1)
                    A(misc_t[:, :, :], bank[3][:, :].rearrange("p (t c) -> p t c", t=NT), ACT.Copy
                      ).then_inc(S("misc_ready"), 1)
                for n in range(4 * (t - IDX_TILE), 4 * (t - IDX_TILE + 1)):
                    if 0 <= n < len(idx_tiles):
                        w = (idx_tiles[n] + 1) * P
                        act.wait_ge(S("idx_dot"), n + 1)
                        if n >= 2:
                            act.wait_ge(S("idx_added"), n - 1)
                        A(relu[:, n % 2, 0:w], bank[4 + n % 4][:, 0:w], ACT.Relu).then_inc(S("idx_relu"), 1)
                if t in ADA_LOAD_AFTER:
                    ada_load(ADA_HEAD + 3 + ADA_LOAD_AFTER.index(t))
                if t in ADA_SCALE_AFTER:
                    c = ADA_POOL + ADA_SCALE_AFTER.index(t)
                    act.wait_ge(S(f"ada_in{c % 3}"), 16 * ada_loads(c))
                    for k in range(KB):
                        ins = A(ada_w[:, c % 3, k, :], ada_w[:, c % 3, k, :], ACT.Copy, scale=silu_c[:, k:k + 1])
                    ins.then_inc(S("ada_scaled"), 1)
                if t == Z_HEAD + 1:
                    f_row = z[32:36, Z_MISC, :]
                    own.do(A(rows[32:36, 0, :], f_row, ACT.Abs))
                    own.do(A(rows[32:36, 1, :], rows[32:36, 0, :], ACT.Exp, scale=-1.0))
                    A(rows[32:36, 2, :], rows[32:36, 1, :], ACT.Ln, bias=1.0).then_inc(S("soft_f"), 1)
                for c in SILU_AFTER.get(t, ()):
                    act.wait_ge(S("conv"), c + 1)
                    A(qk[:, c, :], qk[:, c, :], ACT.Silu).then_inc(S("qk_ready"), 1)
                h = t - V_TR
                if 0 <= h < M_HEADS:
                    act.wait_ge(S("v_tr"), h + 1)
                    A(v_aug[:, :, h, 0:M_DH], bank[4 + h][:, :].rearrange("p (j d) -> p j d", j=NT),
                      ACT.Copy).then_inc(S("v_ready"), 1)
            act.wait_ge(S("tile_out"), Z_TILES + 2)
            act.wait_ge(S("col_tr"), 1)
            A(wcol[:, :, :], bank[3][:, 0:NT * M_HEADS].rearrange("p (j h) -> p j h", j=NT), ACT.Copy
              ).then_inc(S("wcol_ready"), 1)
            act.wait_ge(S("wcol_ready"), 1)
            A(emm[:, :, :], bank[3][:, 16:16 + NT * M_HEADS].rearrange("p (j h) -> p j h", j=NT), ACT.Exp,
              scale=-1.0).then_inc(S("emm_ready"), 1)
            for h in range(M_HEADS):
                act.wait_ge(S("decay_arg"), h + 1)
                A(decay[h % 3][:, :], decay[h % 3][:, :], ACT.Exp).then_inc(S("decay_exp"), 1)
                for k in A_SPLIT[h]:
                    act.wait_ge(S("unit_done"), ZU)
                    A(a_high(k), z[:, Z_AQ + k, :], ACT.Copy).then_inc(S("a_high"), 1)
            for h in range(M_HEADS):
                A(z[:, Z_MO + h, :], z[:, Z_MO + h, :], ACT.Sigmoid).then_inc(S("mo_gate"), 1)
            heads = NT * A_HEADS

            def att_root(t):
                act.wait_ge(S("att_mean"), t + 1)
                A(o_rs[:, t, :], o_rs[:, t, :], ACT.Sqrt).then_inc(S("att_root"), 1)

            def cat_high(k):
                src = z[:, Z_MO + k, :] if k < 4 else z[:, Z_IQ + k - 4, :]
                A(hs_hi[:, k, :], src, ACT.Copy).then_inc(S("cat_high"), 1)

            for n in range(heads + 1):
                if n < heads:
                    act.wait_ge(S("s_masked"), n + 1)
                    w = (n // A_HEADS + 1) * P
                    A(prob[:, n % 3, 0:w], prob[:, n % 3, 0:w], ACT.Exp, bias=s_neg[:, n % 4:n % 4 + 1],
                      scale=A_DH ** -0.5, accum_out=s_sum[:, n % 4:n % 4 + 1]).then_inc(S("p_ready"), 1)
                m = n - 1
                if m >= 0:
                    tiles_of = m // A_HEADS + 1
                    act.wait_ge(S("p_tr"), m + 1)
                    if m >= 2:
                        act.wait_ge(S("o_dot"), m - 1)
                    A(prob_t[:, m % 2, 0:tiles_of, :], bank[6 + m % 2][:, 0:tiles_of * P].rearrange(
                        "p (s q) -> p s q", q=P), ACT.Copy).then_inc(S("pt_ready"), 1)
                if n == 5:
                    act.wait_ge(S("hm_mean"), 1)
                    A(hrs[:, :, :], hrs[:, :, :], ACT.Sqrt).then_inc(S("hm_root"), 1)
                if n > A_HEADS + 4 and n % A_HEADS == 5:
                    att_root(n // A_HEADS - 1)
                if n == 18:
                    for k in range(4):
                        act.wait_ge(S("cat_m"), k + 1)
                        cat_high(k)
            att_root(NT - 1)
            act.wait_ge(S("cat_a"), NT)
            for k in range(4, KB):
                cat_high(k)
            act.dma_start(keys[:, :, :], keys_in).then_inc(S("keys_in"), 16)

            def highs(first, count):
                with act.Fori(0, count // 4) as i:
                    for u in range(4):
                        high_at(i, first + u)

            highs(ZU + 2, OU)
            act.wait_ge(S("consts"), 1)
            act.wait_ge(S("ada_summed"), ADA_POOL)
            root_table()
            for k in range(KB):
                act.wait_ge(S("tile_out"), TILE0["o", 0] + k + 3)
                A(sq[:, k, :], x[:, k, :], ACT.Square).then_inc(S("x_sq"), 1)
            act.dma_start(x2_dram, x[:, :, :]).then_inc(S("x2_saved"), 16)
            root(1)
            norm_high(1)
            def scores_out(k):
                act.wait_ge(S("keys_dot"), k + 1)
                A(s12[:, k // 2, 2 * (k % 2):2 * (k % 2) + 2, :, :], bank[4 + k % 4][:, :].rearrange(
                    "p (t a e) -> p t a e", t=2, a=2), ACT.Copy).then_inc(S("s_ready"), 1)

            act.wait_ge(S("h_low"), KB)
            act.wait_ge(S("h_low_late"), KB)
            for h in range(P_HEADS):
                u = FIRST["q", 0] + 2 * h + 2
                high_at(None, u)
                high_at(None, u + 1)
                act.wait_ge(S("unit_done"), u)
                A(q_t[:, h, :], tile_bank[(TILE0["q", 0] + h) % 2][:, :], ACT.Copy).then_inc(S("tile_out"), 1)
                if h:
                    scores_out(2 * h - 2)
                    scores_out(2 * h - 1)
            scores_out(2 * P_HEADS - 2)
            scores_out(2 * P_HEADS - 1)

            def u_tile(g, i, j, early=None):
                u = FIRST["u", g] + 2 + 2 * j
                high_at(i, u)
                if early:
                    early()
                high_at(i, u + 1)
                act.wait_ge(S("unit_done"), i * 4 + u)
                tile_no = i * 2 + ((g % 2) * GI + j)
                dst = coef[:, tile_no, :] if isinstance(i, int) else coef[:, ds(tile_no, 1), :]
                A(dst, tile_bank[(TILE0["u", g] + j) % 2][:, :], ACT.Gelu).then_inc(S("tile_out"), 1)

            def u_tiles(g):
                with act.Fori(0, GI // 2 - 1) as i:
                    for j in range(2):
                        u_tile(g, i, j)

            def chigh(g, slot, i1):
                src = coef[:, i1, :] if isinstance(i1, int) else coef[:, ds(i1, 1), :]
                A(c_hi[:, slot % SPLIT_SLOTS, :], src, ACT.Copy).then_inc(S(f"c_high{g}"), 1)

            def first_chighs(g, which=(0, 1)):
                act.wait_ge(S("gated"), (g + 1) * T // GT + 2)
                for k in which:
                    chigh(g, FIRST["v", g] + k, (g % 2) * GI + k)

            def v_units(g):
                first, buf = FIRST["v", g], (g % 2) * GI
                if g == GROUPS - 1:
                    first_chighs(g, (1,))
                for half in range(2):
                    f = first + half * GI
                    with act.Fori(0, GI // 4 - 1) as i:
                        for u in range(4):
                            high_at(i, f + u + 2)
                            chigh(g, f + u + 2, i * 4 + (buf + u + 2))
                    for u in range(4):
                        k = GI - 4 + u + 2
                        if g == GROUPS - 2 and half and u == 3:
                            first_chighs(g + 1, (0,))
                        if f + k < UNITS:
                            high_at(None, f + k)
                        if k < GI or half == 0:
                            if f + k >= UNITS:
                                act.wait_ge(S("unit_done"), f + k - 1)
                            chigh(g, f + k, buf + k % GI)

            def gelu_table():
                act.wait_ge(S("c_silu"), 1)
                own.do(A(silu_c[:, 0:1], silu_c[:, 0:1], ACT.Gelu))

            act.wait_ge(S("x2_saved"), 16)
            gelu_table()
            u_tiles(0)
            for t in range(NT):
                act.wait_ge(S("top_shift"), t + 1)
                A(top[:, t * 8:(t + 1) * 8, :], top[:, t * 8:(t + 1) * 8, :], ACT.Exp).then_inc(S("top_exp"), 1)
            u_tile(0, GI // 2 - 1, 0)
            u_tile(0, GI // 2 - 1, 1)
            for k in range(3):
                act.wait_ge(S("slot_tr"), k + 1)
                dst = (slot_i1, slot_i2, slot_gf)[k]
                A(dst[:, :], bank[4 + k][:, :], ACT.Copy, scale=GATE_SCALE if k == 2 else 1.0
                  ).then_inc(S("slot_out"), 1)
            act.wait_ge(S("gate_split"), 1)
            gelu_table()
            for g in range(GROUPS):
                if g + 1 < GROUPS:
                    if g:
                        act.wait_ge(S(f"c_split{g - 1}"), EU)
                    u_tiles(g + 1)
                    u_tile(g + 1, GI // 2 - 1, 0)
                    u_tile(g + 1, GI // 2 - 1, 1, lambda: first_chighs(g))
                v_units(g)
            root_table()
            for k in range(KB):
                act.wait_ge(S("earlier_added"), min(k + 2, KB))
                act.wait_ge(S("sums_added"), k + 1)
                A(sq_end[:, k, :], part[:, 3, k, :], ACT.Square).then_inc(S("x_sq"), 1)
            act.wait_ge(S("mean_ready"), 3)
            A(rstd_end[:, :], rstd_end[:, :], ACT.Sqrt).then_inc(S("root_ready"), 1)
            for k in range(KB):
                act.wait_ge(S("out_ready"), k + 1)
                act.dma_start(out[:, k, :], part[:, 2, k, :]).then_inc(S("out_saved"), 16)
            act.wait_ge(S("out_saved"), 16 * KB)

        @block.vector
        def _(dve):
            own = Steps(dve, S("dve_own"))
            rnd = Rounds(dve, S("dve_round"))
            V = nc.vector

            dve.sem_inc(S("gated"), 2)

            def mean(n, src_bank, rstd=rstd):
                dve.wait_ge(S("sq_sum"), n + 1)
                V.tensor_scalar(rstd[:, :], src_bank[:, :], 1.0 / D, EPS, ALU.mult, ALU.add
                                ).then_inc(S("mean_ready"), 1)
                dve.wait_ge(S("root_ready"), n + 1)
                own.do(V.reciprocal(rstd[:, :], rstd[:, :]))

            def normed(amp, shift, k):
                V.tensor_scalar(h_tmp[:, k, :], h_tmp[:, k, :], amp[:, k:k + 1], ada[:, shift + k:shift + k + 1],
                                ALU.mult, ALU.add).then_inc(S("h_ready"), 1)

            def ada_sums(c):
                if c < ADA_HEAD:
                    dve.wait_ge(S(f"ada_head{c}"), 16)
                    w, acc, blocks = ada_w0[:, c, :, :], ada_acc0[:, c, :], ADA_DVE
                else:
                    dve.wait_ge(S(f"ada_in{c % 3}"), 16 * ada_loads(c))
                    if c >= ADA_HEAD + 2:
                        dve.wait_ge(S("ada_used"), c - 1)
                    w, acc, blocks = ada_w[:, c % 3, :, :], ada_acc[:, c % 2, :], KB
                for k in range(blocks):
                    if k == 0:
                        ins = V.tensor_scalar(acc, w[:, k, :], silu_c[:, k:k + 1], None, ALU.mult)
                    else:
                        ins = V.scalar_tensor_tensor(out=acc, in0=w[:, k, :], scalar=silu_c[:, k:k + 1], in1=acc,
                                                     op0=ALU.mult, op1=ALU.add)
                    if k < blocks - 1:
                        own.do(ins)
                ins.then_inc(S("ada_summed"), 1)

            dve.wait_ge(S("c_silu"), 1)
            dve.wait_ge(S("cols_in"), 16)
            for c in range(ADA_HEAD):
                ada_sums(c)
                if c == 2:
                    mean(0, bank[3])
                    dve.sem_inc(S("rstd0"), 1)
            def late_lows(n):
                for k in range(KB // 2, KB):
                    dve.wait_ge(S("h_high"), KB * n + k + 1)
                    V.tensor_tensor(hs_lo[:, k, :], h_tmp[:, k, :], hs_hi[:, k, :].bitcast(fp32), ALU.subtract
                                    ).then_inc(S("h_low_late"), 1)

            dve.wait_ge(S("cols_in"), 16)
            dve.wait_ge(S("ada_used"), ADA_HEAD)
            own.do(V.tensor_tensor(ada[:, 0:16], bank[2][:, 0:16], cols[:, C_BADA:C_BADA + 16], ALU.add))
            own.do(V.scalar_tensor_tensor(out=amp1[:, :], in0=ada[:, 8:16], scalar=1.0, in1=cols[:, C_N1:C_N1 + 8],
                                          op0=ALU.add, op1=ALU.mult))
            dve.wait_ge(S("x_scaled"), 1)
            for k in range(KB):
                normed(amp1, 0, k)
            late_lows(0)
            dve.wait_ge(S("consts"), 1)
            dve.wait_ge(S("mask0"), 1)
            for c in range(ADA_HEAD, ADA_POOL - 1):
                ada_sums(c)

            def conv_tile(c):
                dve.wait_ge(S("tile_out"), Z_MQ + c + 3)
                src, dst = z[:, Z_MQ + c, :], qk[:, c, :]
                tap = lambda j: cols[:, C_CONV + 4 * c + j:C_CONV + 4 * c + j + 1]
                own.do(V.tensor_scalar(dst, src, tap(CONV_W - 1), None, ALU.mult))
                for back in range(1, CONV_W):
                    ins = V.scalar_tensor_tensor(out=dst[:, back:T], in0=src[:, 0:T - back],
                                                 scalar=tap(CONV_W - 1 - back), in1=dst[:, back:T],
                                                 op0=ALU.mult, op1=ALU.add)
                    if back < CONV_W - 1:
                        own.do(ins)
                ins.then_inc(S("conv"), 1)

            def weights(t, h):
                return misc_t[:, t, MISC_IW + h:MISC_IW + h + 1]
            n, at_score = 0, 0
            for t in range(1, NT):
                w = (t + 1) * P
                dst = score[:, at_score:at_score + w]
                for h in range(IDX_HEADS):
                    dve.wait_ge(S("idx_relu"), n + 1)
                    if h == 0:
                        dve.wait_ge(S("misc_ready"), 1)
                        ins = V.tensor_scalar(dst, relu[:, n % 2, 0:w], weights(t, h), None, ALU.mult)
                    else:
                        dve.wait_ge(S("idx_added"), n)
                        ins = V.scalar_tensor_tensor(out=dst, in0=relu[:, n % 2, 0:w], scalar=weights(t, h), in1=dst,
                                                     op0=ALU.mult, op1=ALU.add)
                    ins.then_inc(S("idx_added"), 1)
                    n += 1
                    if n % 4 == 0:
                        if n == 4:
                            ada_sums(ADA_POOL - 1)
                        else:
                            conv_tile(n // 4 - 2)
                dve.wait_ge(S("idx_added"), n)
                own.do(V.tensor_scalar(dst, dst, 64.0 ** -0.5 * IDX_HEADS ** -0.5, None, ALU.mult))
                own.did(V.tensor_tensor(dst[:, t * P:w], dst[:, t * P:w], mask[:, 0:P], ALU.add))
                at_score += w

            dve.wait_ge(S("soft_f"), 1)
            R = lambda k: rows[0:4, k, :]
            own.do(V.scalar_tensor_tensor(out=R(R_LF), in0=z[32:36, Z_MISC, :], scalar=0.0, in1=rows[32:36, 2, :],
                                          op0=ALU.min, op1=ALU.subtract))
            own.do(V.memset(R(R_W), 1.0))
            own.do(V.tensor_tensor_scan(out=R(R_B), data0=R(R_W), data1=R(R_LF), initial=0.0, op0=ALU.mult, op1=ALU.add))
            own.do(V.tensor_tensor(R(R_W), z[0:4, Z_MISC, :], R(R_B), ALU.subtract))
            own.do(V.tensor_tensor_scan(out=R(R_MX), data0=R(R_W), data1=R(R_W), initial=0.0, op0=ALU.max, op1=ALU.max))
            V.tensor_tensor(R(R_M), R(R_B), R(R_MX), ALU.add).then_inc(S("rows_ready"), 1)
            conv_tile(n // 4 - 1)
            own.settle()
            spans, at_score = [], 0
            for t in range(1, NT):
                spans.append(slice(at_score, at_score + (t + 1) * P))
                at_score += (t + 1) * P
            with dve.Fori(0, N_SEL // 8):
                for k, span in enumerate(spans):
                    rnd.did(V.max(best8[:, 8 * k:8 * k + 8], score[:, span]))
                for k, span in enumerate(spans):
                    rnd.settle(len(spans) - 1)
                    rnd.did(V.match_replace(score[:, span], best8[:, 8 * k:8 * k + 8], score[:, span], TAKEN))
                rnd.turn_over()
            V.tensor_scalar(mask[:, P:P + at_score], score[:, 0:at_score], (NEG + TAKEN) / 2, NEG, ALU.is_gt, ALU.mult
                            ).then_inc(S("mask_ready"), 1)
            for c in range(n // 4, 2 * M_HEADS):
                conv_tile(c)

            dve.wait_ge(S("ada_used"), ADA_CHUNKS)
            V.tensor_tensor(ada[:, 16:48], bank[2][:, 16:48], cols[:, C_BADA + 16:C_BADA + 48], ALU.add
                            ).then_inc(S("ada_ready"), 1)
            dve.wait_ge(S("ada_ready"), 1)
            own.do(V.scalar_tensor_tensor(out=amp2[:, :], in0=ada[:, 32:40], scalar=1.0, in1=cols[:, C_N2:C_N2 + 8],
                                          op0=ALU.add, op1=ALU.mult))
            own.do(V.tensor_scalar(ada[:, 40:48], ada[:, 40:48], 1.0 / GATE_SCALE, None, ALU.mult))
            dve.wait_ge(S("idx_dot"), len(spans) * IDX_HEADS)
            V.memset(v_aug[:, :, :, M_DH:M_DH + 1], 1.0).then_inc(S("v_ones"), 1)
            def decay_arg(h):
                dve.wait_ge(S("neg_m"), h + 1)
                if h == 0:
                    dve.wait_ge(S("wcol_ready"), 1)
                if h >= 3:
                    dve.wait_ge(S("num_half"), 2 * (h - 2))
                off = 0
                for j in range(NT):
                    w = (NT - j) * P
                    ins = V.tensor_scalar(decay[h % 3][:, off:off + w], bank[2 + h % 2][:, j * P:T],
                                          wcol[:, j, h:h + 1], 0.0, ALU.add, ALU.min)
                    off += w
                ins.then_inc(S("decay_arg"), 1)

            def num_out(h):
                for half in range(2):
                    dve.wait_ge(S("num_half"), 2 * h + half + 1)
                    V.tensor_copy(num[:, 2 * half:2 * half + 2, h, :],
                                  bank[6 + half][:, 0:2 * (M_DH + 1)].rearrange("p (i e) -> p i e", i=2)
                                  ).then_inc(S("num_out"), 1)

            decay_arg(0)
            decay_arg(1)
            for h in range(M_HEADS):
                dve.wait_ge(S("decay_cut"), h + 1)
                off = 0
                for j in range(NT):
                    w, n = (NT - j) * P, h * NT + j
                    dve.wait_ge(S("qk_dot"), n + 1)
                    V.scalar_tensor_tensor(out=decay[h % 3][:, off:off + w], in0=bank[4 + n % 2][:, 0:w],
                                           scalar=float(M_DH) ** -0.5, in1=decay[h % 3][:, off:off + w],
                                           op0=ALU.mult, op1=ALU.mult).then_inc(S("decayed"), 1)
                    off += w
                if h:
                    num_out(h - 1)
                if h + 2 < M_HEADS:
                    decay_arg(h + 2)
            num_out(M_HEADS - 1)
            dve.wait_ge(S("num_out"), 2 * M_HEADS)
            dve.wait_ge(S("emm_ready"), 1)

            bc = lambda a, n: a.unsqueeze(3).broadcast_to([P, NT, M_HEADS, n])

            def hm_step(n):
                own.settle()
                if n == 0:
                    own.do(V.scalar_tensor_tensor(out=den[:, :, :], in0=num[:, :, :, M_DH], scalar=-1.0,
                                                  in1=num[:, :, :, M_DH], op0=ALU.mult, op1=ALU.max))
                    own.do(V.tensor_tensor(den[:, :, :], den[:, :, :], emm[:, :, :], ALU.max))
                    own.did(V.reciprocal(den[:, :, :], den[:, :, :]))
                elif n == 1:
                    own.did(V.tensor_tensor(hm[:, :, :, :], num[:, :, :, 0:M_DH], bc(den[:, :, :], M_DH), ALU.mult))
                elif n == 2:
                    own.did(V.tensor_tensor(hm2[:, :, :, :], hm[:, :, :, :], hm[:, :, :, :], ALU.mult))
                elif n == 3:
                    own.do(V.reduce_sum(hrs[:, :, :], hm2[:, :, :, :], AX.X))
                    V.tensor_scalar(hrs[:, :, :], hrs[:, :, :], 1.0 / M_DH, EPS, ALU.mult, ALU.add
                                    ).then_inc(S("hm_mean"), 1)
                elif n == 6:
                    dve.wait_ge(S("hm_root"), 1)
                    own.do(V.reciprocal(hrs[:, :, :], hrs[:, :, :]))
                    V.tensor_tensor(hm[:, :, :, :], hm[:, :, :, :], bc(hrs[:, :, :], M_DH), ALU.mult
                                    ).then_inc(S("hm_ready"), 1)

            def cat_m(h):
                dve.wait_ge(S("mo_gate"), h + 1)
                dve.wait_ge(S("hm_tr"), h + 1)
                V.scalar_tensor_tensor(out=z[:, Z_MO + h, :], in0=bank[h % 2][:, :],
                                       scalar=cols[:, C_OUTN + h:C_OUTN + h + 1], in1=z[:, Z_MO + h, :],
                                       op0=ALU.mult, op1=ALU.mult).then_inc(S("cat_m"), 1)

            def att_step(t, n):
                o = att[:, t, :, :]
                if n == 0:
                    dve.wait_ge(S("o_out"), (t + 1) * A_HEADS)
                    own.did(V.tensor_tensor(att2[:, :, :], o, o, ALU.mult))
                elif n == 1:
                    own.settle()
                    own.do(V.reduce_sum(o_rs[:, t, :], att2[:, :, :], AX.X))
                    V.tensor_scalar(o_rs[:, t, :], o_rs[:, t, :], 1.0 / A_DH, EPS, ALU.mult, ALU.add
                                    ).then_inc(S("att_mean"), 1)
                elif n == 2:
                    dve.wait_ge(S("att_root"), t + 1)
                    own.do(V.reciprocal(o_rs[:, t, :], o_rs[:, t, :]))
                    V.tensor_tensor(o, o, o_rs[:, t, :].unsqueeze(2).broadcast_to([P, A_HEADS, A_DH]), ALU.mult
                                    ).then_inc(S("att_ready"), 1)
                else:
                    dve.wait_ge(S("att_tr"), t + 1)
                    V.tensor_tensor(z[:, Z_IQ:Z_IQ + 4, t * P:(t + 1) * P],
                                    att_bank(t)[:, :].rearrange("p (f q) -> p f q", f=4),
                                    cols[:, C_OUTN + 4:C_OUTN + 8].unsqueeze(2).broadcast_to([P, 4, P]), ALU.mult
                                    ).then_inc(S("cat_a"), 1)

            dve.wait_ge(S("mask_ready"), 1)
            heads = NT * A_HEADS
            for n in range(heads + 3):
                if n < heads:
                    t = n // A_HEADS
                    w, at_mask = (t + 1) * P, t * (t + 1) // 2 * P
                    dve.wait_ge(S("s_dot"), n + 1)
                    if n >= 3:
                        dve.wait_ge(S("p_tr"), n - 2)
                    own.did(V.tensor_tensor_reduce(out=prob[:, n % 3, 0:w], in0=bank[4 + n % 2][:, 0:w],
                                                   in1=mask[:, at_mask:at_mask + w], scale=1.0, scalar=-3.0e38,
                                                   op0=ALU.add, op1=ALU.max, accum_out=s_max[:, n % 4:n % 4 + 1]))
                m = n - 3
                if m >= 0:
                    dve.wait_ge(S("o_dot"), m + 1)
                    own.did(V.reciprocal(s_sum[:, m % 4:m % 4 + 1], s_sum[:, m % 4:m % 4 + 1]))
                if n < heads:
                    own.settle(1 if m >= 0 else 0)
                    V.tensor_scalar(s_neg[:, n % 4:n % 4 + 1], s_max[:, n % 4:n % 4 + 1], -A_DH ** -0.5, None, ALU.mult
                                    ).then_inc(S("s_masked"), 1)
                if m >= 0:
                    own.settle()
                    V.tensor_scalar(att[:, m // A_HEADS, m % A_HEADS, :], bank[2 + m % 2][:, 0:A_DH],
                                    s_sum[:, m % 4:m % 4 + 1], None, ALU.mult).then_inc(S("o_out"), 1)
                if n <= 6:
                    hm_step(n)
                if n - 1 in HM_TR:
                    cat_m(HM_TR.index(n - 1))
                if n >= A_HEADS + 3:
                    t, k = n // A_HEADS - 1, n % A_HEADS
                    if t < NT - 1 and k in (3, 4, 6):
                        att_step(t, (3, 4, 6).index(k))
                if n >= 2 * A_HEADS + 2 and n % A_HEADS == 2:
                    att_step(n // A_HEADS - 2, 3)
            for k in range(4):
                att_step(NT - 1, k)

            for k in range(KB):
                dve.wait_ge(S("unit_done"), FIRST["o", 0] + 2 * k + 2)
                V.scalar_tensor_tensor(out=x[:, k, :], in0=tile_bank[(TILE0["o", 0] + k) % 2][:, :],
                                       scalar=ada[:, 16 + k:17 + k], in1=x[:, k, :], op0=ALU.mult, op1=ALU.add
                                       ).then_inc(S("tile_out"), 1)
            dve.wait_ge(S("tile_out"), TILE0["o", 0] + KB + 2)
            mean(1, bank[3])
            own.did(V.tensor_tensor(h_tmp[:, 0, :], x[:, 0, :], rstd[:, :], ALU.mult))
            for k in range(KB):
                if k + 1 < KB:
                    own.did(V.tensor_tensor(h_tmp[:, k + 1, :], x[:, k + 1, :], rstd[:, :], ALU.mult))
                own.settle(min(1, KB - 1 - k))
                normed(amp2, 24, k)
            late_lows(1)

            H = P_HEADS
            items = [(h, t) for h in range(H) for t in range(NT)]

            def best_keys(n):
                h, t = items[n]
                s_of = lambda a: s12[:, h, t, a, :]
                b = lambda a, k: best[:, t * H + h, a, 8 * k:8 * k + 8]
                bi = lambda a, k: best_iu[:, t * H + h, a, 8 * k:8 * k + 8]
                for k in range(2):
                    yield [lambda a=a: V.max(b(a, k), s_of(a)) for a in range(2)]
                    yield [lambda a=a: V.max_index(bi(a, k), b(a, k), s_of(a)) for a in range(2)]
                    if k == 0:
                        yield [lambda a=a: V.match_replace(s_of(a), b(a, 0), s_of(a), TAKEN) for a in range(2)]

            def best_sums(n):
                h, t = items[n]
                c0, c1 = cand[:, n % 2, 0, :], cand[:, n % 2, 1, :]
                i = t * H + h
                yield [lambda: V.tensor_tensor(c0.rearrange("p (a b) -> p a b", a=16),
                                               best[:, i, 0, :].unsqueeze(2).broadcast_to([P, 16, 16]),
                                               best[:, i, 1, :].unsqueeze(1).broadcast_to([P, 16, 16]), ALU.add)]
                yield [lambda: V.max(top[:, i, 0:8], c0)]
                yield [lambda: V.max_index(pos_u[:, i, 0:8], top[:, i, 0:8], c0),
                       lambda: V.match_replace(c1, top[:, i, 0:8], c0, TAKEN)]
                yield [lambda: V.max(top[:, i, 8:16], c1)]
                yield [lambda: V.max_index(pos_u[:, i, 8:16], top[:, i, 8:16], c1)]

            for n in range(len(items) + 1):
                if n < len(items):
                    h, t = items[n]
                    dve.wait_ge(S("s_ready"), 2 * h + t // 2 + 1)
                keys_steps = best_keys(n) if n < len(items) else iter([[]] * 5)
                sums_steps = best_sums(n - 1) if n else iter([[]] * 5)
                last = [0, 0]
                own.settle()
                for ours, theirs in zip(keys_steps, sums_steps):
                    for chain, step in enumerate((ours, theirs)):
                        if not step:
                            continue
                        own.settle(own.n - last[chain] if last[chain] else 0)
                        for op in step:
                            own.did(op())
                        last[chain] = own.n
            own.settle()
            own.did(V.tensor_copy(best_if[:, :, :, :], best_iu[:, :, :, :]))
            own.did(V.tensor_copy(gsum[:, :], top[:, :, 0]))
            own.settle()
            own.do(V.tensor_scalar(pos_f[:, 1, :, :].bitcast(u32), pos_u[:, :, :], 15, None, ALU.bitwise_and))
            own.do(V.tensor_scalar(pos_u[:, :, :], pos_u[:, :, :], 4, None, ALU.logical_shift_right))
            own.do(V.tensor_copy(pos_f[:, 1, :, :], pos_f[:, 1, :, :].bitcast(u32)))
            own.do(V.tensor_copy(pos_f[:, 0, :, :], pos_u[:, :, :]))
            for t in range(NT):
                sl = slice(t * P_HEADS, (t + 1) * P_HEADS)
                V.tensor_tensor(top[:, sl, :], top[:, sl, :], gsum[:, sl].unsqueeze(2).broadcast_to([P, P_HEADS, 16]),
                                ALU.subtract).then_inc(S("top_shift"), 1)
                for a in range(2):
                    ranks = iota[:, 0:16].unsqueeze(1).unsqueeze(1).broadcast_to([P, P_HEADS, 16, 16])
                    pf = pos_f[:, a, sl, :].unsqueeze(3).broadcast_to([P, P_HEADS, 16, 16])
                    idx = best_if[:, sl, a, :].unsqueeze(2).broadcast_to([P, P_HEADS, 16, 16])
                    own.do(V.tensor_tensor(pick[:, :, :, :], pf, ranks, ALU.is_equal))
                    own.do(V.tensor_tensor(pick[:, :, :, :], pick[:, :, :, :], idx, ALU.mult))
                    own.do(V.reduce_sum(slot_t[:, a, t * P:(t + 1) * P].rearrange("p (h k) -> p h k", h=P_HEADS),
                                        pick[:, :, :, :], AX.X))
            for t in range(NT):
                sl = slice(t * P_HEADS, (t + 1) * P_HEADS)
                dve.wait_ge(S("top_exp"), t + 1)
                own.do(V.reduce_sum(gsum[:, sl], top[:, sl, :], AX.X))
                own.do(V.reciprocal(gsum[:, sl], gsum[:, sl]))
                V.tensor_tensor(slot_t[:, 2, t * P:(t + 1) * P].rearrange("p (h k) -> p h k", h=P_HEADS), top[:, sl, :],
                                gsum[:, sl].unsqueeze(2).broadcast_to([P, P_HEADS, 16]), ALU.mult
                                ).then_inc(S("slots_ready"), 1)
            dve.wait_ge(S("slot_out"), 3)
            for k in range(2):
                ins = V.tensor_copy(slot_g[:, k, :], slot_gf[:, :])
                if k < 1:
                    own.do(ins)
                    own.do(V.tensor_tensor(slot_gf[:, :], slot_gf[:, :], slot_g[:, k, :], ALU.subtract))
            ins.then_inc(S("gate_split"), 1)
            dve.wait_ge(S("gate_split"), 1)

            def one_hots(g, i, par):
                if g or not isinstance(i, int):
                    dve.wait_ge(S("rows_used"), i + (g * (T // GT) - 1))
                keys_of = lambda table, n: table[:, ds(i * GT, GT)].unsqueeze(1).broadcast_to([P, n, GT])
                own.did(V.tensor_tensor(eq1[:, par, :, :], key_rep[:, g * GI:(g + 1) * GI, :], keys_of(slot_i1, GI),
                                        ALU.is_equal))
                V.tensor_tensor(rows2[:, par, :, :], key_rep[:, :, :], keys_of(slot_i2, N_KEYS), ALU.is_equal
                                ).then_inc(S("rows2_ready"), 1)
                own.settle()
                V.tensor_tensor(rows1[:, par, :, :, :], eq1[:, par, :, :].unsqueeze(1).broadcast_to([P, 2, GI, GT]),
                                slot_g[:, :, ds(i * GT, GT)].unsqueeze(2).broadcast_to([P, 2, GI, GT]), ALU.mult
                                ).then_inc(S("rows1_ready"), 1)

            def apply_gates(g, i, par):
                buf = (g % 2) * GI
                dve.wait_ge(S("rows_used"), i + (g * (T // GT) + 1))
                c = coef[:, buf:buf + GI, ds(i * GT, GT)]
                V.tensor_tensor(c, c, gate_bank[par][:, 0:GT * GI].rearrange("p (n e) -> p e n", n=GT), ALU.mult
                                ).then_inc(S("gated"), 1)

            def gate_group(g, between=None):
                if g in (0, GROUPS - 1):
                    for q in range(2):
                        one_hots(g, q, q)
                dve.wait_ge(S("tile_out"), TILE0["u", g] + GI + 2)
                pairs = T // GT // 2
                for start, end in ((1, pairs // 2 + 1), (pairs // 2 + 1, pairs)):
                    with own.loop(start, end, 2) as i:
                        for par in range(2):
                            one_hots(g, i * 2 + par, par)
                            apply_gates(g, i * 2 + (par - 2), par)
                    if between and end < pairs:
                        between()
                for q in range(T // GT - 2, T // GT):
                    apply_gates(g, q, q % 2)

            def sums_out(g, half, ds_=range(4)):
                for d in ds_:
                    k = half * 4 + d
                    if d < 3:
                        dve.wait_ge(S("sum_done"), (g * 2 + half) * 3 + d + 1)
                    else:
                        dve.wait_ge(S("unit_done"), FIRST["v", g] + (half + 1) * GI)
                    if g < GROUPS - 1:
                        if g or half:
                            dve.wait_ge(S(f"part_saved{d}"), 16 * (2 * g + half))
                        V.tensor_copy(y_stage[:, d, :], sum_bank[d][:, :]).then_inc(S("y_out"), 1)
                    else:
                        V.scalar_tensor_tensor(out=part[:, 3, k, :], in0=sum_bank[d][:, :],
                                               scalar=ada[:, 40 + k:41 + k], in1=part[:, 3, k, :],
                                               op0=ALU.mult, op1=ALU.add).then_inc(S("sums_added"), 1)

            def v_phase(g):
                coef_lows(dve, own, V.tensor_tensor, g, None, (lambda: sums_out(g, 0, range(3)),
                                                          lambda: sums_out(g, 0, range(3, 4))))
                for q in range(2):
                    one_hots(g + 1, q, q)
                sums_out(g, 1)

            for g in range(GROUPS - 2):
                gate_group(g)
                v_phase(g)
            gate_group(GROUPS - 2)
            gate_group(GROUPS - 1, lambda: sums_out(GROUPS - 2, 0))
            def add_earlier(k, step):
                blk = lambda n: part[:, n, k, :] if isinstance(k, int) else part[:, n, ds(k, 1), :]
                if step == 0:
                    own.did(V.tensor_tensor(blk(0), blk(0), blk(1), ALU.add))
                    return
                own.settle()
                if step == 1:
                    own.did(V.tensor_tensor(blk(2), blk(2), blk(0), ALU.add))
                    return
                ins = V.scalar_tensor_tensor(out=blk(3), in0=blk(2), scalar=ada[:, 40 + k:41 + k] if isinstance(
                    k, int) else ada[:, ds(k + 40, 1)], in1=blk(3), op0=ALU.mult, op1=ALU.add)
                own.did(ins)
                dve.sem_inc(S("earlier_added"), 1)
            def first_half_out():
                dve.wait_ge(S("x2_back"), 16 * KB)
                sums_out(GROUPS - 1, 0, range(3))
            def rest_out():
                sums_out(GROUPS - 1, 0, range(3, 4))
                dve.wait_ge(S("part_back"), 16 * KB * (GROUPS - 1))
                dve.wait_ge(S("sums_added"), 4)
            coef_lows(dve, own, V.tensor_tensor, GROUPS - 1, None, (first_half_out, rest_out), add_earlier,
                      lambda: sums_out(GROUPS - 2, 1))
            own.settle()
            sums_out(GROUPS - 1, 1)
            dve.wait_ge(S("sums_added"), KB)
            mean(2, bank[3], rstd_end)
            for k in range(KB):
                V.scalar_tensor_tensor(out=part[:, 2, k, :], in0=part[:, 3, k, :], scalar=cols[:, C_FG + k:C_FG + k + 1],
                                       in1=rstd_end[:, :], op0=ALU.mult, op1=ALU.mult).then_inc(S("out_ready"), 1)

        @block.tensor
        def _(pe):
            mm = nc.tensor.matmul

            def square_sums(n, sq=sq):
                for k in range(KB):
                    pe.wait_ge(S("x_sq"), KB * n + k + 1)
                    ins = mm(bank[3][:, :], ones[:, :], sq[:, k, :], start=(k == 0), stop=(k == KB - 1))
                ins.then_inc(S("sq_sum"), 1)

            def ada_chunk(c):
                ada_summed(pe, c)
                parts = [ada_acc[:, c % 2, :]]
                if c < ADA_HEAD:
                    pe.wait_ge(S("ada_paired"), c + 1)
                    parts = [ada_acc0[:, c, :], ada_w0[:, c, ADA_DVE, :]]
                for j in range(2):
                    for n, part_sum in enumerate(parts):
                        ins = mm(bank[2][:, 2 * c + j:2 * c + j + 1], part_sum[:, j * P:(j + 1) * P], ones[:, 0:1],
                                 start=(n == 0), stop=(n == len(parts) - 1))
                ins.then_inc(S("ada_used"), 1)

            def split_unit(u, out_of, start, stop, inputs=None):
                s = u % SPLIT_SLOTS
                half = 4 * (not start)
                for k in range(4):
                    if inputs:
                        inputs(half + k)
                    wh = w_hi[:, s, k * P:(k + 1) * P]
                    mm(out_of, wh, hs_hi[:, half + k, :], start=(start and k == 0), stop=False)
                    mm(out_of, wh, hs_lo[:, half + k, :], start=False, stop=False)
                    ins = mm(out_of, w_lo[:, s, k * P:(k + 1) * P], hs_hi[:, half + k, :], start=False,
                             stop=(stop and k == 3))
                return ins

            def tile(phase, i, j, extra=None, inputs=None):
                u0, t0 = FIRST[phase] + 2 * j, TILE0[phase] + j
                dst = tile_bank[t0 % 2][:, :]
                pe.wait_ge(S("tile_out"), i * 2 + (t0 + 1))
                for h in range(2):
                    pe.wait_ge(S("w_split"), i * 4 + (u0 + h + 1))
                    split_unit(u0 + h, dst, h == 0, h == 1, inputs).then_inc(S("unit_done"), 1)
                    if extra:
                        extra(i, 2 * j + h)

            def tiles(phase, count, extra=None, inputs=None):
                if inputs:
                    for j in range(2):
                        tile(phase, 0, j, extra, inputs if j == 0 else None)
                with pe.Fori(1 if inputs else 0, count // 2) as i:
                    for j in range(2):
                        tile(phase, i, j, extra)

            def normed_input(n):
                half = KB // 2
                return lambda k: pe.wait_ge(S("h_low" if k < half else "h_low_late"), n * half + k % half + 1)

            def three_passes(dst, q_hi, q_lo, k_hi, k_lo):
                for n, (a, b) in enumerate(((q_hi, k_hi), (q_hi, k_lo), (q_lo, k_hi))):
                    ins = mm(dst, a, b, start=(n == 0), stop=(n == 2))
                return ins

            def transposes(dst, sources):
                for n, src in enumerate(sources):
                    w = src.shape[0]
                    ins = nc.tensor.transpose(dst[:, n * w:(n + 1) * w], src, ident[0:w, 0:w])
                return ins

            pe.wait_ge(S("consts"), 1)
            square_sums(0)
            for c in range(ADA_HEAD):
                ada_chunk(c)

            idx = [(t, h) for t in range(1, NT) for h in range(IDX_HEADS)]

            def index_product(n):
                t, h = idx[n]
                if n >= 4:
                    pe.wait_ge(S("idx_relu"), n - 3)
                r = slice(64 * (h % 2), 64 * (h % 2) + 64)
                if n == 0:
                    pe.wait_ge(S("i_low"), 5)
                q, k = slice(t * P, (t + 1) * P), slice(0, (t + 1) * P)
                three_passes(bank[4 + n % 4][:, k], i_hi[r, h // 2, q], i_lo[r, h // 2, q], i_hi[r, 4, k], i_lo[r, 4, k]
                             ).then_inc(S("idx_dot"), 1)

            def beside(i, unit):
                u = unit - 2 * Z_HEAD
                if u == 1:
                    pe.wait_ge(S("tile_out"), Z_HEAD + 2)
                    transposes(bank[3], [z[:, Z_MISC, t * P:(t + 1) * P] for t in range(NT)]).then_inc(S("misc_tr"), 1)
                n = 2 * (unit - 2 * IDX_TILE)
                for n in (n, n + 1):
                    if 0 <= n < len(idx):
                        index_product(n)
                if unit % 2 and unit // 2 in ADA_BESIDE:
                    ada_chunk(ADA_HEAD + ADA_BESIDE.index(unit // 2))
                h = unit // 2 - V_TR
                if unit % 2 and 0 <= h < M_HEADS:
                    pe.wait_ge(S("idx_relu"), len(idx))
                    pe.wait_ge(S("tile_out"), Z_MV + h + 3)
                    transposes(bank[4 + h], [z[:, Z_MV + h, t * P:(t + 1) * P] for t in range(NT)]
                               ).then_inc(S("v_tr"), 1)

            for t in range(Z_TILES):
                tile(("z", 0), 0, t, beside, normed_input(0) if t == 0 else None)
            pe.wait_ge(S("v_ready"), M_HEADS)
            pe.wait_ge(S("rows_ready"), 1)
            pe.wait_ge(S("misc_ready"), 1)
            for k, row in enumerate((R_W, R_M)):
                for j in range(NT):
                    c = 16 * k + 4 * j
                    ins = nc.tensor.transpose(bank[3][:, c:c + 4], rows[0:4, row, j * P:(j + 1) * P], ident[0:4, 0:4])
            ins.then_inc(S("col_tr"), 1)
            pe.wait_ge(S("qk_ready"), 2 * M_HEADS)
            pe.wait_ge(S("v_ready"), M_HEADS)
            pe.wait_ge(S("v_ones"), 1)
            pe.wait_ge(S("ada_ready"), 1)
            pe.wait_ge(S("emm_ready"), 1)

            def neg_m(h):
                if h >= 2:
                    pe.wait_ge(S("decay_arg"), h - 1)
                mm(bank[2 + h % 2][:, :], sel[0:4, h, :], rows[0:4, R_MX, :], start=True, stop=True
                   ).then_inc(S("neg_m"), 1)

            def key_products(h):
                for j in range(NT):
                    n = h * NT + j
                    if n >= 2:
                        pe.wait_ge(S("decayed"), n - 1)
                    mm(bank[4 + n % 2][:, 0:(NT - j) * P], qk[:, M_HEADS + h, j * P:(j + 1) * P], qk[:, h, j * P:T],
                       start=True, stop=True).then_inc(S("qk_dot"), 1)

            def value_products(h):
                pe.wait_ge(S("decayed"), (h + 1) * NT)
                for i in range(NT):
                    if h and i % 2 == 0:
                        pe.wait_ge(S("num_out"), 2 * (h - 1) + i // 2 + 1)
                    c = (i % 2) * (M_DH + 1)
                    off = 0
                    for j in range(i + 1):
                        a = off + (i - j) * P
                        ins = mm(bank[6 + i // 2][:, c:c + M_DH + 1], decay[h % 3][:, a:a + P], v_aug[:, j, h, :],
                                 start=(j == 0), stop=(j == i))
                        off += (NT - j) * P
                    if i % 2:
                        ins.then_inc(S("num_half"), 1)

            def att_transposes(t):
                pe.wait_ge(S("cat_m"), M_HEADS)
                pe.wait_ge(S("att_ready"), t + 1)
                if t >= 2:
                    pe.wait_ge(S("cat_a"), t if t == NT - 1 else t - 1)
                transposes(att_bank(t), [att[:, t, 2 * f:2 * f + 2, :].rearrange("p h d -> p (h d)") for f in range(4)]
                           ).then_inc(S("att_tr"), 1)

            neg_m(0)
            for h in range(M_HEADS):
                if h + 1 < M_HEADS:
                    neg_m(h + 1)
                key_products(h)
                if h:
                    value_products(h - 1)
            value_products(M_HEADS - 1)

            heads = NT * A_HEADS
            pe.wait_ge(S("decayed"), M_HEADS * NT)
            pe.wait_ge(S("num_out"), 2 * M_HEADS)
            for n in range(heads + 2):
                if n < heads:
                    t, h = divmod(n, A_HEADS)
                    if n >= 2:
                        pe.wait_ge(S("s_masked"), n - 1)
                    r = slice(64 * (h % 2), 64 * (h % 2) + 64)
                    if n == 0:
                        pe.wait_ge(S("a_low"), 5)
                    q, k = slice(t * P, (t + 1) * P), slice(0, (t + 1) * P)
                    three_passes(bank[4 + n % 2][:, k], aq_hi[r, h // 2, q], a_lo[r, h // 2, q], ak_hi[r, k],
                                 a_lo[r, 4, k]).then_inc(S("s_dot"), 1)
                m = n - 1
                if 0 <= m < heads:
                    pe.wait_ge(S("p_ready"), m + 1)
                    if m >= 2:
                        pe.wait_ge(S("pt_ready"), m - 1)
                    transposes(bank[6 + m % 2], [prob[:, m % 3, s * P:(s + 1) * P] for s in range(m // A_HEADS + 1)]
                               ).then_inc(S("p_tr"), 1)
                m = n - 2
                if 0 <= m < heads:
                    t = m // A_HEADS
                    pe.wait_ge(S("pt_ready"), m + 1)
                    if m >= 2:
                        pe.wait_ge(S("o_out"), m - 1)
                    for s in range(t + 1):
                        ins = mm(bank[2 + m % 2][:, 0:A_DH], prob_t[:, m % 2, s, :],
                                 misc_t[:, s, MISC_AV:MISC_AV + A_DH], start=(s == 0), stop=(s == t))
                    ins.then_inc(S("o_dot"), 1)
                if n in HM_TR:
                    h = HM_TR.index(n)
                    pe.wait_ge(S("hm_ready"), 1)
                    if h >= 2:
                        pe.wait_ge(S("cat_m"), h - 1)
                    transposes(bank[h % 2], [hm[:, t, h, :] for t in range(NT)]).then_inc(S("hm_tr"), 1)
                if n >= ATT_TR and (n - ATT_TR) % A_HEADS == 0:
                    att_transposes((n - ATT_TR) // A_HEADS)
            att_transposes(NT - 1)
            tiles(("o", 0), KB, inputs=lambda k: pe.wait_ge(S("cat_low"), k + 1))
            square_sums(1)
            def key_scores(i, unit):
                h, pair = divmod(unit - 2, 2)
                if h < 0:
                    return
                k = 2 * h + pair
                pe.wait_ge(S("tile_out"), TILE0["q", 0] + h + 3)
                pe.wait_ge(S("keys_in"), 16)
                if k >= 4:
                    pe.wait_ge(S("s_ready"), k - 3)
                for a in range(2):
                    t = 2 * pair + a
                    ins = mm(bank[4 + k % 4][:, a * 256:(a + 1) * 256], q_t[:, h, t * P:(t + 1) * P], keys[:, h, :],
                             start=True, stop=True)
                ins.then_inc(S("keys_dot"), 1)

            for h in range(P_HEADS):
                tile(("q", 0), 0, h, key_scores, normed_input(1) if h == 0 else None)
            for pair in range(2):
                key_scores(0, 2 * P_HEADS + pair)

            def gates(g, q, par):
                pe.wait_ge(S("gated"), q + (g * (T // GT) + 1))
                pe.wait_ge(S("rows1_ready"), q + (g * (T // GT) + 1))
                pe.wait_ge(S("rows2_ready"), q + (g * (T // GT) + 1))
                for n in range(GT):
                    dst = gate_bank[par][:, n * GI:(n + 1) * GI]
                    for k in range(2):
                        ins = mm(dst, rows2[:, par, :, n], rows1[:, par, k, :, n], start=(k == 0), stop=(k == 1))
                ins.then_inc(S("rows_used"), 1)

            def v_units(g, with_gates):
                first = FIRST["v", g]
                if with_gates is not None:
                    gates(with_gates, 0, 0)
                for half in range(2):
                    f = first + half * GI

                    def unit(i, u, start, stop):
                        s = (f + u) % SPLIT_SLOTS
                        pe.wait_ge(S("w_split"), i * 4 + (f + u + 1))
                        pe.wait_ge(S(f"c_split{g}"), i * 4 + (half * GI + u + 1))
                        for d in range(4):
                            if start and (g or half):
                                if g == GROUPS - 1 and half:
                                    pe.wait_ge(S("sums_added"), d + 1)
                                else:
                                    pe.wait_ge(S("y_out"), g * KB + (half - 1) * 4 + d + 1)
                            wh, wl = (w[:, s, d * P:(d + 1) * P] for w in (w_hi, w_lo))
                            dst = sum_bank[d][:, :]
                            mm(dst, wh, c_hi[:, s, :], start=start, stop=False)
                            mm(dst, wh, c_lo[:, s, :], start=False, stop=False)
                            ins = mm(dst, wl, c_hi[:, s, :], start=False, stop=stop)
                            if stop and d < 3:
                                ins.then_inc(S("sum_done"), 1)
                        ins.then_inc(S("unit_done"), 1)
                        q = half * GI + u + 1
                        last = isinstance(i, int) and i * 4 + q == EU
                        if with_gates is not None and not last:
                            gates(with_gates, i * 4 + q, q % 2)

                    for u in range(4):
                        unit(0, u, u == 0, False)
                    with pe.Fori(1, GI // 4 - 1) as i:
                        for u in range(4):
                            unit(i, u, False, False)
                    for u in range(4):
                        unit(GI // 4 - 1, u, False, u == 3)

            tiles(("u", 0), GI)
            pe.wait_ge(S("s_ready"), NT * P_HEADS // 2)
            pe.wait_ge(S("slots_ready"), NT)
            for k in range(3):
                transposes(bank[4 + k], [slot_t[:, k, t * P:(t + 1) * P] for t in range(NT)]).then_inc(S("slot_tr"), 1)

            def u_tiles_and_gates(g):
                steady = lambda i, n: gates(g, i * 4 + (n + 1), (n + 1) % 2)
                if g:
                    gates(g, 0, 0)
                    first_turn = steady
                else:
                    def first_turn(i, n):
                        for q in ((), (0, 1), (2, 3), (4,))[n]:
                            gates(0, q, q % 2)
                last_turn = lambda i, n: steady(i, n) if n < 3 else None
                for j in range(2):
                    tile(("u", g + 1), 0, j, first_turn)
                with pe.Fori(1, GI // 2 - 1) as i:
                    for j in range(2):
                        tile(("u", g + 1), i, j, steady)
                for j in range(2):
                    tile(("u", g + 1), GI // 2 - 1, j, last_turn)

            u_tiles_and_gates(0)
            pe.wait_ge(S("slot_out"), 3)
            for g in range(GROUPS):
                v_units(g, GROUPS - 1 if g == GROUPS - 2 else None)
                if g + 2 < GROUPS:
                    u_tiles_and_gates(g + 1)
            square_sums(2, sq_end)


_INS = ["x_t", "cols", "wada", "stream", "keys"]


def lay_out(inputs):
    import numpy as np

    a = {k: np.asarray(v) for k, v in inputs.items()}
    f32 = np.float32
    by_block = lambda v: v.reshape(-1, P).T
    x_t = a["x"].reshape(T, KB, P).transpose(2, 1, 0)

    sizes = (512, 512, 512, 512, 4, 4, 512, 64, 64, 512, 64, 8)
    starts = np.concatenate([[0], np.cumsum(sizes)])
    mq, mk, mv, mo, mi, mf, aq, ak, av, iq, ik, iw = (slice(starts[n], starts[n + 1]) for n in range(12))
    w_in, b_in = a["w_in"][0], a["b_in"][0][None, :]

    def arrange(m):
        out = np.zeros((m.shape[0], Z_TILES * P), f32)
        put = lambda c, s: out.__setitem__((slice(None), slice(c, c + s.stop - s.start)), m[:, s])
        put(Z_IQ * P, iq)
        put(Z_IK * P, ik)
        put(Z_IK * P + 64, ik)
        put(Z_MISC * P + MISC_MI, mi)
        put(Z_MISC * P + MISC_IW, iw)
        put(Z_MISC * P + MISC_MF, mf)
        put(Z_MISC * P + MISC_AV, av)
        put(Z_AQ * P, aq)
        put(Z_AK * P, ak)
        put(Z_AK * P + 64, ak)
        for c, s in ((Z_MQ, mq), (Z_MK, mk), (Z_MV, mv), (Z_MO, mo)):
            put(c * P, s)
        return out

    cols = np.concatenate([
        by_block(a["c"].reshape(-1)), by_block(a["b_ada"].reshape(-1)), by_block(a["norm1_g"].reshape(-1)),
        by_block(arrange(b_in).reshape(-1)),
        a["conv_qk"][0].reshape(CONV_W, 8, P).transpose(2, 1, 0).reshape(P, 32),
        by_block(a["out_norm_m"].reshape(-1)), by_block(a["out_norm_a"].reshape(-1)),
        by_block(a["norm2_g"].reshape(-1)), by_block(a["final_g"].reshape(-1))], axis=1)
    wada = a["w_ada"][0].reshape(KB, P, 24, 256).transpose(2, 1, 0, 3)

    def units(w):
        n = w.shape[1] // P
        return w.reshape(2, 4, P, n, P).transpose(3, 0, 2, 1, 4).reshape(2 * n, P, UNIT)

    u, v = a["peer_u"][0], a["peer_v"][0]
    order, first = stream_order()
    stream = np.empty((UNITS, P, UNIT), f32)
    for name, g, n in order:
        e = slice(g * GI * N_KEYS, (g + 1) * GI * N_KEYS)
        if name == "u":
            part = units(u[e].T)
        elif name == "v":
            part = v[e].reshape(GI, P, 2, UNIT).transpose(2, 0, 1, 3).reshape(n, P, UNIT)
        else:
            part = units({"z": arrange(w_in) if name == "z" else None, "o": a["w_out"][0], "q": a["w_peer_q"][0]}[name])
        stream[first[name, g]:first[name, g] + n] = part
    keys = np.zeros((P, P_HEADS, 2 * N_KEYS), f32)
    sub = a["peer_sub_keys"][0]
    for side in range(2):
        keys[side * 64:(side + 1) * 64, :, side * N_KEYS:(side + 1) * N_KEYS] = sub[:, side].transpose(2, 0, 1)
    return {"x_t": x_t, "cols": cols, "wada": wada, "stream": stream, "keys": keys}


def kernel(**inputs):
    import numpy as np
    import concourse.bacc as bacc
    from concourse.bass_utils import run_bass_kernel_spmd

    nc = bacc.Bacc("TRN2", target_bir_lowering=False, num_devices=1)
    laid = lay_out(inputs)
    arrays, args = {}, []
    for name in _INS:
        arr = np.ascontiguousarray(laid[name])
        arrays[f"in_{name}"] = arr
        args.append(nc.dram_tensor(f"in_{name}", arr.shape, mybir.dt.float32, kind="ExternalInput").ap())
    out = nc.dram_tensor("out_t", [P, KB, T], mybir.dt.float32, kind="ExternalOutput").ap()
    build_layer(nc, *args, out)
    r = run_bass_kernel_spmd(nc, [arrays], core_ids=[0])
    return np.ascontiguousarray(np.asarray(r.results[0]["out_t"]).transpose(2, 1, 0)).reshape(1, T, D)
```
